# Optimizing a Trainium2 kernel written in Bass

```python
import jax, jax.numpy as jnp
from jax import lax
import numpy as np

D_MODEL = 2048
BATCH = 1
SEQ = 256
DEPTH = 2

N_A_LAYERS = DEPTH // 2
N_B_LAYERS = DEPTH - N_A_LAYERS

GLA_HEADS = 4
GLA_QK_DIM = D_MODEL // 2
GLA_V_DIM = D_MODEL
GLA_DK = GLA_QK_DIM // GLA_HEADS
GLA_DV = GLA_V_DIM // GLA_HEADS
GLA_GATE_RANK = 16
GLA_GATE_TAU = 16.0
GLA_CHUNK = 64
GLA_IN_DIM = 2 * GLA_QK_DIM + 2 * GLA_V_DIM + GLA_GATE_RANK

SB_HEADS = 16
SB_HEAD_DIM = D_MODEL // SB_HEADS
SB_DIM = SB_HEADS * SB_HEAD_DIM
SB_Q_BLOCK = 128

D_FF = 4 * D_MODEL
N_MOD = 6
DEEPNORM_ALPHA = (2.0 * DEPTH) ** 0.25
DEEPNORM_BETA = (8.0 * DEPTH) ** -0.25
LN_EPS = 1e-5
RMS_EPS = 1e-5

kernel_name = "yoco_gla_stickbreaking_deepnorm_adaln"

def layer_norm(x, g, b):
    xf = x.astype(jnp.float32)
    mu = jnp.mean(xf, axis=-1, keepdims=True)
    xc = xf - mu
    var = jnp.mean(xc * xc, axis=-1, keepdims=True)
    return (xc * lax.rsqrt(var + LN_EPS) * g.astype(jnp.float32) + b.astype(jnp.float32)).astype(x.dtype)

def gla_mixer(h, w_in, w_gate_up, b_gate, norm_g, w_out):
    B, T, _ = h.shape
    n_chunks = T // GLA_CHUNK
    proj = h @ w_in
    q, k, v, r, gl = jnp.split(
        proj, [GLA_QK_DIM, 2 * GLA_QK_DIM, 2 * GLA_QK_DIM + GLA_V_DIM, 2 * GLA_QK_DIM + 2 * GLA_V_DIM], axis=-1)
    log_a = jax.nn.log_sigmoid((gl @ w_gate_up + b_gate).astype(jnp.float32)) / GLA_GATE_TAU

    def to_chunks(t, d):
        return t.astype(jnp.float32).reshape(B, n_chunks, GLA_CHUNK, GLA_HEADS, d).transpose(0, 3, 1, 2, 4)

    qc = to_chunks(q, GLA_DK) * (GLA_DK ** -0.5)
    kc = to_chunks(k, GLA_DK)
    vc = to_chunks(v, GLA_DV)
    bc = jnp.cumsum(to_chunks(log_a, GLA_DK), axis=3)
    b_last = bc[:, :, :, -1:, :]
    q_dec = qc * jnp.exp(bc)
    k_intra = kc * jnp.exp(-bc)
    k_state = kc * jnp.exp(b_last - bc)
    chunk_decay = jnp.exp(b_last[:, :, :, 0, :])

    causal = jnp.tril(jnp.ones((GLA_CHUNK, GLA_CHUNK), dtype=jnp.float32))
    scores = jnp.einsum('bhncd,bhnsd->bhncs', q_dec, k_intra) * causal
    o_intra = jnp.einsum('bhncs,bhnse->bhnce', scores, vc)

    def step(state, xs):
        qd, ks, vv, dec = xs
        o = jnp.einsum('bhcd,bhde->bhce', qd, state)
        state = state * dec[..., None] + jnp.einsum('bhcd,bhce->bhde', ks, vv)
        return state, o

    xs = (jnp.moveaxis(q_dec, 2, 0), jnp.moveaxis(k_state, 2, 0),
          jnp.moveaxis(vc, 2, 0), jnp.moveaxis(chunk_decay, 2, 0))
    s0 = jnp.zeros((B, GLA_HEADS, GLA_DK, GLA_DV), jnp.float32)
    _, o_inter = lax.scan(step, s0, xs)
    o = o_intra + jnp.moveaxis(o_inter, 0, 2)
    o = o.transpose(0, 2, 3, 1, 4).reshape(B, T, GLA_HEADS, GLA_DV)
    o = o * lax.rsqrt(jnp.mean(o * o, axis=-1, keepdims=True) + RMS_EPS) * norm_g.astype(jnp.float32)
    o = o.reshape(B, T, GLA_V_DIM) * jax.nn.silu(r.astype(jnp.float32))
    return o.astype(h.dtype) @ w_out

def shared_kv(x, cs, kv_ada_w, kv_ada_b, w_kv):
    B, T, _ = x.shape
    mod = (cs @ kv_ada_w + kv_ada_b)[:, None, :]
    shift, scale = jnp.split(mod, 2, axis=-1)
    kv = (x * (1.0 + scale) + shift) @ w_kv
    k, v = jnp.split(kv, 2, axis=-1)
    return (k.reshape(B, T, SB_HEADS, SB_HEAD_DIM), v.reshape(B, T, SB_HEADS, SB_HEAD_DIM))

def stick_breaking_attention(q, k, v):
    B, T, H, dh = q.shape
    nb = T // SB_Q_BLOCK
    qf = (q.astype(jnp.float32) * (dh ** -0.5)).reshape(B, nb, SB_Q_BLOCK, H, dh).transpose(1, 0, 3, 2, 4)
    kf = k.astype(jnp.float32).transpose(0, 2, 1, 3)
    vf = v.astype(jnp.float32).transpose(0, 2, 1, 3)
    k_pos = jnp.arange(T)

    def block(args):
        qb, start = args
        q_pos = start + jnp.arange(SB_Q_BLOCK)
        mask = k_pos[None, :] < q_pos[:, None]
        z = jnp.einsum('bhqd,bhkd->bhqk', qb, kf)
        log_beta = jax.nn.log_sigmoid(z)
        log_not = jnp.where(mask, log_beta - z, 0.0)
        later = lax.cumsum(log_not, axis=3, reverse=True) - log_not
        a = jnp.where(mask, jnp.exp(log_beta + later), 0.0)
        return jnp.einsum('bhqk,bhkd->bhqd', a, vf)

    starts = jnp.arange(nb) * SB_Q_BLOCK
    o = lax.map(block, (qf, starts))
    return o.transpose(1, 0, 3, 2, 4).reshape(B, T, H * dh).astype(q.dtype)

def sb_mixer(h, k, v, w_q, w_out):
    B, T, _ = h.shape
    q = (h @ w_q).reshape(B, T, SB_HEADS, SB_HEAD_DIM)
    return stick_breaking_attention(q, k, v) @ w_out

def sq_relu_mlp(h, w1, b1, w2, b2):
    u = jax.nn.relu(h @ w1 + b1)
    return (u * u) @ w2 + b2

def setup_inputs(seed: int = 0) -> dict:
    key = jax.random.key(seed)
    ks = jax.random.split(key, 24)

    def nrm(k, shape, std):
        return jax.random.normal(k, shape, jnp.float32) * std

    d = D_MODEL
    gla_col_scale = jnp.concatenate([
        jnp.ones((2 * GLA_QK_DIM,), jnp.float32),
        jnp.full((GLA_V_DIM,), DEEPNORM_BETA, jnp.float32),
        jnp.ones((GLA_V_DIM + GLA_GATE_RANK,), jnp.float32)])
    kv_col_scale = jnp.concatenate([
        jnp.ones((SB_DIM,), jnp.float32), jnp.full((SB_DIM,), DEEPNORM_BETA, jnp.float32)])
    return {
        "x": nrm(ks[0], (BATCH, SEQ, d), 1.0),
        "c": nrm(ks[1], (BATCH, d), 1.0),
        "ada_w": nrm(ks[2], (DEPTH, d, N_MOD * d), 0.1 * d ** -0.5),
        "ada_b": nrm(ks[3], (DEPTH, N_MOD * d), 0.01),
        "ln_g": 1.0 + nrm(ks[4], (DEPTH, 2, d), 0.02),
        "ln_b": nrm(ks[5], (DEPTH, 2, d), 0.02),
        "gla_w_in": nrm(ks[6], (N_A_LAYERS, d, GLA_IN_DIM), d ** -0.5) * gla_col_scale,
        "gla_w_gate_up": nrm(ks[7], (N_A_LAYERS, GLA_GATE_RANK, GLA_QK_DIM), GLA_GATE_RANK ** -0.5),
        "gla_b_gate": nrm(ks[8], (N_A_LAYERS, GLA_QK_DIM), 0.5),
        "gla_norm_g": 1.0 + nrm(ks[9], (N_A_LAYERS, GLA_DV), 0.02),
        "gla_w_out": nrm(ks[10], (N_A_LAYERS, GLA_V_DIM, d), DEEPNORM_BETA * GLA_V_DIM ** -0.5),
        "kv_ada_w": nrm(ks[11], (d, 2 * d), 0.1 * d ** -0.5),
        "kv_ada_b": nrm(ks[12], (2 * d,), 0.01),
        "w_kv": nrm(ks[13], (d, 2 * SB_DIM), d ** -0.5) * kv_col_scale,
        "sb_w_q": nrm(ks[14], (N_B_LAYERS, d, SB_DIM), d ** -0.5),
        "sb_w_out": nrm(ks[15], (N_B_LAYERS, SB_DIM, d), DEEPNORM_BETA * SB_DIM ** -0.5),
        "mlp_w1": nrm(ks[16], (DEPTH, d, D_FF), d ** -0.5),
        "mlp_b1": nrm(ks[17], (DEPTH, D_FF), 0.02),
        "mlp_w2": nrm(ks[18], (DEPTH, D_FF, d), DEEPNORM_BETA * D_FF ** -0.5),
        "mlp_b2": nrm(ks[19], (DEPTH, d), 0.02),
    }

def reference(x, c, ada_w, ada_b, ln_g, ln_b, gla_w_in, gla_w_gate_up, gla_b_gate, gla_norm_g,
              gla_w_out, kv_ada_w, kv_ada_b, w_kv, sb_w_q, sb_w_out, mlp_w1, mlp_b1, mlp_w2, mlp_b2):
    cs = jax.nn.silu(c)
    k_shared = None
    v_shared = None
    for l in range(DEPTH):
        mod = (cs @ ada_w[l] + ada_b[l])[:, None, :]
        sh_a, sc_a, g_a, sh_m, sc_m, g_m = jnp.split(mod, N_MOD, axis=-1)
        h = x * (1.0 + sc_a) + sh_a
        if l < N_A_LAYERS:
            y = gla_mixer(h, gla_w_in[l], gla_w_gate_up[l], gla_b_gate[l], gla_norm_g[l], gla_w_out[l])
        else:
            if k_shared is None:
                k_shared, v_shared = shared_kv(x, cs, kv_ada_w, kv_ada_b, w_kv)
            j = l - N_A_LAYERS
            y = sb_mixer(h, k_shared, v_shared, sb_w_q[j], sb_w_out[j])
        x = layer_norm(DEEPNORM_ALPHA * x + (1.0 + g_a) * y, ln_g[l, 0], ln_b[l, 0])
        h = x * (1.0 + sc_m) + sh_m
        y = sq_relu_mlp(h, mlp_w1[l], mlp_b1[l], mlp_w2[l], mlp_b2[l])
        x = layer_norm(DEEPNORM_ALPHA * x + (1.0 + g_m) * y, ln_g[l, 1], ln_b[l, 1])
    return x


_drawn_inputs = setup_inputs


def setup_inputs(seed=0):
    import zlib

    import numpy as np

    out = dict(_drawn_inputs(seed))
    spreads = {}
    factors = {'ada_b': 4.379,
     'gla_norm_g': 25.36,
     'kv_ada_w': 4.094,
     'kv_ada_b': 25.624,
     'mlp_b1': 4.353,
     'mlp_b2': 2.965}
    for name, (base, spread) in spreads.items():
        noise = np.random.default_rng([zlib.crc32(name.encode()), seed]).standard_normal(out[name].shape)
        drawn = base * np.exp(spread * noise) if base else spread * noise
        out[name] = __import__('jax').numpy.asarray(drawn.astype(out[name].dtype))
    for name, factor in factors.items():
        out[name] = (out[name] * factor).astype(out[name].dtype)
    return out
```

```python
import concourse.bass as bass
import numpy as np
from concourse import mybir
from contextlib import ExitStack

P = 128
D = 2048
SEQ = 256
TOK = SEQ // P
KT = D // P
FF = 4 * D
RANK = 16
TAU = 16.0
CHUNK = 64
NCH = SEQ // CHUNK
GLA_H = 4
GLA_DK = D // 2 // GLA_H
GLA_DV = D // GLA_H
GJ = D // 2 // P
SB_H = 16
DH = D // SB_H
ALPHA = 4.0 ** 0.25
EPS = 1e-5

TW = 1024
SW = 512
ST = 8
BODY = 16
RING = 4
_sizes = [("gl", 4), ("gk", 16), ("gq", 16), ("gv", 32), ("gr", 32), ("go", 32),
          ("u0", 128), ("d0", 128), ("ak", 32), ("av", 32), ("aq", 32), ("ao", 32),
          ("u1", 128), ("d1", 128)]
T0 = {}
_at = 0
for _n, _s in _sizes:
    T0[_n] = _at
    _at += _s
N_TILES = _at

MODS = ["sc_a0", "sh_a0", "g_a0", "sh_m0", "sc_m0", "g_m0", "sh_k", "sc_k", "sh_a1", "sc_a1",
        "g_a1", "sh_m1", "sc_m1", "g_m1"]
MOD = {n: KT * i for i, n in enumerate(MODS)}
N_MODT = KT * len(MODS)
MOD_AT = {6: (1, 4, 6, 9, 12, 14), 4: (1, 5, 9, 13), 0: ()}
A0 = {"gk": 32, "gq": 38, "gv": 44, "gr": 56, "go": 68, "u0": 80, "d0": 112, "ak": 160, "av": 172,
      "aq": 184, "ao": 196, "u1": 208}
LEAD = 32

U0 = {"gk": 0, "gq": 2, "gv": 4, "gr": 8, "u0": 12, "ak": 28, "av": 32, "aq": 36, "u1": 40}
S0 = {"gk": 0, "gq": 2, "u0": 4, "ak": 20, "aq": 24, "u1": 28}
N_GLA_TURNED = 4
H_GLA, H_GLAO, H_M0, H_KV, H_Q, H_M1 = range(6)
PAIRS = KT // 2


def build_kernel(nc, tiles, mods, c_rows, x_rows, mod_b, ln_t, b1_t, bg_t, wgu, normg, ln_rows, b2_rows, out):
    F32, F32R = mybir.dt.float32, mybir.dt.float32r
    ACT, ALU = mybir.ActivationFunctionType, mybir.AluOpType
    ctx = ExitStack()
    with ctx:
        def sb(name, shape, dt=F32):
            return ctx.enter_context(nc.sbuf_tensor(name, shape, dt))

        def sem(name):
            return ctx.enter_context(nc.semaphore(name))

        raw = sb("raw", [P, RING, TW])
        w_hi = sb("w_hi", [P, RING, TW], F32R)
        w_lo = sb("w_lo", [P, RING, TW], F32R)
        mod_w = sb("mod_w", [P, 2, D])
        cs = sb("cs", [P, D])
        X = sb("X", [P, TOK, D])
        h_hi = sb("h_hi", [P, KT, SEQ], F32R)
        h_lo = sb("h_lo", [P, KT, SEQ], F32R)
        R = sb("R", [P, 8 * D])
        G = sb("G", [P, D])
        S = sb("S", [P, D])
        ident = sb("ident", [P, P])
        ones = sb("ones", [P, P])
        neg_ones = sb("neg_ones", [P, P])
        neg_later = sb("neg_later", [P, P])
        incl = sb("incl", [P, P])
        strict = sb("strict", [P, P])
        mod_t = sb("mod_t", [P, N_MODT])
        mod_bt = sb("mod_bt", [P, N_MODT])
        lnt = sb("lnt", [P, 4 * 2 * KT])
        b1t = sb("b1t", [P, 2 * FF // P])
        bgt = sb("bgt", [P, GJ])
        coef = sb("coef", [P, 4, KT])
        coef2 = sb("coef2", [P, 4, KT])
        stats = sb("stats", [P, TOK, 4, 6])
        mv = sb("mv", [P, TOK, 2])
        rstd = sb("rstd", [P, 8])
        ssq = sb("ssq", [P, 8])
        eps = sb("eps", [P, 1])
        ps = ctx.enter_context(nc.psum_tensor("ps", [P, 8, 512], F32))
        rows_buf, turned_buf = S[:, 0:TW], S[:, TW:2 * TW]

        gEq, gEki, gEks, gqd = (R[:, i * D:(i + 1) * D].rearrange("p (j t) -> p j t", j=GJ) for i in range(4))
        kk_at = [4 * D + GJ * CHUNK * (n * (n + 1) // 2) for n in range(NCH + 1)]
        KK = [R[:, kk_at[n]:kk_at[n + 1]].rearrange("p (j t) -> p j t", j=GJ) for n in range(NCH)]
        bc_f, tmp_f = R[:, 4 * D:5 * D], R[:, 5 * D:6 * D]
        reset_f, wgu_f = R[:, 3 * D:4 * D], R[:, 2 * D:2 * D + D // 2]
        SC = R[:, kk_at[NCH]:kk_at[NCH] + D].rearrange("p (h s t) -> p h s t", h=GLA_H, s=TOK)
        normg_sb = R[:, kk_at[NCH] + D:kk_at[NCH] + D + GLA_DV]
        gV = R[:, 0:2 * D].rearrange("p (a d) -> p a d", a=TOK)
        gR = R[:, 2 * D:4 * D].rearrange("p (a d) -> p a d", a=TOK)
        gO = R[:, 4 * D:6 * D].rearrange("p (a d) -> p a d", a=TOK)
        glT = S[:, 0:SEQ]
        decay = sb("decay", [P, GJ, NCH])
        kT = R[:, 0:2 * D].rearrange("p (h t) -> p h t", h=SB_H)
        aV = R[:, 2 * D:4 * D].rearrange("p (a d) -> p a d", a=TOK)
        qT = R[:, 4 * D:6 * D].rearrange("p (h t) -> p h t", h=SB_H)
        ZW = SEQ + P
        wk = [[R[:, 6 * D + (2 * a + b) * 2 * ZW:6 * D + (2 * a + b + 1) * 2 * ZW].rearrange("p (h c) -> p h c", h=2)
               for b in range(2)] for a in range(2)]
        ln_at = [5 * D, 6 * D, 5 * D, 0]
        Bg = [R[:, a:a + D] for a in ln_at]
        Bb = [R[:, a + D:a + 2 * D] for a in ln_at]
        B2 = R[:, 7 * D:8 * D]

        raw_loaded = [sem(f"raw_loaded{i}") for i in range(RING)]
        mod_loaded = [sem(f"mod_loaded{i}") for i in range(2)]
        c_loaded, x_loaded, setup_loaded = sem("c_loaded"), sem("x_loaded"), sem("setup_loaded")
        ln_loaded, out_stored = sem("ln_loaded"), sem("out_stored")
        consts_made = sem("consts_made")
        hi_ready, lo_ready, tile_used, mod_done = sem("hi_ready"), sem("lo_ready"), sem("tile_used"), sem("mod_done")
        cs_exp, cs_ready = sem("cs_exp"), sem("cs_ready")
        coef_ready, xn_ready, x_updated = sem("coef_ready"), sem("xn_ready"), sem("x_updated")
        h_turned, h_full, h_hi_ready, h_lo_ready = (sem(n) for n in ("h_turned", "h_full", "h_hi_ready", "h_lo_ready"))
        rows_copied, blocks_turned = sem("rows_copied"), sem("blocks_turned")
        turned_act, turned_dve, squared = sem("turned_act"), sem("turned_dve"), sem("squared")
        src_hi, src_lo = sem("src_hi"), sem("src_lo")
        g_diag, g_summed, g_copied = sem("g_diag"), sem("g_summed"), sem("g_copied")
        var_ready, rstd_ready = sem("var_ready"), sem("rstd_ready")
        act_step, dve_step = sem("act_step"), sem("dve_step")
        gl_copied, gate_done, gate_sum = sem("gl_copied"), sem("gate_done"), sem("gate_sum")
        gate_ln, bc_ready, decay_ready = sem("gate_ln"), sem("bc_ready"), sem("decay_ready")
        qk_ready, scores_done, scores_copied, scores_masked = (
            sem("qk_ready"), sem("scores_done"), sem("scores_copied"), sem("scores_masked"))
        r_exp, r_silu = sem("r_exp"), sem("r_silu")
        o_done, o_copied, o_squares, o_rstd, o_ready = (
            sem("o_done"), sem("o_copied"), sem("o_squares"), sem("o_rstd"), sem("o_ready"))
        z_done, z_ln, sp_ready, later_done, logit_ready, a_exp, a_ready, head_done, head_hi, head_lo = (
            sem(n) for n in ("z_done", "z_ln", "sp_ready", "later_done", "logit_ready", "a_exp", "a_ready",
                             "head_done", "head_hi", "head_lo"))

        block = ctx.enter_context(nc.Block())

        def mod_positions(per_body):
            return {j: i for i, j in enumerate(MOD_AT[per_body])}

        @block.sync
        def _(sp):
            sp.dma_start(cs[:], c_rows).then_inc(c_loaded, 16)

            def load_tile(t, slot, first=False):
                if not first:
                    sp.wait_ge(lo_ready, t - RING + 1)
                sp.dma_start(raw[:, slot, :], tiles[bass.ds(t, 1), :, :].rearrange("a p n -> p (a n)"))\
                  .then_inc(raw_loaded[slot], 16)

            def load_mod(a, slot, first=False):
                if not first:
                    sp.wait_ge(mod_done, a - 1)
                sp.dma_start(mod_w[:, slot, :], mods[bass.ds(a, 1), :, :].rearrange("a p n -> p (a n)"))\
                  .then_inc(mod_loaded[slot], 16)

            def body(t, a, per_body):
                at = mod_positions(per_body)
                for j in range(BODY):
                    load_tile(t + j, j % RING)
                    if j in at:
                        load_mod(a + at[j], at[j] % 2)

            load_mod(0, 0, first=True)
            load_mod(1, 1, first=True)
            sp.dma_start(X[:], x_rows).then_inc(x_loaded, 16)
            with sp.Fori(1, LEAD // 2) as i:
                load_mod(2 * i, 0)
                load_mod(2 * i + 1, 1)
            for j in range(4):
                load_tile(j, j, first=True)
            for t, a, bodies, per in ((T0["gk"], A0["gk"], 8, 6), (T0["u0"], A0["u0"], 8, 4), (T0["d0"], A0["d0"], 8, 6),
                                      (T0["ak"], A0["ak"], 8, 6), (T0["u1"], A0["u1"], 4, 4), (T0["u1"] + 64, 0, 12, 0)):
                with sp.Fori(0, bodies) as b:
                    body(t + BODY * b, a + per * b, per)
            for tok in range(TOK):
                sp.wait_ge(x_updated, 3 + tok + 1)
                sp.dma_start(out[tok * P:(tok + 1) * P, :], X[:, tok, :]).then_inc(out_stored, 16)
            sp.wait_ge(out_stored, 16 * TOK)

        @block.gpsimd
        def _(pool):
            for i, (dst, src) in enumerate(((mod_bt, mod_b), (lnt, ln_t), (b1t, b1_t), (bgt, bg_t))):
                pool.dma_start(dst[:], src).then_inc(setup_loaded, 16)
            pool.dma_start(wgu_f, wgu).then_inc(setup_loaded, 16)
            pool.dma_start(normg_sb, normg).then_inc(setup_loaded, 16)
            nc.gpsimd.memset(ident[:], 0.0).then_inc(consts_made, 1)
            nc.gpsimd.memset(ones[:], 1.0).then_inc(consts_made, 1)
            nc.gpsimd.memset(neg_ones[:], -1.0).then_inc(consts_made, 1)
            nc.gpsimd.memset(neg_later[:], -1.0).then_inc(consts_made, 1)
            nc.gpsimd.memset(incl[:], 1.0).then_inc(consts_made, 1)
            nc.gpsimd.memset(strict[:], 1.0).then_inc(consts_made, 1)
            nc.gpsimd.memset(eps[:], EPS).then_inc(consts_made, 1)
            nc.gpsimd.memset(SC, 0.0).then_inc(consts_made, 1)
            nc.gpsimd.memset(reset_f, 1.0).then_inc(consts_made, 1)
            pool.wait_ge(consts_made, 9)
            nc.gpsimd.memset(reset_f.rearrange("p (c t) -> p c t", t=CHUNK)[:, :, 0:1], 0.0).then_inc(consts_made, 1)
            nc.gpsimd.affine_select(out=ident[:], in_=ident[:], compare_op=ALU.not_equal, fill=1.0, base=0,
                                    pattern=[[-1, P]], channel_multiplier=1).then_inc(consts_made, 1)
            nc.gpsimd.affine_select(out=neg_later[:], in_=neg_later[:], compare_op=ALU.is_ge, fill=0.0, base=-1,
                                    pattern=[[-1, P]], channel_multiplier=1).then_inc(consts_made, 1)
            nc.gpsimd.affine_select(out=incl[:], in_=incl[:], compare_op=ALU.is_ge, fill=0.0, base=0,
                                    pattern=[[1, P]], channel_multiplier=-1).then_inc(consts_made, 1)
            nc.gpsimd.affine_select(out=strict[:], in_=strict[:], compare_op=ALU.is_ge, fill=0.0, base=-1,
                                    pattern=[[1, P]], channel_multiplier=-1).then_inc(consts_made, 1)

            def load_rows(l):
                pool.dma_start(Bg[l], ln_rows[l, 0, :, :]).then_inc(ln_loaded, 16)
                pool.dma_start(Bb[l], ln_rows[l, 1, :, :]).then_inc(ln_loaded, 16)

            pool.wait_ge(h_lo_ready, PAIRS * (H_GLAO + 1))
            load_rows(0)
            pool.dma_start(B2, b2_rows[0, :, :]).then_inc(ln_loaded, 16)
            pool.wait_ge(tile_used, T0["d0"] + 128)
            load_rows(1)
            pool.wait_ge(head_lo, SB_H // 2)
            load_rows(2)
            pool.dma_start(B2, b2_rows[1, :, :]).then_inc(ln_loaded, 16)
            pool.wait_ge(tile_used, T0["d1"] + 64 + 32)
            load_rows(3)

        CONSTS = 14
        HALF_END = [[T0[n] + k * (h + 1) for h in range(2)] for n, k in (("go", 16), ("d0", 64), ("ao", 16), ("d1", 64))]
        LN_LOADS = [48, 80, 128, 160]

        @block.scalar
        def _(act):
            steps = [0]

            def link(ins):
                steps[0] += 1
                ins.then_inc(act_step, 1)
                act.wait_ge(act_step, steps[0])

            def split_tile(t, slot, lap, first=False):
                act.wait_ge(raw_loaded[slot], 16 * lap)
                if not first:
                    act.wait_ge(tile_used, t - RING + 1)
                nc.scalar.activation(w_hi[:, slot, :], raw[:, slot, :], ACT.Copy).then_inc(hi_ready, 1)

            def body(t, hooks={}):
                for j in range(BODY):
                    split_tile(t + j, j % RING, (t // RING if isinstance(t, int) else t4(t)) + j // RING + 1)
                    for f in hooks.get(j, ()):
                        f()

            cur = {}

            def t4(t):
                return cur["t4"]

            def loop(t_first, n, make_hooks):
                with act.Fori(0, n) as b:
                    cur["t4"] = t_first // RING + (BODY // RING) * b
                    body(t_first + BODY * b, make_hooks(b))

            def rows_out(done, par, dst, s=None):
                def f():
                    act.wait_ge(tile_used, done)
                    if s is not None and not (isinstance(s, int) and s == 0):
                        act.wait_ge(blocks_turned, s)
                    nc.scalar.activation(dst, ps[:, 2 * par:2 * par + 2, :], ACT.Copy).then_inc(rows_copied, 1)
                return f

            def staged():
                return rows_buf.rearrange("p (a n) -> p a n", a=TOK)

            def relu(s, i, layer):
                def f():
                    act.wait_ge(blocks_turned, s + 1)
                    if isinstance(i, int) and i == 0 and layer == 0:
                        pass
                    else:
                        act.wait_ge(squared, 16 * layer + i)
                    for blk in range(4):
                        col = 64 * layer + 4 * i + blk
                        ins = nc.scalar.activation(turned_buf[:, blk * SEQ:(blk + 1) * SEQ], ps[:, 6 + blk // 2, (blk % 2) * SEQ:(blk % 2 + 1) * SEQ],
                                                   ACT.Relu, bias=b1t[:, bass.ds(col, 1)])
                    ins.then_inc(turned_act, 1)
                return f

            def keep_turned(s, dst, scale=1.0):
                def f():
                    act.wait_ge(blocks_turned, s + 1)
                    nc.scalar.activation(dst, ps[:, 6:8, :].rearrange("p a n -> p (a n)"), ACT.Copy, scale=scale)\
                      .then_inc(turned_act, 1)
                return f

            def h_full_pair(occ, pr, plain=False, co=None):
                act.wait_ge(h_turned, PAIRS * occ + pr + 1)
                if pr >= 2:
                    act.wait_ge(h_lo_ready, PAIRS * occ + pr - 1)
                full = turned_buf[:, (pr % 2) * 512:(pr % 2 + 1) * 512]
                if plain:
                    ins = nc.scalar.activation(full, ps[:, 4 + pr % 4, :], ACT.Copy)
                else:
                    for i in range(2):
                        kt = 2 * pr + i
                        ins = nc.scalar.activation(full[:, i * SEQ:(i + 1) * SEQ], ps[:, 4 + pr % 4, i * SEQ:(i + 1) * SEQ],
                                                   ACT.Identity, scale=co[:, 0, kt:kt + 1], bias=co[:, 1, kt:kt + 1])
                ins.then_inc(h_full, 1)

            def h_split_pair(occ, pr, used=None):
                act.wait_ge(h_full, PAIRS * occ + pr + 1)
                if used is not None:
                    act.wait_ge(tile_used, used)
                full = turned_buf[:, (pr % 2) * 512:(pr % 2 + 1) * 512]
                nc.scalar.activation(h_hi[:, 2 * pr:2 * pr + 2, :], full.rearrange("p (a t) -> p a t", a=2), ACT.Copy)\
                  .then_inc(h_hi_ready, 1)

            def h_build(occ, n_coef, co=None, plain=False):
                if not plain:
                    act.wait_ge(coef_ready, n_coef)
                h_full_pair(occ, 0, plain, co)
                for pr in range(PAIRS):
                    if pr + 1 < PAIRS:
                        h_full_pair(occ, pr + 1, plain, co)
                    h_split_pair(occ, pr)

            def gate_rows(occ):
                for r in range(2):
                    act.wait_ge(g_summed, 2 * occ + r + 1)
                    nc.scalar.activation(G[:, r * TW:(r + 1) * TW], ps[:, 4:6, :].rearrange("p a n -> p (a n)"), ACT.Copy)\
                      .then_inc(g_copied, 1)

            def norm_scale(occ):
                act.wait_ge(var_ready, occ + 1)
                link(nc.scalar.activation(rstd[:, 0:TOK], mv[:, :, 1], ACT.Ln, bias=eps[:]))
                nc.scalar.activation(rstd[:, 0:TOK], rstd[:, 0:TOK], ACT.Exp, scale=-0.5).then_inc(rstd_ready, 1)

            act.wait_ge(c_loaded, 16)
            nc.scalar.activation(S[:], cs[:], ACT.Exp, scale=-1.0).then_inc(cs_exp, 1)
            act.wait_ge(consts_made, CONSTS)
            act.wait_ge(setup_loaded, 96)
            h_build(H_GLA, 1, coef)
            for j in range(4):
                split_tile(j, j, 1, first=True)
            act.wait_ge(tile_used, 4)
            nc.scalar.activation(glT, ps[:, 0, 0:SEQ], ACT.Copy).then_inc(gl_copied, 1)
            act.wait_ge(gate_sum, 1)
            link(nc.scalar.activation(tmp_f, bc_f, ACT.Abs))
            link(nc.scalar.activation(tmp_f, tmp_f, ACT.Exp, scale=-1.0))
            nc.scalar.activation(tmp_f, tmp_f, ACT.Ln, bias=1.0).then_inc(gate_ln, 1)
            act.wait_ge(bc_ready, 1)
            flat = lambda v: v.rearrange("p j t -> p (j t)")
            nc.scalar.activation(flat(gEq), bc_f, ACT.Exp, scale=1.0 / TAU).then_inc(decay_ready, 1)
            nc.scalar.activation(flat(gEki), bc_f, ACT.Exp, scale=-1.0 / TAU).then_inc(decay_ready, 1)
            nc.scalar.activation(decay[:], bc_f.rearrange("p (j n t) -> p j n t", j=GJ, t=CHUNK)[:, :, :, CHUNK - 1],
                                 ACT.Exp, scale=1.0 / TAU).then_inc(decay_ready, 1)
            act.wait_ge(bc_ready, 2)
            nc.scalar.activation(flat(gEks), tmp_f, ACT.Exp, scale=1.0 / TAU).then_inc(decay_ready, 1)

            t = T0["gk"]
            body(t, {10: [rows_out(t + 8, 0, staged(), 0)]})
            body(t + 16, {2: [rows_out(t + 16, 1, staged(), 1)], 10: [rows_out(t + 24, 0, staged(), 2)]})

            def scores_out():
                act.wait_ge(scores_done, 1)
                nc.scalar.activation(SC[:, :, 0, P:SEQ], ps[:, 4:8, P:SEQ], ACT.Copy).then_inc(scores_copied, 1)

            def v_out(i, dst, t):
                return rows_out(t + ST * (i + 1), i % 2, dst[:, :, i * SW:(i + 1) * SW])

            t = T0["gv"]
            body(t, {2: [rows_out(t, 1, staged(), 3)], 15: [scores_out, v_out(0, gV, t)]})
            body(t + 16, {2: [v_out(1, gV, t)], 10: [v_out(2, gV, t)]})

            def r_out(i):
                def f():
                    v_out(i, gR, T0["gr"])()
                    if i:
                        act.wait_ge(r_silu, i)
                    else:
                        act.wait_ge(blocks_turned, N_GLA_TURNED)
                    act.wait_ge(rows_copied, U0["gr"] + i + 1)
                    nc.scalar.activation(staged(), gR[:, :, i * SW:(i + 1) * SW], ACT.Exp, scale=-1.0).then_inc(r_exp, 1)
                return f

            t = T0["gr"]
            body(t, {2: [v_out(3, gV, T0["gv"])], 10: [r_out(0)]})
            body(t + 16, {2: [r_out(1)], 10: [r_out(2)]})
            r_out(3)()
            gate_rows(0)
            for h in range(GLA_H):
                act.wait_ge(o_done, h + 1)
                nc.scalar.activation(gO[:, :, h * GLA_DV:(h + 1) * GLA_DV], ps[:, 2 * h:2 * h + 2, :], ACT.Copy).then_inc(o_copied, 1)
            act.wait_ge(o_squares, 1)
            link(nc.scalar.activation(rstd[:], ssq[:], ACT.Ln, scale=1.0 / GLA_DV, bias=eps[:]))
            nc.scalar.activation(rstd[:], rstd[:], ACT.Exp, scale=-0.5).then_inc(o_rstd, 1)
            h_build(H_GLAO, 0, plain=True)
            for i in range(2):
                body(T0["go"] + 16 * i)
            norm_scale(0)

            def mlp(layer):
                up, down, s = T0[f"u{layer}"], T0[f"d{layer}"], S0[f"u{layer}"]

                def hooks(b, first=False):
                    i, t = 2 * b, up + BODY * b
                    late = {10: [rows_out(t + 8, 0, staged(), s + i)], 14: [relu(s + i, i, layer)]}
                    early = {2: [rows_out(t, 1, staged(), s + i - 1)], 6: [relu(s + i - 1, i - 1, layer)]}
                    return late if first else {**late, **early}

                h_build(H_M0 if layer == 0 else H_M1, 2 if layer == 0 else 5, coef)
                body(up, hooks(0, first=True))
                loop(up + BODY, 5, lambda b: hooks(b + 1))
                gate_rows(1 + 2 * layer)
                loop(up + 6 * BODY, 2, lambda b: hooks(b + 6))

                def split_src(kt, slot, m):
                    def f():
                        act.wait_ge(tile_used, m)
                        act.wait_ge(squared, 16 * (layer + 1) if not isinstance(kt, int) else 16 * layer + 4)
                        nc.scalar.activation(h_hi[:, slot:slot + 2, :], R[:, bass.ds(kt * SEQ, 2 * SEQ)].rearrange("p (a t) -> p a t", a=2),
                                             ACT.Copy).then_inc(src_hi, 1)
                    return f

                def src_hooks(t, b, extra={}):
                    hooks = {j: [split_src(16 * b + j, j, t + j - 14)] for j in range(0, BODY, 2)}
                    for j, f in extra.items():
                        hooks[j] = f + hooks.get(j, [])
                    return hooks

                for half in range(2):
                    t = down + 64 * half
                    extra = {2: [rows_out(down, 1, staged(), s + 15)], 6: [relu(s + 15, 15, layer)]} if half == 0 else {}
                    body(t, src_hooks(t, 0, extra))
                    loop(t + BODY, 3, lambda b: src_hooks(t + BODY + BODY * b, b + 1))
                norm_scale(1 + 2 * layer)

            mlp(0)
            h_build(H_KV, 3, coef)
            t, s = T0["ak"], S0["ak"]

            def k_keep(i):
                return keep_turned(s + i, kT[:, 4 * i:4 * i + 4, :].rearrange("p h t -> p (h t)"))

            def q_keep(i):
                return keep_turned(S0["aq"] + i, qT[:, 4 * i:4 * i + 4, :].rearrange("p h t -> p (h t)"), DH ** -0.5)

            body(t, {10: [rows_out(t + 8, 0, staged(), s)], 14: [k_keep(0)]})
            body(t + 16, {2: [rows_out(t + 16, 1, staged(), s + 1)], 6: [k_keep(1)],
                          10: [rows_out(t + 24, 0, staged(), s + 2)], 14: [k_keep(2)]})
            t = T0["av"]
            body(t, {2: [rows_out(t, 1, staged(), s + 3)], 6: [k_keep(3)], 10: [v_out(0, aV, t)]})

            def q_pair(pr):
                def f():
                    if pr == 0:
                        act.wait_ge(coef_ready, 4)
                    h_full_pair(H_Q, pr, co=coef2)
                    h_split_pair(H_Q, pr, used=T0["aq"] - 8 + pr + 1)
                return f

            hooks = {8 + 3 + pr: [q_pair(pr)] for pr in range(5)}
            hooks[2] = [v_out(1, aV, t)]
            hooks[10] = [v_out(2, aV, t)]
            body(t + 16, hooks)
            t, s2 = T0["aq"], S0["aq"]
            body(t, {0: [q_pair(5)], 1: [q_pair(6)], 2: [q_pair(7), v_out(3, aV, T0["av"])],
                     10: [rows_out(t + 8, 0, staged(), s2)], 14: [q_keep(0)]})
            body(t + 16, {2: [rows_out(t + 16, 1, staged(), s2 + 1)], 6: [q_keep(1)],
                          10: [rows_out(t + 24, 0, staged(), s2 + 2)], 14: [q_keep(2)]})
            rows_out(t + 32, 1, staged(), s2 + 3)()
            q_keep(3)()
            gate_rows(2)

            def z_part(p):
                a = p % 2
                z, w1 = ps[:, 2 * a:2 * a + 2, 0:ZW], wk[a][0]
                act.wait_ge(z_done, p + 1)
                if p >= 2:
                    act.wait_ge(head_done, p - 1)
                else:
                    act.wait_ge(x_updated, 2)
                for f, kw in ((ACT.Abs, {}), (ACT.Exp, {"scale": -1.0})):
                    link(nc.scalar.activation(w1, z if f == ACT.Abs else w1, f, **kw))
                nc.scalar.activation(w1, w1, ACT.Ln, bias=1.0).then_inc(z_ln, 1)

            def a_part(p):
                act.wait_ge(logit_ready, p + 1)
                nc.scalar.activation(wk[p % 2][0], wk[p % 2][0], ACT.Exp).then_inc(a_exp, 1)

            def o_part(p):
                act.wait_ge(head_done, p + 1)
                nc.scalar.activation(h_hi[:, 2 * p:2 * p + 2, :], ps[:, 6 + p % 2, :].rearrange("p (a t) -> p a t", a=2), ACT.Copy)\
                  .then_inc(head_hi, 1)

            z_part(0)
            for p in range(SB_H // 2):
                if p + 1 < SB_H // 2:
                    z_part(p + 1)
                a_part(p)
                o_part(p)
            for i in range(2):
                body(T0["ao"] + 16 * i)
            norm_scale(2)
            mlp(1)

        @block.vector
        def _(dve):
            steps = [0]

            def link(ins):
                steps[0] += 1
                ins.then_inc(dve_step, 1)
                dve.wait_ge(dve_step, steps[0])

            def split_tile(t, slot, first=False):
                dve.wait_ge(hi_ready, t + 1)
                if not first:
                    dve.wait_ge(tile_used, t - RING + 1)
                nc.vector.tensor_tensor(w_lo[:, slot, :], raw[:, slot, :], w_hi[:, slot, :].bitcast(F32), ALU.subtract)\
                  .then_inc(lo_ready, 1)

            def mod_tile(a, slot, lap):
                dve.wait_ge(mod_loaded[slot], 16 * lap)
                nc.vector.scalar_tensor_tensor(mod_w[:, slot, :], mod_w[:, slot, :], 1.0, cs[:], ALU.mult, ALU.mult,
                                               accum_out=mod_t[:, bass.ds(a, 1)]).then_inc(mod_done, 1)

            def body(t, a, half_a, per, hooks={}):
                at = mod_positions(per)
                for j in range(BODY):
                    split_tile(t + j, j % RING)
                    if j in at:
                        mod_tile(a + at[j], at[j] % 2, half_a + at[j] // 2 + 1)
                    for f in hooks.get(j, ()):
                        f()

            def run(t, a, per, hooks={}):
                body(t, a, a // 2, per, hooks)

            def loop(t_first, a_first, per, n, make_hooks):
                with dve.Fori(0, n) as b:
                    body(t_first + BODY * b, a_first + per * b, a_first // 2 + (per // 2) * b, per, make_hooks(b))

            def make_coef(co, scale, shift, ln=None):
                sc, sh = MOD[scale], MOD[shift]
                dve.wait_ge(mod_done, max(sc, sh) + KT)
                link(nc.vector.tensor_tensor(co[:, 2, :], mod_t[:, sc:sc + KT], mod_bt[:, sc:sc + KT], ALU.add))
                link(nc.vector.tensor_tensor(co[:, 1, :], mod_t[:, sh:sh + KT], mod_bt[:, sh:sh + KT], ALU.add))
                if ln is None:
                    nc.vector.tensor_scalar(co[:, 0, :], co[:, 2, :], 1.0, None, ALU.add).then_inc(coef_ready, 1)
                else:
                    g, b = lnt[:, 2 * ln * KT:(2 * ln + 1) * KT], lnt[:, (2 * ln + 1) * KT:(2 * ln + 2) * KT]
                    link(nc.vector.scalar_tensor_tensor(co[:, 3, :], co[:, 2, :], 1.0, b, ALU.add, ALU.mult))
                    link(nc.vector.tensor_tensor(co[:, 1, :], co[:, 1, :], co[:, 3, :], ALU.add))
                    nc.vector.scalar_tensor_tensor(co[:, 0, :], co[:, 2, :], 1.0, g, ALU.add, ALU.mult).then_inc(coef_ready, 1)

            def h_pair(occ, pr):
                dve.wait_ge(h_hi_ready, PAIRS * occ + pr + 1)
                full = turned_buf[:, (pr % 2) * 512:(pr % 2 + 1) * 512]
                nc.vector.tensor_tensor(h_lo[:, 2 * pr:2 * pr + 2, :], full.rearrange("p (a t) -> p a t", a=2),
                                        h_hi[:, 2 * pr:2 * pr + 2, :].bitcast(F32), ALU.subtract).then_inc(h_lo_ready, 1)

            def h_build(occ):
                for pr in range(PAIRS):
                    h_pair(occ, pr)

            def gate_diag(occ, name):
                g = MOD[name]
                dve.wait_ge(mod_done, g + KT)
                link(nc.vector.scalar_tensor_tensor(coef[:, 2, :], mod_t[:, g:g + KT], 1.0, mod_bt[:, g:g + KT], ALU.add, ALU.add))
                nc.vector.tensor_tensor(G[:].rearrange("p (j n) -> p j n", n=P), ident[:].unsqueeze(1).to_broadcast([P, KT, P]),
                                        coef[:, 2, :].unsqueeze(2).to_broadcast([P, KT, P]), ALU.mult).then_inc(g_diag, 1)

            def residual(occ, half, tok, alpha):
                bank = {(0, 0): 0, (0, 1): 4, (1, 0): 2, (1, 1): 6}[half, tok]
                cols = slice(half * TW, (half + 1) * TW)
                stage = S[:, tok * TW:(tok + 1) * TW]
                dve.wait_ge(tile_used, HALF_END[occ][half])
                dve.wait_ge(g_copied, 2 * occ + 2)
                link(nc.vector.tensor_tensor(stage, ps[:, bank:bank + 2, :].rearrange("p a n -> p (a n)"), G[:, cols], ALU.mult))
                link(nc.vector.scalar_tensor_tensor(X[:, tok, cols], X[:, tok, cols], alpha, stage, ALU.mult, ALU.add))
                for i in range(2):
                    ins = nc.vector.bn_stats(stats[:, tok, 2 * half + i, :], X[:, tok, half * TW + i * 512:half * TW + (i + 1) * 512])
                return ins

            def normalise(occ, alpha):
                for tok in range(TOK):
                    link(residual(occ, 1, tok, alpha))
                for tok in range(TOK):
                    ins = nc.vector.bn_aggr(mv[:, tok, :], stats[:, tok, :, :].rearrange("p a b -> p (a b)"))
                ins.then_inc(var_ready, 1)
                dve.wait_ge(var_ready, occ + 1)
                dve.wait_ge(rstd_ready, occ + 1)
                for tok in range(TOK):
                    nc.vector.tensor_scalar(X[:, tok, :], X[:, tok, :], mv[:, tok, 0:1], rstd[:, tok:tok + 1],
                                            ALU.subtract, ALU.mult).then_inc(xn_ready, 1)

            def half0(occ, alpha):
                return {4: [lambda: link(residual(occ, 0, 0, alpha))], 7: [lambda: link(residual(occ, 0, 1, alpha))]}

            def update_piece(l, q, mult):
                tok, cols = q // 2, slice((q % 2) * TW, (q % 2 + 1) * TW)

                def f():
                    if q == 0 and mult:
                        dve.wait_ge(ln_loaded, LN_LOADS[l])
                        dve.wait_ge(h_turned, PAIRS * {0: H_M0, 1: H_Q, 2: H_M1}[l] + PAIRS)
                        dve.wait_ge(xn_ready, 2 * (l + 1))
                    row = (Bg if mult else Bb)[l][:, cols]
                    ins = nc.vector.tensor_tensor(X[:, tok, cols], X[:, tok, cols], row, ALU.mult if mult else ALU.add)
                    if q == 3 and not mult:
                        ins.then_inc(x_updated, 1)
                    else:
                        link(ins)
                return f

            def update_hooks(l, positions):
                pieces = [update_piece(l, q, m) for q in range(4) for m in (True, False)]
                return {j: [f] for j, f in zip(positions, pieces)}

            def merge(a, b):
                return {j: a.get(j, []) + b.get(j, []) for j in {*a, *b}}

            dve.wait_ge(cs_exp, 1)
            link(nc.vector.tensor_scalar(S[:], S[:], 1.0, None, ALU.add))
            link(nc.vector.reciprocal(S[:], S[:]))
            nc.vector.tensor_tensor(cs[:], cs[:], S[:], ALU.mult).then_inc(cs_ready, 1)
            dve.wait_ge(cs_ready, 1)
            with dve.Fori(0, LEAD // 2) as i:
                mod_tile(2 * i, 0, i + 1)
                mod_tile(2 * i + 1, 1, i + 1)
            dve.wait_ge(setup_loaded, 96)
            dve.wait_ge(consts_made, CONSTS)
            make_coef(coef, "sc_a0", "sh_a0")
            h_build(H_GLA)
            for j in range(4):
                split_tile(j, j, first=True)
            g3 = lambda v: v.rearrange("p (j t) -> p j t", j=GJ)
            dve.wait_ge(gate_done, 1)
            nc.vector.tensor_tensor(g3(bc_f), ps[:, 4:8, :].rearrange("p a (b t) -> p (a b) t", b=2),
                                    bgt[:].unsqueeze(2).to_broadcast([P, GJ, SEQ]), ALU.add).then_inc(gate_sum, 1)
            dve.wait_ge(gate_sum, 1)
            dve.wait_ge(gate_ln, 1)
            link(nc.vector.scalar_tensor_tensor(tmp_f, bc_f, 0.0, tmp_f, ALU.min, ALU.subtract))
            nc.vector.tensor_tensor_scan(bc_f, reset_f, tmp_f, 0.0, ALU.mult, ALU.add).then_inc(bc_ready, 1)
            dve.wait_ge(bc_ready, 1)
            bc4 = bc_f.rearrange("p (c t) -> p c t", t=CHUNK)
            nc.vector.tensor_tensor(tmp_f.rearrange("p (c t) -> p c t", t=CHUNK),
                                    bc4[:, :, CHUNK - 1:CHUNK].to_broadcast([P, GJ * NCH, CHUNK]), bc4, ALU.subtract)\
              .then_inc(bc_ready, 1)

            def gla_keys(i):
                def f():
                    dve.wait_ge(blocks_turned, S0["gk"] + i + 1)
                    dve.wait_ge(decay_ready, 4)
                    turned = ps[:, 6:8, :].rearrange("p a (b t) -> p (a b) t", b=2)
                    js = slice(4 * i, 4 * i + 4)
                    for n in range(NCH):
                        c = slice(n * CHUNK, (n + 1) * CHUNK)
                        ins = nc.vector.tensor_tensor(KK[n][:, js, c], turned[:, :, c], gEki[:, js, c], ALU.mult)
                        if n + 1 < NCH:
                            ins = nc.vector.tensor_tensor(KK[n + 1][:, js, c], turned[:, :, c], gEks[:, js, c], ALU.mult)
                    ins.then_inc(turned_dve, 1)
                return f

            def gla_decayed():
                dve.wait_ge(turned_dve, 2)
                for n in (2, 3):
                    w = CHUNK * (n - 1)
                    link(nc.vector.tensor_tensor(KK[n][:, :, 0:w], KK[n - 1][:, :, 0:w],
                                                 decay[:, :, n - 1:n].to_broadcast([P, GJ, w]), ALU.mult))

            def gla_queries(i):
                def f():
                    dve.wait_ge(blocks_turned, S0["gq"] + i + 1)
                    turned = ps[:, 6:8, :].rearrange("p a n -> p (a n)")
                    js = slice(4 * i, 4 * i + 4)
                    nc.vector.scalar_tensor_tensor(gqd[:, js, :].rearrange("p j t -> p (j t)"), turned, GLA_DK ** -0.5,
                                                   gEq[:, js, :].rearrange("p j t -> p (j t)"), ALU.mult, ALU.mult)\
                      .then_inc(turned_dve, 1)
                return f

            def scores_masked_out():
                dve.wait_ge(scores_copied, 1)
                for st in range(TOK):
                    lo = slice(st * SEQ + st * P, st * SEQ + st * P + CHUNK)
                    hi = slice(st * SEQ + st * P + CHUNK, st * SEQ + (st + 1) * P)
                    nc.vector.tensor_tensor(SC[0:CHUNK, :, st, st * P:st * P + CHUNK], ps[0:CHUNK, 4:8, lo],
                                            incl[0:CHUNK, 0:CHUNK].unsqueeze(1).to_broadcast([CHUNK, GLA_H, CHUNK]), ALU.mult)
                    ins = nc.vector.tensor_tensor(SC[:, :, st, st * P + CHUNK:(st + 1) * P], ps[:, 4:8, hi],
                                                  incl[:, CHUNK:P].unsqueeze(1).to_broadcast([P, GLA_H, CHUNK]), ALU.mult)
                ins.then_inc(scores_masked, 1)

            t, a = T0["gk"], A0["gk"]
            run(t, a, 6, {15: [gla_keys(0)]})
            run(t + 16, a + 6, 6, {7: [gla_keys(1)], 8: [gla_decayed], 15: [gla_queries(0)]})
            t, a = T0["gv"], A0["gv"]
            run(t, a, 6, {7: [gla_queries(1)], 15: [scores_masked_out]})
            run(t + 16, a + 6, 6)

            def silu_r(i):
                def f():
                    dve.wait_ge(r_exp, i + 1)
                    link(nc.vector.tensor_scalar(rows_buf, rows_buf, 1.0, None, ALU.add))
                    link(nc.vector.reciprocal(rows_buf, rows_buf))
                    part = gR[:, :, i * SW:(i + 1) * SW]
                    nc.vector.tensor_tensor(part, part, rows_buf.rearrange("p (a n) -> p a n", a=TOK), ALU.mult).then_inc(r_silu, 1)
                return f

            t, a = T0["gr"], A0["gr"]
            run(t, a, 6, {13: [silu_r(0)]})
            run(t + 16, a + 6, 6, {5: [silu_r(1)], 13: [silu_r(2)]})
            gate_diag(0, "g_a0")
            silu_r(3)()
            for h in range(GLA_H):
                dve.wait_ge(o_copied, h + 1)
                for tok in range(TOK):
                    o = gO[:, tok, h * GLA_DV:(h + 1) * GLA_DV]
                    ins = nc.vector.scalar_tensor_tensor(turned_buf[:, 0:GLA_DV], o, 1.0, o, ALU.mult, ALU.mult,
                                                         accum_out=ssq[:, 2 * h + tok:2 * h + tok + 1])
                    if (h, tok) != (GLA_H - 1, TOK - 1):
                        link(ins)
            ins.then_inc(o_squares, 1)
            dve.wait_ge(o_rstd, 1)
            for h in range(GLA_H):
                for tok in range(TOK):
                    o = gO[:, tok, h * GLA_DV:(h + 1) * GLA_DV]
                    ins = nc.vector.scalar_tensor_tensor(o, o, rstd[:, 2 * h + tok:2 * h + tok + 1], normg_sb, ALU.mult, ALU.mult)
            link(ins)
            for q in range(4):
                tok, cols = q // 2, slice((q % 2) * TW, (q % 2 + 1) * TW)
                ins = nc.vector.tensor_tensor(gO[:, tok, cols], gO[:, tok, cols], gR[:, tok, cols], ALU.mult)
            ins.then_inc(o_ready, 1)
            h_build(H_GLAO)
            t, a = T0["go"], A0["go"]
            run(t, a, 6)
            run(t + 16, a + 6, 6, half0(0, ALPHA))
            make_coef(coef, "sc_m0", "sh_m0", 0)
            normalise(0, ALPHA)

            def mlp(layer):
                up, down, s = T0[f"u{layer}"], T0[f"d{layer}"], S0[f"u{layer}"]
                a_up, l = A0[f"u{layer}"], 2 * layer
                per_down = 6 if layer == 0 else 0
                a_down = A0["d0"] if layer == 0 else 0

                def square(i):
                    def f():
                        dve.wait_ge(turned_act, s - N_GLA_TURNED + i + 1)
                        nc.vector.tensor_tensor(R[:, bass.ds(i * TW, TW)], turned_buf, turned_buf, ALU.mult).then_inc(squared, 1)
                    return f

                def hooks(b, first=False):
                    late = {15: [square(2 * b)]}
                    return late if first else {**late, 7: [square(2 * b - 1)]}

                h_build(H_M0 if layer == 0 else H_M1)
                run(up, a_up, 4, merge(update_hooks(l, (2, 3, 6, 7, 10, 11, 14, 15)), hooks(0, first=True)))
                if layer == 0:
                    loop(up + BODY, a_up + 4, 4, 5, lambda b: hooks(b + 1))
                else:
                    loop(up + BODY, a_up + 4, 4, 3, lambda b: hooks(b + 1))
                    loop(up + 4 * BODY, 0, 0, 2, lambda b: hooks(b + 4))
                gate_diag(1 + 2 * layer, f"g_m{layer}")
                dve.wait_ge(g_copied, 4 + 4 * layer)
                dve.wait_ge(x_updated, l + 1)
                link(nc.vector.tensor_tensor(B2, B2, G[:], ALU.mult))
                for tok in range(TOK):
                    link(nc.vector.scalar_tensor_tensor(X[:, tok, :], X[:, tok, :], ALPHA, B2, ALU.mult, ALU.add))
                if layer == 0:
                    loop(up + 6 * BODY, a_up + 24, 4, 2, lambda b: hooks(b + 6))
                else:
                    loop(up + 6 * BODY, 0, 0, 2, lambda b: hooks(b + 6))

                def split_src(kt, slot, m):
                    def f():
                        dve.wait_ge(src_hi, m)
                        dve.wait_ge(squared, 16 * (layer + 1) if not isinstance(kt, int) else 16 * layer + 4)
                        nc.vector.tensor_tensor(h_lo[:, slot:slot + 2, :], R[:, bass.ds(kt * SEQ, 2 * SEQ)].rearrange("p (a t) -> p a t", a=2),
                                                h_hi[:, slot:slot + 2, :].bitcast(F32), ALU.subtract).then_inc(src_lo, 1)
                    return f

                for half in range(2):
                    t = down + 64 * half
                    m = 64 * layer + 32 * half

                    def src_hooks(b, m=m):
                        return {j: [split_src(16 * b + j, j, m + 8 * b + j // 2 + 1)] for j in range(0, BODY, 2)}

                    extra = {7: [square(15)]} if half == 0 else half0(1 + 2 * layer, 1.0)
                    run(t, a_down + 4 * per_down * half, per_down, merge(src_hooks(0), extra))
                    loop(t + BODY, a_down + 4 * per_down * half + per_down, per_down, 3, lambda b: src_hooks(b + 1))

            mlp(0)
            make_coef(coef, "sc_k", "sh_k", 1)
            make_coef(coef2, "sc_a1", "sh_a1", 1)
            normalise(1, 1.0)
            h_build(H_KV)
            t, a = T0["ak"], A0["ak"]
            run(t, a, 6)
            run(t + 16, a + 6, 6)
            t, a = T0["av"], A0["av"]
            run(t, a, 6)
            q_pair = lambda pr: (lambda: h_pair(H_Q, pr))
            run(t + 16, a + 6, 6, {11 + pr: [q_pair(pr)] for pr in range(5)})
            t, a = T0["aq"], A0["aq"]
            run(t, a, 6, merge({0: [q_pair(5)], 1: [q_pair(6)], 2: [q_pair(7)]}, update_hooks(1, (3, 5, 7, 8, 10, 11, 13, 15))))
            run(t + 16, a + 6, 6)
            gate_diag(2, "g_a1")

            def diag(w, sem_done):
                for h in range(2):
                    v = w[:, h, :].rearrange("p (b c) -> p b c", c=P)[:, 0:3:2, :]
                    ins = nc.vector.tensor_tensor(v, v, strict[:].unsqueeze(1).to_broadcast([P, 2, P]), ALU.mult)
                ins.then_inc(sem_done, 1)

            def z_part(p):
                a = p % 2
                z, w1, w2 = ps[:, 2 * a:2 * a + 2, 0:ZW], wk[a][0], wk[a][1]
                dve.wait_ge(z_ln, p + 1)
                link(nc.vector.scalar_tensor_tensor(w2, z, 0.0, w1, ALU.max, ALU.add))
                link(nc.vector.tensor_tensor(w1, z, w2, ALU.subtract))
                diag(w2, sp_ready)

            def a_part(p):
                w1 = wk[p % 2][0]
                dve.wait_ge(later_done, p + 1)
                nc.vector.tensor_tensor(w1, w1, ps[:, 4:6, 0:ZW], ALU.add).then_inc(logit_ready, 1)
                dve.wait_ge(a_exp, p + 1)
                diag(w1, a_ready)

            def o_part(p):
                dve.wait_ge(head_hi, p + 1)
                nc.vector.tensor_tensor(h_lo[:, 2 * p:2 * p + 2, :], ps[:, 6 + p % 2, :].rearrange("p (a t) -> p a t", a=2),
                                        h_hi[:, 2 * p:2 * p + 2, :].bitcast(F32), ALU.subtract).then_inc(head_lo, 1)

            z_part(0)
            for p in range(SB_H // 2):
                if p + 1 < SB_H // 2:
                    z_part(p + 1)
                a_part(p)
                o_part(p)
            t, a = T0["ao"], A0["ao"]
            run(t, a, 6)
            run(t + 16, a + 6, 6, half0(2, ALPHA))
            make_coef(coef, "sc_m1", "sh_m1", 2)
            normalise(2, ALPHA)
            mlp(1)
            normalise(3, 1.0)
            dve.wait_ge(ln_loaded, LN_LOADS[3])
            dve.wait_ge(xn_ready, 8)
            for tok in range(TOK):
                link(nc.vector.tensor_tensor(X[:, tok, :], X[:, tok, :], Bg[3], ALU.mult))
                nc.vector.tensor_tensor(X[:, tok, :], X[:, tok, :], Bb[3], ALU.add).then_inc(x_updated, 1)

        @block.tensor
        def _(pe):
            mm = nc.tensor.matmul

            def product(dst, hs, ws, start, stop, more=False):
                hh, hl = hs
                wh, wl = ws
                mm(dst, hh, wh, start=start, stop=False, skip_group_check=more)
                mm(dst, hh, wl, start=False, stop=False, skip_group_check=more)
                return mm(dst, hl, wh, start=False, stop=stop, skip_group_check=more)

            def h_part(kt, tok):
                c = slice(tok * P, (tok + 1) * P)
                return h_hi[:, kt, c], h_lo[:, kt, c]

            def w_part(slot, c):
                return w_hi[:, slot, c], w_lo[:, slot, c]

            def stripe_tile(t, j, par, inputs=None):
                pe.wait_ge(lo_ready, t + 1)
                if inputs is not None:
                    pe.wait_ge(h_lo_ready, inputs)
                slot = j % RING
                for i in range(2):
                    kt = 2 * (j % ST) + i
                    for tok in range(TOK):
                        last = product(ps[:, 2 * par + tok, :], h_part(kt, tok), w_part(slot, slice(i * SW, (i + 1) * SW)),
                                       kt == 0, kt == KT - 1)
                last.then_inc(tile_used, 1)

            def stripes(t, u, occ=None, hooks={}):
                for j in range(BODY):
                    if j % ST == 0 and not (isinstance(u, int) and u + j // ST < 2):
                        pe.wait_ge(rows_copied, u + j // ST - 1)
                    stripe_tile(t + j, j, j // ST, None if occ is None or j >= ST else PAIRS * occ + j + 1)
                    for f in hooks.get(j, ()):
                        f()

            def turn(u, s, freed):
                def f():
                    pe.wait_ge(rows_copied, u + 1)
                    for sm, v in freed:
                        pe.wait_ge(sm, v)
                    for blk in range(4):
                        for tok in range(TOK):
                            o = (blk % 2) * SEQ + tok * P
                            last = nc.tensor.transpose(ps[:, 6 + blk // 2, o:o + P],
                                                       rows_buf[:, tok * SW + blk * P:tok * SW + (blk + 1) * P], ident[:])
                    last.then_inc(blocks_turned, 1)
                return f

            def turn_pair(occ, pr, src):
                if pr >= 4:
                    pe.wait_ge(h_lo_ready, PAIRS * occ + pr - 3)
                for i in range(2):
                    kt = 2 * pr + i
                    for tok in range(TOK):
                        last = nc.tensor.transpose(ps[:, 4 + pr % 4, i * SEQ + tok * P:i * SEQ + (tok + 1) * P],
                                                   src[:, tok, kt * P:(kt + 1) * P], ident[:])
                last.then_inc(h_turned, 1)

            def turn_all(occ, src):
                for pr in range(PAIRS):
                    turn_pair(occ, pr, src)

            def gate_sums(occ):
                pe.wait_ge(g_diag, occ + 1)
                for r in range(2):
                    if r:
                        pe.wait_ge(g_copied, 2 * occ + 1)
                    for n in range(2):
                        last = mm(ps[:, 4 + n, :], ones[:], G[:, r * TW + n * 512:r * TW + (n + 1) * 512], start=True, stop=True)
                    last.then_inc(g_summed, 1)

            HALF_BANKS = {0: (0, 4), 1: (2, 6)}

            def wide(t, half, first, src, hooks={}):
                for j in range(BODY):
                    pe.wait_ge(lo_ready, t + j + 1)
                    if src(j) is not None:
                        pe.wait_ge(*src(j))
                    for tok in range(TOK):
                        for n in range(2):
                            ins = product(ps[:, HALF_BANKS[half][tok] + n, :], h_part(j, tok), w_part(j % RING, slice(n * SW, (n + 1) * SW)),
                                          first and j == 0, first and j == BODY - 1, more=not first)
                    ins.then_inc(tile_used, 1)
                    for f in hooks.get(j, ()):
                        f()

            pe.wait_ge(x_loaded, 16)
            pe.wait_ge(consts_made, CONSTS)
            turn_all(H_GLA, X)
            pe.wait_ge(h_lo_ready, PAIRS)
            for j in range(4):
                pe.wait_ge(lo_ready, j + 1)
                for i in range(4):
                    kt = 4 * j + i
                    c = slice(i * SEQ, i * SEQ + P)
                    last = product(ps[:, 0, 0:SEQ], (w_hi[:, j, c], w_lo[:, j, c]), (h_hi[:, kt, :], h_lo[:, kt, :]), kt == 0, kt == KT - 1)
                last.then_inc(tile_used, 1)
            pe.wait_ge(gl_copied, 1)
            pe.wait_ge(setup_loaded, 96)
            for j in range(GJ):
                last = mm(ps[:, 4 + j // 2, (j % 2) * SEQ:(j % 2 + 1) * SEQ], wgu_f[:, j * P:(j + 1) * P], glT, start=True, stop=True)
            last.then_inc(gate_done, 1)

            t, u, s = T0["gk"], U0["gk"], S0["gk"]
            stripes(t, u, H_GLA, {11: [turn(u, 0, [(gate_sum, 1)])]})
            stripes(t + 16, u + 2, None, {3: [turn(u + 1, 1, [(turned_dve, 1)])], 11: [turn(u + 2, 2, [(turned_dve, 2)])]})

            def scores():
                pe.wait_ge(turned_dve, 4)
                for h in range(GLA_H):
                    for n in range(NCH):
                        for st in range(n // 2 + 1):
                            m = min(P, CHUNK * (n + 1) - st * P)
                            for j in (2 * h, 2 * h + 1):
                                last = mm(ps[0:m, 4 + h, st * SEQ + n * CHUNK:st * SEQ + (n + 1) * CHUNK],
                                          KK[n][:, j, st * P:st * P + m], gqd[:, j, n * CHUNK:(n + 1) * CHUNK],
                                          start=j % 2 == 0, stop=j % 2 == 1)
                last.then_inc(scores_done, 1)

            t, u = T0["gv"], U0["gv"]
            stripes(t, u, None, {3: [turn(u - 1, 3, [(turned_dve, 3)])], 11: [scores]})
            stripes(t + 16, u + 2)
            t, u = T0["gr"], U0["gr"]
            stripes(t, u)
            stripes(t + 16, u + 2)
            pe.wait_ge(scores_copied, 1)
            pe.wait_ge(scores_masked, 1)
            gate_sums(0)
            pe.wait_ge(g_copied, 2)
            pe.wait_ge(rows_copied, u + 4)
            for h in range(GLA_H):
                for tok in range(TOK):
                    for st in range(tok + 1):
                        last = mm(ps[:, 2 * h + tok, :], SC[:, h, st, tok * P:(tok + 1) * P],
                                  gV[:, st, h * GLA_DV:(h + 1) * GLA_DV], start=st == 0, stop=st == tok)
                last.then_inc(o_done, 1)
            pe.wait_ge(o_ready, 1)
            turn_all(H_GLAO, gO)

            def narrow_input(occ):
                return lambda j: (h_lo_ready, PAIRS * occ + j // 2 + 1)

            for half in range(2):
                wide(T0["go"] + 16 * half, half, True, narrow_input(H_GLAO))

            def mlp(layer):
                up, down, u, s = T0[f"u{layer}"], T0[f"d{layer}"], U0[f"u{layer}"], S0[f"u{layer}"]
                occ = H_M0 if layer == 0 else H_M1
                pe.wait_ge(xn_ready, 2 + 4 * layer)
                turn_all(occ, X)

                def freed(s):
                    return [] if isinstance(s, int) and s == N_GLA_TURNED else [(turned_act, s - N_GLA_TURNED)]

                def hooks(b, first=False):
                    i = 2 * b
                    late = {11: [turn(u + i, s + i, freed(s + i))]}
                    return late if first else {**late, 3: [turn(u + i - 1, s + i - 1, freed(s + i - 1))]}

                stripes(up, u, occ, hooks(0, first=True))
                with pe.Fori(1, 6) as b:
                    stripes(up + BODY * b, u + 2 * b, None, hooks(b))
                gate_sums(1 + 2 * layer)
                with pe.Fori(6, 8) as b:
                    stripes(up + BODY * b, u + 2 * b, None, hooks(b))

                for half in range(2):
                    m = 64 * layer + 32 * half

                    def src(b, m=m):
                        return lambda j: (src_lo, m + 8 * b + j // 2 + 1)

                    if half == 0:
                        pe.wait_ge(rows_copied, u + 15)
                        pe.wait_ge(g_copied, 4 + 4 * layer)
                    else:
                        pe.wait_ge(rows_copied, u + 16)
                        pe.wait_ge(turned_act, s - N_GLA_TURNED + 16)
                    t = down + 64 * half
                    wide(t, half, True, src(0), {3: [turn(u + 15, s + 15, freed(s + 15))]} if half == 0 else {})
                    with pe.Fori(1, 4) as b:
                        wide(t + BODY * b, half, False, src(b))

            mlp(0)
            pe.wait_ge(xn_ready, 4)
            turn_all(H_KV, X)
            t, u, s = T0["ak"], U0["ak"], S0["ak"]
            at = lambda i: turn(u + i, s + i, [(turned_act, s + i - N_GLA_TURNED)])
            stripes(t, u, H_KV, {11: [at(0)]})
            stripes(t + 16, u + 2, None, {3: [at(1)], 11: [at(2)]})
            stripes(T0["av"], u + 4, None, {3: [at(3)]})

            def q_pair(pr):
                def f():
                    if pr == 0:
                        pe.wait_ge(turned_act, s + 4 - N_GLA_TURNED)
                    turn_pair(H_Q, pr, X)
                return f

            stripes(T0["av"] + 16, u + 6, None, {8 + pr: [q_pair(pr)] for pr in range(PAIRS)})
            t, u, s = T0["aq"], U0["aq"], S0["aq"]
            stripes(t, u, H_Q, {11: [turn(u, s, [(h_lo_ready, PAIRS * (H_Q + 1))])]})
            nxt = lambda i: turn(u + i, s + i, [(turned_act, s + i - N_GLA_TURNED)])
            stripes(t + 16, u + 2, None, {3: [nxt(1)], 11: [nxt(2)]})
            nxt(3)()
            gate_sums(2)
            pe.wait_ge(g_copied, 6)
            pe.wait_ge(turned_act, s + 4 - N_GLA_TURNED)
            pe.wait_ge(rows_copied, u + 4)

            def z_part(p):
                for i in range(2):
                    h, bank = 2 * p + i, 2 * (p % 2) + i
                    mm(ps[:, bank, 0:SEQ], kT[:, h, 0:P], qT[:, h, :], start=True, stop=True)
                    last = mm(ps[:, bank, SEQ:ZW], kT[:, h, P:SEQ], qT[:, h, P:SEQ], start=True, stop=True)
                last.then_inc(z_done, 1)

            z_part(0)
            for p in range(SB_H // 2):
                w1, w2 = wk[p % 2]
                if p + 1 < SB_H // 2:
                    z_part(p + 1)
                pe.wait_ge(sp_ready, p + 1)
                if p:
                    pe.wait_ge(logit_ready, p)
                for i in range(2):
                    o = ps[:, 4 + i, :]
                    mm(o[:, 0:SEQ], neg_later[:], w2[:, i, 0:SEQ], start=True, stop=False)
                    mm(o[:, P:SEQ], neg_ones[:], w2[:, i, SEQ:ZW], start=False, stop=True)
                    last = mm(o[:, SEQ:ZW], neg_later[:], w2[:, i, SEQ:ZW], start=True, stop=True)
                last.then_inc(later_done, 1)
                pe.wait_ge(a_ready, p + 1)
                if p >= 2:
                    pe.wait_ge(head_lo, p - 1)
                for i in range(2):
                    h = 2 * p + i
                    c = slice(h * DH, (h + 1) * DH)
                    mm(ps[:, 6 + p % 2, i * SEQ:(i + 1) * SEQ], aV[:, 0, c], w1[:, i, 0:SEQ], start=True, stop=False)
                    last = mm(ps[:, 6 + p % 2, i * SEQ + P:(i + 1) * SEQ], aV[:, 1, c], w1[:, i, SEQ:ZW], start=False, stop=True)
                last.then_inc(head_done, 1)
            pe.wait_ge(head_lo, SB_H // 2)
            for half in range(2):
                wide(T0["ao"] + 16 * half, half, True, lambda j: None)
            mlp(1)


def _stripes(w):
    n = w.shape[1] // SW
    return w.reshape(ST, 2, P, n, SW).transpose(3, 0, 2, 1, 4).reshape(n * ST, P, TW)


def _halves(w):
    k = w.shape[0] // P
    return w.reshape(k, P, 2, TW).transpose(2, 0, 1, 3).reshape(2 * k, P, TW)


def _cols(v):
    return v.reshape(-1, P).T


def _rows(v):
    return np.broadcast_to(v[None, :], (P, v.shape[0]))


def _layout(x, c, ada_w, ada_b, ln_g, ln_b, gla_w_in, gla_w_gate_up, gla_b_gate, gla_norm_g, gla_w_out, kv_ada_w,
            kv_ada_b, w_kv, sb_w_q, sb_w_out, mlp_w1, mlp_b1, mlp_w2, mlp_b2):
    qk = D // 2
    w_in = gla_w_in[0]
    gl = np.zeros((4, P, 4, SEQ), np.float32)
    gl[:, :, :, :RANK] = w_in[:, 2 * qk + 2 * D:].reshape(4, 4, P, RANK).transpose(0, 2, 1, 3)
    tiles = [gl.reshape(4, P, TW), _stripes(w_in[:, qk:2 * qk]), _stripes(w_in[:, :qk]),
             _stripes(w_in[:, 2 * qk:2 * qk + D]), _stripes(w_in[:, 2 * qk + D:2 * qk + 2 * D]), _halves(gla_w_out[0]),
             _stripes(mlp_w1[0]), _halves(mlp_w2[0]), _stripes(w_kv[:, :D]), _stripes(w_kv[:, D:]),
             _stripes(sb_w_q[0]), _halves(sb_w_out[0]), _stripes(mlp_w1[1]), _halves(mlp_w2[1])]
    at = {"sh_a": 0, "sc_a": 1, "g_a": 2, "sh_m": 3, "sc_m": 4, "g_m": 5}
    mods, mod_b = [], []
    for name in MODS:
        if name in ("sh_k", "sc_k"):
            w, b, i = kv_ada_w, kv_ada_b, int(name == "sc_k")
        else:
            w, b, i = ada_w[int(name[-1])], ada_b[int(name[-1])], at[name[:-1]]
        mods.append(w[:, i * D:(i + 1) * D].T.reshape(KT, P, D))
        mod_b.append(_cols(b[i * D:(i + 1) * D]))
    wgu = np.zeros((P, qk), np.float32)
    wgu[:RANK] = gla_w_gate_up[0]
    lns = [(l, i) for l in range(2) for i in range(2)]
    return {
        "tiles": np.concatenate(tiles), "mods": np.concatenate(mods), "c_rows": _rows(c[0]),
        "x_rows": x[0].reshape(TOK, P, D).transpose(1, 0, 2), "mod_b": np.concatenate(mod_b, axis=1),
        "ln_t": np.concatenate([_cols(v[l, i]) for l, i in lns for v in (ln_g, ln_b)], axis=1),
        "b1_t": np.concatenate([_cols(mlp_b1[l]) for l in range(2)], axis=1), "bg_t": _cols(gla_b_gate[0]),
        "wgu": wgu, "normg": _rows(gla_norm_g[0]),
        "ln_rows": np.stack([np.stack([_rows(v[l, i]) for v in (ln_g, ln_b)]) for l, i in lns]),
        "b2_rows": np.stack([_rows(mlp_b2[l]) for l in range(2)]),
    }


def kernel(**inputs):
    import concourse.bacc as _bacc
    from concourse.bass_utils import run_bass_kernel_spmd as _run

    nc = _bacc.Bacc("TRN2", target_bir_lowering=False, num_devices=1)
    arrays, args = {}, []
    for name, a in _layout(**{k: np.asarray(v) for k, v in inputs.items()}).items():
        a = np.ascontiguousarray(a)
        arrays[f"in_{name}"] = a
        args.append(nc.dram_tensor(f"in_{name}", a.shape, mybir.dt.from_np(a.dtype), kind="ExternalInput").ap())
    args.append(nc.dram_tensor("out", (SEQ, D), mybir.dt.float32, kind="ExternalOutput").ap())
    build_kernel(nc, *args)
    r = _run(nc, [arrays], core_ids=[0])
    return r.results[0]["out"].reshape(1, SEQ, D)
```

```python
import concourse.bass as bass
import numpy as np
from concourse import mybir
from collections import defaultdict
from contextlib import ExitStack

P = 128
D = 2048
SEQ = 256
TOK = SEQ // P
KT = D // P
FF = 4 * D
RANK = 16
TAU = 16.0
CHUNK = 64
NCH = SEQ // CHUNK
GLA_H = 4
GLA_DK = D // 2 // GLA_H
GLA_DV = D // GLA_H
GJ = D // 2 // P
SB_H = 16
DH = D // SB_H
ALPHA = 4.0 ** 0.25
EPS = 1e-5

TW = 1024
SW = 512
ST = 8
BODY = 16
RING = 4
_sizes = [("gl", 4), ("gk", 16), ("gq", 16), ("gv", 32), ("gr", 32), ("go", 32),
          ("u0", 128), ("d0", 128), ("aq", 32), ("ak", 32), ("av", 32), ("ao", 32),
          ("u1", 128), ("d1", 128)]
T0 = {}
_at = 0
for _n, _s in _sizes:
    T0[_n] = _at
    _at += _s
N_TILES = _at

MODS = ["sc_a0", "sh_a0", "g_a0", "sh_m0", "sc_m0", "g_m0", "sh_k", "sc_k", "sh_a1", "sc_a1",
        "g_a1", "sh_m1", "sc_m1", "g_m1"]
MOD = {n: KT * i for i, n in enumerate(MODS)}
N_MODT = KT * len(MODS)
LEAD, LEAD_BUFS = 32, 8
MOD_AT = {6: (1, 4, 6, 9, 12, 14), 4: (1, 5, 9, 13), 2: (6, 14), 0: ()}
SCHEDULE = [("gk", 0, 8, 6), ("u0", 0, 8, 6), ("d0", 0, 4, 6), ("d0", 64, 1, 2), ("d0", 80, 3, 6),
            ("aq", 0, 4, 6), ("av", 0, 2, 2), ("ao", 0, 2, 4), ("u1", 0, 4, 4), ("u1", 64, 12, 0)]
PLAN = {}
_a = LEAD
for _n, _off, _bodies, _per in SCHEDULE:
    for _b in range(_bodies):
        PLAN[T0[_n] + _off + BODY * _b] = (_a, _per)
        _a += _per
assert _a == N_MODT

U0 = {"gk": 0, "gq": 2, "gv": 4, "gr": 8, "u0": 12, "aq": 28, "ak": 32, "av": 36, "u1": 40}
S0 = {"gk": 0, "gq": 2, "u0": 4, "aq": 20, "ak": 24, "u1": 28}
N_GLA_TURNED = 4
H_GLA, H_GLAO, H_M0, H_Q, H_KV, H_M1 = range(6)
PAIRS = KT // 2
Z_AT = [T0["ak"] + 15 + 6 * p for p in range(SB_H // 2)]
HEAD_AT = [T0["av"] + 8 * (p // 2) + 12 + p % 2 for p in range(SB_H // 2)]
HEAD_SPLIT_AT = [T0["av"] + 28 + p for p in range(4)] + [T0["ao"] + i for i in (1, 2, 9, 10)]
GLAO_AT = [T0["gr"] + i for i in (24, 25, 26, 27, 31)] + [T0["go"] + i for i in (0, 7, 8)]
PRE = 2


def build_kernel(nc, tiles, mods, c_rows, x_rows, mod_b, ln_t, b1_t, bg_t, wgu, normg, ln_rows, b2_rows, out):
    F32, F32R, BF16 = mybir.dt.float32, mybir.dt.float32r, mybir.dt.bfloat16
    ACT, ALU = mybir.ActivationFunctionType, mybir.AluOpType
    ctx = ExitStack()
    with ctx:
        def sb(name, shape, dt=F32):
            return ctx.enter_context(nc.sbuf_tensor(name, shape, dt))

        def sem(name):
            return ctx.enter_context(nc.semaphore(name))

        raw = sb("raw", [P, RING, TW])
        w_hi = sb("w_hi", [P, RING, TW], F32R)
        w_lo = sb("w_lo", [P, RING, TW], F32R)
        mod_w = sb("mod_w", [P, 2, D])
        cs = sb("cs", [P, D])
        X = sb("X", [P, TOK, D])
        h_hi = sb("h_hi", [P, KT, SEQ], F32R)
        h_lo = sb("h_lo", [P, KT, SEQ], F32R)
        R = sb("R", [P, 8 * D])
        G = sb("G", [P, D])
        S = sb("S", [P, D])
        ident = sb("ident", [P, P])
        ones = sb("ones", [P, P])
        neg_ones = sb("neg_ones", [P, P])
        neg_later = sb("neg_later", [P, P])
        incl = sb("incl", [P, P])
        mask_bf = sb("mask_bf", [P, P], BF16)
        ident_bf = sb("ident_bf", [P, P], BF16)
        mod_t = sb("mod_t", [P, N_MODT])
        mod_bt = sb("mod_bt", [P, N_MODT])
        lnt = sb("lnt", [P, 4 * 2 * KT])
        b1t = sb("b1t", [P, 2 * FF // P])
        bgt = sb("bgt", [P, GJ])
        coef = sb("coef", [P, 4, KT])
        coef2 = sb("coef2", [P, 4, KT])
        stats = sb("stats", [P, TOK, 4, 6])
        mv = sb("mv", [P, TOK, 2])
        rstd = sb("rstd", [P, 8])
        ssq = sb("ssq", [P, 8])
        eps = sb("eps", [P, 1])
        ps = ctx.enter_context(nc.psum_tensor("ps", [P, 8, 512], F32))
        rows_buf, turned_buf = S[:, 0:TW], S[:, TW:2 * TW]

        gEq, gEki, gEks, gqd = (R[:, i * D:(i + 1) * D].rearrange("p (j t) -> p j t", j=GJ) for i in range(4))
        kk_at = [4 * D + GJ * CHUNK * (n * (n + 1) // 2) for n in range(NCH + 1)]
        KK = [R[:, kk_at[n]:kk_at[n + 1]].rearrange("p (j t) -> p j t", j=GJ) for n in range(NCH)]
        bc_f, tmp_f = R[:, 4 * D:5 * D], R[:, 5 * D:6 * D]
        reset_f, wgu_f = R[:, 3 * D:4 * D], R[:, 2 * D:2 * D + D // 2]
        SC = R[:, kk_at[NCH]:kk_at[NCH] + D].rearrange("p (h s t) -> p h s t", h=GLA_H, s=TOK)
        o_junk = R[:, 8 * D - GLA_DV:8 * D]
        normg_sb = R[:, kk_at[NCH] + D:kk_at[NCH] + D + GLA_DV]
        gV = R[:, 0:2 * D].rearrange("p (a d) -> p a d", a=TOK)
        gR = R[:, 2 * D:4 * D].rearrange("p (a d) -> p a d", a=TOK)
        gO = R[:, 4 * D:6 * D].rearrange("p (a d) -> p a d", a=TOK)
        glT = S[:, 0:SEQ]
        decay = sb("decay", [P, GJ, NCH])
        kT = R[:, 0:2 * D].rearrange("p (h t) -> p h t", h=SB_H)
        aV = R[:, 2 * D:4 * D].rearrange("p (a d) -> p a d", a=TOK)
        qT = R[:, 4 * D:6 * D].rearrange("p (h t) -> p h t", h=SB_H)
        ZW = SEQ + P
        wk = [[R[:, 6 * D + (2 * a + b) * 2 * ZW:6 * D + (2 * a + b + 1) * 2 * ZW].rearrange("p (h c) -> p h c", h=2)
               for b in range(2)] for a in range(2)]
        ln_at = [6 * D, 6 * D, 6 * D, 0]
        Bg = [R[:, a:a + D] for a in ln_at]
        Bb = [R[:, a + D:a + 2 * D] for a in ln_at]
        lead_bufs = [mod_w[:, 0, :], mod_w[:, 1, :], R[:, 0:D], R[:, D:2 * D], R[:, 4 * D:5 * D], R[:, 5 * D:6 * D], G[:], S[:]]

        raw_loaded = [sem(f"raw_loaded{i}") for i in range(RING)]
        mod_loaded = [sem(f"mod_loaded{i}") for i in range(2)]
        c_loaded, x_loaded, setup_loaded = sem("c_loaded"), sem("x_loaded"), sem("setup_loaded")
        ln_loaded, b2_loaded, out_stored = sem("ln_loaded"), sem("b2_loaded"), sem("out_stored")
        lead_loaded = [sem(f"lead_loaded{i}") for i in range(LEAD_BUFS)]
        consts_made = sem("consts_made")
        hi_ready, lo_ready, tile_used, mod_done = sem("hi_ready"), sem("lo_ready"), sem("tile_used"), sem("mod_done")
        c_ln, c_log, c_sig, cs_ready = sem("c_ln"), sem("c_log"), sem("c_sig"), sem("cs_ready")
        coef_ready, xn_ready, x_updated = sem("coef_ready"), sem("xn_ready"), sem("x_updated")
        h_turned, h_full, h_hi_ready, h_lo_ready = (sem(n) for n in ("h_turned", "h_full", "h_hi_ready", "h_lo_ready"))
        rows_copied, blocks_turned = sem("rows_copied"), sem("blocks_turned")
        turned_act, turned_dve, squared = sem("turned_act"), sem("turned_dve"), sem("squared")
        src_hi, src_lo = sem("src_hi"), sem("src_lo")
        g_diag, g_summed, g_copied = sem("g_diag"), sem("g_summed"), sem("g_copied")
        var_ready, rstd_ready = sem("var_ready"), sem("rstd_ready")
        act_step, dve_step = sem("act_step"), sem("dve_step")
        gl_copied, gate_done, gate_sum = sem("gl_copied"), sem("gate_done"), sem("gate_sum")
        gate_ln, bc_ready, decay_ready = sem("gate_ln"), sem("bc_ready"), sem("decay_ready")
        qk_ready, scores_done, scores_copied, scores_masked = (
            sem("qk_ready"), sem("scores_done"), sem("scores_copied"), sem("scores_masked"))
        r_ln, r_log, r_sig, tok0_done = sem("r_ln"), sem("r_log"), sem("r_sig"), sem("tok0_done")
        o_done, o_copied, o_squares, o_rstd, o_ready = (
            sem("o_done"), sem("o_copied"), sem("o_squares"), sem("o_rstd"), sem("o_ready"))
        z_done, z_ln, sp_ready, later_done, logit_ready, a_exp, head_done, head_kept, head_hi, head_lo = (
            sem(n) for n in ("z_done", "z_ln", "sp_ready", "later_done", "logit_ready", "a_exp",
                             "head_done", "head_kept", "head_hi", "head_lo"))

        block = ctx.enter_context(nc.Block())

        def h_bank(occ, pr):
            return {H_GLAO: 6 + pr % 2, H_KV: 4 + pr % 2}.get(occ, 4 + pr % 4)

        def mod_positions(per_body):
            return {j: i for i, j in enumerate(MOD_AT[per_body])}

        @block.sync
        def _(sp):
            sp.dma_start(cs[:], c_rows).then_inc(c_loaded, 16)

            def load_tile(t, slot, first=False):
                if not first:
                    sp.wait_ge(lo_ready, t - RING + 1)
                sp.dma_start(raw[:, slot, :], tiles[bass.ds(t, 1), :, :].rearrange("a p n -> p (a n)"))\
                  .then_inc(raw_loaded[slot], 16)

            def load_mod(a, slot, first=False):
                if not first:
                    sp.wait_ge(mod_done, a - 1)
                sp.dma_start(mod_w[:, slot, :], mods[bass.ds(a, 1), :, :].rearrange("a p n -> p (a n)"))\
                  .then_inc(mod_loaded[slot], 16)

            def body(t, a, per_body):
                at = mod_positions(per_body)
                for j in range(BODY):
                    load_tile(t + j, j % RING)
                    if j in at:
                        load_mod(a + at[j], at[j] % 2)

            def load_lead(a, i, first=False):
                if not first:
                    sp.wait_ge(mod_done, a - LEAD_BUFS + 1)
                sp.dma_start(lead_bufs[i], mods[bass.ds(a, 1), :, :].rearrange("a p n -> p (a n)")).then_inc(lead_loaded[i], 16)

            for i in range(LEAD_BUFS):
                if i == LEAD_BUFS - 1:
                    sp.wait_ge(cs_ready, 1)
                load_lead(i, i, first=True)
                if i == 0:
                    sp.dma_start(X[:], x_rows).then_inc(x_loaded, 16)
            with sp.Fori(1, LEAD // LEAD_BUFS) as lap:
                for i in range(LEAD_BUFS):
                    load_lead(LEAD_BUFS * lap + i, i)
            for j in range(4):
                load_tile(j, j, first=True)
            for name, off, bodies, per in SCHEDULE:
                t = T0[name] + off
                with sp.Fori(0, bodies) as b:
                    body(t + BODY * b, PLAN[t][0] + per * b, per)
            for tok in range(TOK):
                sp.wait_ge(x_updated, 3 + tok + 1)
                sp.dma_start(out[tok * P:(tok + 1) * P, :], X[:, tok, :]).then_inc(out_stored, 16)
            sp.wait_ge(out_stored, 16 * TOK)

        @block.gpsimd
        def _(pool):
            for i, (dst, src) in enumerate(((mod_bt, mod_b), (lnt, ln_t), (b1t, b1_t), (bgt, bg_t))):
                pool.dma_start(dst[:], src).then_inc(setup_loaded, 16)
            pool.dma_start(wgu_f, wgu).then_inc(setup_loaded, 16)
            pool.dma_start(normg_sb, normg).then_inc(setup_loaded, 16)
            nc.gpsimd.memset(ident[:], 0.0).then_inc(consts_made, 1)
            nc.gpsimd.memset(ones[:], 1.0).then_inc(consts_made, 1)
            nc.gpsimd.memset(neg_ones[:], -1.0).then_inc(consts_made, 1)
            nc.gpsimd.memset(neg_later[:], -1.0).then_inc(consts_made, 1)
            nc.gpsimd.memset(incl[:], 1.0).then_inc(consts_made, 1)
            nc.gpsimd.memset(mask_bf[:], -1e30).then_inc(consts_made, 1)
            nc.gpsimd.memset(eps[:], EPS).then_inc(consts_made, 1)
            nc.gpsimd.memset(SC, 0.0).then_inc(consts_made, 1)
            nc.gpsimd.memset(reset_f, 1.0).then_inc(consts_made, 1)
            pool.wait_ge(consts_made, 9)
            nc.gpsimd.memset(reset_f.rearrange("p (c t) -> p c t", t=CHUNK)[:, :, 0:1], 0.0).then_inc(consts_made, 1)
            nc.gpsimd.affine_select(out=ident[:], in_=ident[:], compare_op=ALU.not_equal, fill=1.0, base=0,
                                    pattern=[[-1, P]], channel_multiplier=1).then_inc(consts_made, 1)
            nc.gpsimd.affine_select(out=neg_later[:], in_=neg_later[:], compare_op=ALU.is_ge, fill=0.0, base=-1,
                                    pattern=[[-1, P]], channel_multiplier=1).then_inc(consts_made, 1)
            nc.gpsimd.affine_select(out=incl[:], in_=incl[:], compare_op=ALU.is_ge, fill=0.0, base=0,
                                    pattern=[[1, P]], channel_multiplier=-1).then_inc(consts_made, 1)
            nc.gpsimd.affine_select(out=mask_bf[:], in_=mask_bf[:], compare_op=ALU.is_ge, fill=0.0, base=0,
                                    pattern=[[-1, P]], channel_multiplier=1).then_inc(consts_made, 1)
            pool.wait_ge(consts_made, 14)
            nc.gpsimd.tensor_copy(ident_bf[:], ident[:]).then_inc(consts_made, 1)

            def load_rows(l):
                pool.dma_start(Bg[l], ln_rows[l, 0, :, :]).then_inc(ln_loaded, 16)
                pool.dma_start(Bb[l], ln_rows[l, 1, :, :]).then_inc(ln_loaded, 16)

            def load_b2(layer):
                pool.wait_ge(squared, 16 * (layer + 1))
                pool.dma_start(S[:], b2_rows[layer, :, :]).then_inc(b2_loaded, 16)

            pool.wait_ge(h_lo_ready, PAIRS * (H_GLAO + 1))
            load_rows(0)
            load_b2(0)
            pool.wait_ge(tile_used, T0["d0"] + 128)
            load_rows(1)
            pool.wait_ge(a_exp, SB_H // 2)
            load_rows(2)
            load_b2(1)
            pool.wait_ge(tile_used, T0["d1"] + 64 + 32)
            load_rows(3)

        CONSTS = 15
        GATE_BANK = [4, 2, 4, 2]
        HALF_END = [[T0[n] + k * (h + 1) for h in range(2)] for n, k in (("go", 16), ("d0", 64), ("ao", 16), ("d1", 64))]
        LN_LOADS = [32, 64, 96, 128]

        @block.scalar
        def _(act):
            steps = [0]

            def link(ins):
                steps[0] += 1
                ins.then_inc(act_step, 1)
                act.wait_ge(act_step, steps[0])

            def split_tile(t, slot, lap, first=False):
                act.wait_ge(raw_loaded[slot], 16 * lap)
                if not first:
                    act.wait_ge(tile_used, t - RING + 1)
                nc.scalar.activation(w_hi[:, slot, :], raw[:, slot, :], ACT.Copy).then_inc(hi_ready, 1)

            H = defaultdict(list)

            def body(t, hooks=None, lap0=None, skip=0):
                for j in range(skip, BODY):
                    split_tile(t + j, j % RING, (t // RING if lap0 is None else lap0) + j // RING + 1)
                    for f in (H.get(t + j, ()) if hooks is None else hooks.get(j, ())):
                        f()

            def pre_split(t):
                for j in range(PRE):
                    split_tile(t + j, j % RING, t // RING + 1)

            def loop(t_first, n, make_hooks):
                with act.Fori(0, n) as b:
                    body(t_first + BODY * b, make_hooks(b), t_first // RING + (BODY // RING) * b)

            def rows_out(done, par, dst, s=None):
                def f():
                    act.wait_ge(tile_used, done)
                    if s is not None and not (isinstance(s, int) and s == 0):
                        act.wait_ge(blocks_turned, s)
                    nc.scalar.activation(dst, ps[:, 2 * par:2 * par + 2, :], ACT.Copy).then_inc(rows_copied, 1)
                return f

            def staged():
                return rows_buf.rearrange("p (a n) -> p a n", a=TOK)

            def relu(s, i, layer):
                def f():
                    act.wait_ge(blocks_turned, s + 1)
                    if isinstance(i, int) and i == 0 and layer == 0:
                        pass
                    else:
                        act.wait_ge(squared, 16 * layer + i)
                    for blk in range(4):
                        col = 64 * layer + 4 * i + blk
                        ins = nc.scalar.activation(turned_buf[:, blk * SEQ:(blk + 1) * SEQ], ps[:, 6 + blk // 2, (blk % 2) * SEQ:(blk % 2 + 1) * SEQ],
                                                   ACT.Relu, bias=b1t[:, bass.ds(col, 1)])
                    ins.then_inc(turned_act, 1)
                return f

            def keep_turned(s, dst, scale=1.0):
                def f():
                    act.wait_ge(blocks_turned, s + 1)
                    nc.scalar.activation(dst, ps[:, 6:8, :].rearrange("p a n -> p (a n)"), ACT.Copy, scale=scale)\
                      .then_inc(turned_act, 1)
                return f

            def h_full_pair(occ, pr, plain=False, co=None):
                act.wait_ge(h_turned, PAIRS * occ + pr + 1)
                if pr >= 2:
                    act.wait_ge(h_lo_ready, PAIRS * occ + pr - 1)
                full = turned_buf[:, (pr % 2) * 512:(pr % 2 + 1) * 512]
                if plain:
                    ins = nc.scalar.activation(full, ps[:, h_bank(occ, pr), :], ACT.Copy)
                else:
                    for i in range(2):
                        kt = 2 * pr + i
                        ins = nc.scalar.activation(full[:, i * SEQ:(i + 1) * SEQ], ps[:, h_bank(occ, pr), i * SEQ:(i + 1) * SEQ],
                                                   ACT.Identity, scale=co[:, 0, kt:kt + 1], bias=co[:, 1, kt:kt + 1])
                ins.then_inc(h_full, 1)

            def h_split_pair(occ, pr, used=None):
                act.wait_ge(h_full, PAIRS * occ + pr + 1)
                if used is not None:
                    act.wait_ge(tile_used, used)
                full = turned_buf[:, (pr % 2) * 512:(pr % 2 + 1) * 512]
                nc.scalar.activation(h_hi[:, 2 * pr:2 * pr + 2, :], full.rearrange("p (a t) -> p a t", a=2), ACT.Copy)\
                  .then_inc(h_hi_ready, 1)

            def h_pair(occ, pr, plain=False, co=None, used=None):
                def f():
                    h_full_pair(occ, pr, plain, co)
                    h_split_pair(occ, pr, used)
                return f

            def h_start(occ, n_coef, t, co):
                act.wait_ge(coef_ready, n_coef)
                h_full_pair(occ, 0, co=co)
                h_full_pair(occ, 1, co=co)
                h_split_pair(occ, 0)
                h_split_pair(occ, 1)
                for pr in range(2, PAIRS):
                    H[t + pr].append(h_pair(occ, pr, co=co))

            def gate_rows(occ, r):
                def f():
                    bank = GATE_BANK[occ]
                    act.wait_ge(g_summed, 2 * occ + r + 1)
                    nc.scalar.activation(G[:, r * TW:(r + 1) * TW], ps[:, bank:bank + 2, :].rearrange("p a n -> p (a n)"), ACT.Copy)\
                      .then_inc(g_copied, 1)
                return f

            def norm_scale(occ):
                for tok in range(TOK):
                    act.wait_ge(var_ready, 2 * occ + tok + 1)
                    link(nc.scalar.activation(rstd[:, tok:tok + 1], mv[:, tok, 1:2], ACT.Ln, bias=eps[:]))
                    nc.scalar.activation(rstd[:, tok:tok + 1], rstd[:, tok:tok + 1], ACT.Exp, scale=-0.5).then_inc(rstd_ready, 1)

            def ln_of_exp(dst, src, done):
                link(nc.scalar.activation(dst, src, ACT.Abs))
                link(nc.scalar.activation(dst, dst, ACT.Exp, scale=-1.0))
                nc.scalar.activation(dst, dst, ACT.Ln, bias=1.0).then_inc(done, 1)

            act.wait_ge(c_loaded, 16)
            ln_of_exp(S[:], cs[:], c_ln)
            act.wait_ge(c_log, 1)
            nc.scalar.activation(S[:], S[:], ACT.Exp).then_inc(c_sig, 1)
            act.wait_ge(consts_made, CONSTS)
            act.wait_ge(setup_loaded, 96)
            for j in range(4):
                split_tile(j, j, 1, first=True)
            act.wait_ge(coef_ready, 1)
            for pr in range(PAIRS):
                h_full_pair(H_GLA, pr, co=coef)
                h_split_pair(H_GLA, pr)

            def gl_out():
                act.wait_ge(tile_used, 4)
                act.wait_ge(h_lo_ready, PAIRS)
                nc.scalar.activation(glT, ps[:, 2, 0:SEQ], ACT.Copy).then_inc(gl_copied, 1)

            flat = lambda v: v.rearrange("p j t -> p (j t)")

            def gate_log():
                act.wait_ge(gate_sum, 1)
                link(nc.scalar.activation(tmp_f, bc_f, ACT.Abs))

            def gate_log2():
                link(nc.scalar.activation(tmp_f, tmp_f, ACT.Exp, scale=-1.0))

            def gate_log3():
                nc.scalar.activation(tmp_f, tmp_f, ACT.Ln, bias=1.0).then_inc(gate_ln, 1)

            def decays1():
                act.wait_ge(bc_ready, 1)
                nc.scalar.activation(flat(gEq), bc_f, ACT.Exp, scale=1.0 / TAU).then_inc(decay_ready, 1)
                nc.scalar.activation(decay[:], bc_f.rearrange("p (j n t) -> p j n t", j=GJ, t=CHUNK)[:, :, :, CHUNK - 1],
                                     ACT.Exp, scale=1.0 / TAU).then_inc(decay_ready, 1)

            def decays2():
                nc.scalar.activation(flat(gEki), bc_f, ACT.Exp, scale=-1.0 / TAU).then_inc(decay_ready, 1)

            def decays3():
                act.wait_ge(bc_ready, 2)
                nc.scalar.activation(flat(gEks), tmp_f, ACT.Exp, scale=1.0 / TAU).then_inc(decay_ready, 1)

            def v_out(i, dst, t):
                return rows_out(t + ST * (i + 1), i % 2, dst[:, :, i * SW:(i + 1) * SW])

            def scores_out():
                act.wait_ge(scores_done, 1)
                nc.scalar.activation(SC[:, :, 0, P:SEQ], ps[:, 4:8, P:SEQ], ACT.Copy).then_inc(scores_copied, 1)

            K, V, RR, O = T0["gk"], T0["gv"], T0["gr"], T0["go"]
            for at, f in ((0, gl_out), (4, gate_log), (5, gate_log2), (6, gate_log3), (9, decays1), (10, decays2), (12, decays3)):
                H[K + at].append(f)
            for i in range(4):
                H[K + 8 * i + 10].append(rows_out(K + 8 * i + 8, i % 2, staged(), i))
            H[V + 14].append(scores_out)
            for i in range(4):
                H[V + 8 * i + (15 if i == 0 else 10)].append(v_out(i, gV, V))

            def o_out(h):
                def f():
                    act.wait_ge(o_done, h + 1)
                    nc.scalar.activation(gO[:, :, h * GLA_DV:(h + 1) * GLA_DV], ps[:, 4:6, :], ACT.Copy).then_inc(o_copied, 1)
                return f

            def o_scale(h):
                def f():
                    act.wait_ge(o_squares, h + 1)
                    two = slice(2 * h, 2 * h + 2)
                    link(nc.scalar.activation(rstd[:, two], ssq[:, two], ACT.Ln, scale=1.0 / GLA_DV, bias=eps[:]))
                    nc.scalar.activation(rstd[:, two], rstd[:, two], ACT.Exp, scale=-0.5).then_inc(o_rstd, 1)
                return f

            def r_out(i):
                def f():
                    v_out(i, gR, RR)()
                    if i:
                        act.wait_ge(r_sig, i)
                        act.wait_ge(o_ready, i)
                    else:
                        act.wait_ge(blocks_turned, N_GLA_TURNED)
                    act.wait_ge(rows_copied, U0["gr"] + i + 1)
                    ln_of_exp(staged(), gR[:, :, i * SW:(i + 1) * SW], r_ln)
                return f

            def r_gate(i):
                def f():
                    act.wait_ge(r_log, i + 1)
                    nc.scalar.activation(rows_buf, rows_buf, ACT.Exp).then_inc(r_sig, 1)
                return f

            for h in range(GLA_H):
                B = RR + 8 * h
                H[B + 6].append(o_out(h))
                H[B + 8].append(o_scale(h))
                H[B + 10].append(r_out(h))
                H[B + 12].append(r_gate(h))
            H[RR + 9].append(gate_rows(0, 0))
            H[RR + 17].append(gate_rows(0, 1))
            for pr in range(PAIRS):
                H[GLAO_AT[pr] + 3].append(h_pair(H_GLAO, pr, plain=True, used=RR + 24 + pr + 1))
            for i in range(8):
                body(K + BODY * i)
            pre_split(T0["u0"])
            norm_scale(0)

            def mlp(layer):
                up, down, s = T0[f"u{layer}"], T0[f"d{layer}"], S0[f"u{layer}"]

                def hooks(b, first=False):
                    i, t = 2 * b, up + BODY * b
                    late = {10: [rows_out(t + 8, 0, staged(), s + i)], 14: [relu(s + i, i, layer)]}
                    early = {2: [rows_out(t, 1, staged(), s + i - 1)], 6: [relu(s + i - 1, i - 1, layer)]}
                    return late if first else {**late, **early}

                h_start(H_M0 if layer == 0 else H_M1, 2 if layer == 0 else 5, up, coef)
                for j, f in hooks(0, first=True).items():
                    H[up + j] += f
                body(up, skip=PRE)
                loop(up + BODY, 7, lambda b: hooks(b + 1))

                def split_src(kt, slot, m):
                    def f():
                        act.wait_ge(tile_used, m)
                        act.wait_ge(squared, 16 * (layer + 1) if not isinstance(kt, int) else 16 * layer + 4)
                        nc.scalar.activation(h_hi[:, slot:slot + 2, :], R[:, bass.ds(kt * SEQ, 2 * SEQ)].rearrange("p (a t) -> p a t", a=2),
                                             ACT.Copy).then_inc(src_hi, 1)
                    return f

                def src_hooks(t, b, extra={}):
                    hooks = {j: [split_src(16 * b + j, j, t + j - 14)] for j in range(0, BODY, 2)}
                    for j, f in extra.items():
                        hooks[j] = f + hooks.get(j, [])
                    return hooks

                for half in range(2):
                    t = down + 64 * half
                    extra = {2: [rows_out(down, 1, staged(), s + 15)], 6: [relu(s + 15, 15, layer)],
                             12: [gate_rows(1 + 2 * layer, 0)], 15: [gate_rows(1 + 2 * layer, 1)]} if half == 0 else {}
                    body(t, src_hooks(t, 0, extra))
                    loop(t + BODY, 3, lambda b: src_hooks(t + BODY + BODY * b, b + 1))
                if layer == 0:
                    pre_split(T0["aq"])
                norm_scale(1 + 2 * layer)

            mlp(0)
            Q, K, V, O = T0["aq"], T0["ak"], T0["av"], T0["ao"]
            h_start(H_Q, 4, Q, coef2)
            for i in range(8):
                t = Q + 8 * i
                dst, scale = (qT, DH ** -0.5) if i < 4 else (kT, 1.0)
                H[t + 10].append(rows_out(t + 8, i % 2, staged(), S0["aq"] + i))
                H[t + 14].append(keep_turned(S0["aq"] + i, dst[:, 4 * (i % 4):4 * (i % 4) + 4, :].rearrange("p h t -> p (h t)"), scale))
            H[Q + 21].append(gate_rows(2, 0))
            H[Q + 26].append(gate_rows(2, 1))
            for pr in range(PAIRS):
                H[Q + 27 + pr].append(h_pair(H_KV, pr, co=coef, used=Q + 24 + pr + 1))
            for i in range(4):
                H[V + 8 * i + 10].append(v_out(i, aV, V))

            def z_part(p):
                def f():
                    if p < 2:
                        act.wait_ge(x_updated, 2)
                    act.wait_ge(z_done, p + 1)
                    if p >= 2:
                        act.wait_ge(a_exp, p - 1)
                    ln_of_exp(wk[p % 2][0], ps[:, 4:6, 0:ZW], z_ln)
                return f

            def a_part(p):
                def f():
                    act.wait_ge(logit_ready, p + 1)
                    w1 = wk[p % 2][0]
                    nc.scalar.activation(qT[:, 2 * p:2 * p + 2, :], w1[:, :, 0:SEQ], ACT.Exp)
                    nc.scalar.activation(kT[:, 2 * p:2 * p + 2, 0:P], w1[:, :, SEQ:ZW], ACT.Exp).then_inc(a_exp, 1)
                return f

            def o_part(p):
                def f():
                    act.wait_ge(head_done, p + 1)
                    nc.scalar.activation(qT[:, 2 * p:2 * p + 2, :], ps[:, 6 + p % 2, :].rearrange("p (a t) -> p a t", a=2), ACT.Copy)\
                      .then_inc(head_kept, 1)
                return f

            def o_split(p):
                def f():
                    act.wait_ge(head_kept, p + 1)
                    act.wait_ge(tile_used, V + 24 + p + 1)
                    nc.scalar.activation(h_hi[:, 2 * p:2 * p + 2, :], qT[:, 2 * p:2 * p + 2, :], ACT.Copy).then_inc(head_hi, 1)
                return f

            for p in range(SB_H // 2):
                H[Z_AT[p] + 3].append(z_part(p))
                H[Z_AT[p] + 7].append(a_part(p))
                H[HEAD_AT[p] + 3].append(o_part(p))
                H[HEAD_SPLIT_AT[p]].append(o_split(p))
            body(Q, skip=PRE)
            for i in range(1, 8):
                body(Q + BODY * i)
            pre_split(T0["u1"])
            norm_scale(2)
            mlp(1)

        @block.vector
        def _(dve):
            steps = [0]

            def link(ins):
                steps[0] += 1
                ins.then_inc(dve_step, 1)
                dve.wait_ge(dve_step, steps[0])

            def split_tile(t, slot, first=False):
                dve.wait_ge(hi_ready, t + 1)
                if not first:
                    dve.wait_ge(tile_used, t - RING + 1)
                nc.vector.tensor_tensor(w_lo[:, slot, :], raw[:, slot, :], w_hi[:, slot, :].bitcast(F32), ALU.subtract)\
                  .then_inc(lo_ready, 1)

            def mod_tile(a, buf, loaded, lap):
                dve.wait_ge(loaded, 16 * lap)
                nc.vector.scalar_tensor_tensor(buf, buf, 1.0, cs[:], ALU.mult, ALU.mult,
                                               accum_out=mod_t[:, bass.ds(a, 1)]).then_inc(mod_done, 1)

            H = defaultdict(list)

            def body(t, a, lap, per, hooks, skip=0):
                at = mod_positions(per)
                for j in range(BODY):
                    if j >= skip:
                        split_tile(t + j, j % RING)
                    if j in at:
                        mod_tile(a + at[j], mod_w[:, at[j] % 2, :], mod_loaded[at[j] % 2], lap + at[j] // 2 + 1)
                    for f in hooks.get(j, ()):
                        f()

            def run(t, hooks=None, skip=0):
                a, per = PLAN[t]
                body(t, a, (a - LEAD) // 2, per, {j: H.get(t + j, []) for j in range(BODY)} if hooks is None else hooks, skip)

            def loop(t_first, n, make_hooks):
                a, per = PLAN[t_first]
                with dve.Fori(0, n) as b:
                    body(t_first + BODY * b, a + per * b, (a - LEAD) // 2 + (per // 2) * b, per, make_hooks(b))

            def pre_split(t):
                for j in range(PRE):
                    split_tile(t + j, j % RING)

            def make_coef(co, scale, shift, ln=None):
                sc, sh = MOD[scale], MOD[shift]
                dve.wait_ge(mod_done, max(sc, sh) + KT)
                link(nc.vector.tensor_tensor(co[:, 2, :], mod_t[:, sc:sc + KT], mod_bt[:, sc:sc + KT], ALU.add))
                link(nc.vector.tensor_tensor(co[:, 1, :], mod_t[:, sh:sh + KT], mod_bt[:, sh:sh + KT], ALU.add))
                if ln is None:
                    nc.vector.tensor_scalar(co[:, 0, :], co[:, 2, :], 1.0, None, ALU.add).then_inc(coef_ready, 1)
                else:
                    g, b = lnt[:, 2 * ln * KT:(2 * ln + 1) * KT], lnt[:, (2 * ln + 1) * KT:(2 * ln + 2) * KT]
                    link(nc.vector.scalar_tensor_tensor(co[:, 3, :], co[:, 2, :], 1.0, b, ALU.add, ALU.mult))
                    link(nc.vector.tensor_tensor(co[:, 1, :], co[:, 1, :], co[:, 3, :], ALU.add))
                    nc.vector.scalar_tensor_tensor(co[:, 0, :], co[:, 2, :], 1.0, g, ALU.add, ALU.mult).then_inc(coef_ready, 1)

            def h_pair(occ, pr):
                dve.wait_ge(h_hi_ready, PAIRS * occ + pr + 1)
                full = turned_buf[:, (pr % 2) * 512:(pr % 2 + 1) * 512]
                nc.vector.tensor_tensor(h_lo[:, 2 * pr:2 * pr + 2, :], full.rearrange("p (a t) -> p a t", a=2),
                                        h_hi[:, 2 * pr:2 * pr + 2, :].bitcast(F32), ALU.subtract).then_inc(h_lo_ready, 1)

            def h_start(occ, t):
                h_pair(occ, 0)
                h_pair(occ, 1)
                for pr in range(2, PAIRS):
                    H[t + pr].append(lambda pr=pr: h_pair(occ, pr))

            def gate_diag(occ, name):
                g = MOD[name]
                dve.wait_ge(mod_done, g + KT)
                link(nc.vector.scalar_tensor_tensor(coef[:, 2, :], mod_t[:, g:g + KT], 1.0, mod_bt[:, g:g + KT], ALU.add, ALU.add))
                nc.vector.tensor_tensor(G[:].rearrange("p (j n) -> p j n", n=P), ident[:].unsqueeze(1).to_broadcast([P, KT, P]),
                                        coef[:, 2, :].unsqueeze(2).to_broadcast([P, KT, P]), ALU.mult).then_inc(g_diag, 1)

            def residual(occ, half, tok, alpha):
                bank = {(0, 0): 0, (0, 1): 4, (1, 0): 2, (1, 1): 6}[half, tok]
                cols = slice(half * TW, (half + 1) * TW)
                stage = S[:, tok * TW:(tok + 1) * TW]
                if (half, tok) == (1, 0):
                    dve.wait_ge(tok0_done, occ + 1)
                else:
                    dve.wait_ge(tile_used, HALF_END[occ][half])
                dve.wait_ge(g_copied, 2 * occ + 2)
                link(nc.vector.tensor_tensor(stage, ps[:, bank:bank + 2, :].rearrange("p a n -> p (a n)"), G[:, cols], ALU.mult))
                link(nc.vector.scalar_tensor_tensor(X[:, tok, cols], X[:, tok, cols], alpha, stage, ALU.mult, ALU.add))
                for i in range(2):
                    ins = nc.vector.bn_stats(stats[:, tok, 2 * half + i, :], X[:, tok, half * TW + i * 512:half * TW + (i + 1) * 512])
                return ins

            def normalise(occ, alpha):
                for tok in range(TOK):
                    link(residual(occ, 1, tok, alpha))
                    nc.vector.bn_aggr(mv[:, tok, :], stats[:, tok, :, :].rearrange("p a b -> p (a b)")).then_inc(var_ready, 1)
                for tok in range(TOK):
                    dve.wait_ge(var_ready, 2 * occ + tok + 1)
                    dve.wait_ge(rstd_ready, 2 * occ + tok + 1)
                    nc.vector.tensor_scalar(X[:, tok, :], X[:, tok, :], mv[:, tok, 0:1], rstd[:, tok:tok + 1],
                                            ALU.subtract, ALU.mult).then_inc(xn_ready, 1)

            def half0(occ, alpha):
                return {8: [lambda: link(residual(occ, 0, 0, alpha))], 12: [lambda: link(residual(occ, 0, 1, alpha))]}

            def update_piece(l, q, mult):
                tok, cols = q // 2, slice((q % 2) * TW, (q % 2 + 1) * TW)

                def f():
                    if q == 0 and mult:
                        dve.wait_ge(ln_loaded, LN_LOADS[l])
                        dve.wait_ge(h_turned, PAIRS * {0: H_M0, 1: H_KV, 2: H_M1}[l] + PAIRS)
                        dve.wait_ge(xn_ready, 2 * (l + 1))
                    row = (Bg if mult else Bb)[l][:, cols]
                    ins = nc.vector.tensor_tensor(X[:, tok, cols], X[:, tok, cols], row, ALU.mult if mult else ALU.add)
                    if q == 3 and not mult:
                        ins.then_inc(x_updated, 1)
                    else:
                        link(ins)
                return f

            def update_hooks(l, t):
                pieces = [update_piece(l, q, m) for q in range(4) for m in (True, False)]
                for j, f in enumerate(pieces):
                    H[t + j].append(f)

            def merge(a, b):
                return {j: a.get(j, []) + b.get(j, []) for j in {*a, *b}}

            dve.wait_ge(c_ln, 1)
            nc.vector.scalar_tensor_tensor(S[:], cs[:], 0.0, S[:], ALU.min, ALU.subtract).then_inc(c_log, 1)
            dve.wait_ge(c_sig, 1)
            nc.vector.tensor_tensor(cs[:], cs[:], S[:], ALU.mult).then_inc(cs_ready, 1)
            dve.wait_ge(cs_ready, 1)
            with dve.Fori(0, LEAD // LEAD_BUFS) as lap:
                for i in range(LEAD_BUFS):
                    mod_tile(LEAD_BUFS * lap + i, lead_bufs[i], lead_loaded[i], lap + 1)
            dve.wait_ge(setup_loaded, 96)
            dve.wait_ge(consts_made, CONSTS)
            make_coef(coef, "sc_a0", "sh_a0")
            for j in range(4):
                split_tile(j, j, first=True)
            for pr in range(PAIRS):
                h_pair(H_GLA, pr)
            g3 = lambda v: v.rearrange("p (j t) -> p j t", j=GJ)
            chunks = lambda v: v.rearrange("p (c t) -> p c t", t=CHUNK)

            def gate_logits():
                dve.wait_ge(gate_done, 1)
                nc.vector.tensor_tensor(g3(bc_f), ps[:, 4:8, :].rearrange("p a (b t) -> p (a b) t", b=2),
                                        bgt[:].unsqueeze(2).to_broadcast([P, GJ, SEQ]), ALU.add).then_inc(gate_sum, 1)

            def log_sigmoid():
                dve.wait_ge(gate_sum, 1)
                dve.wait_ge(gate_ln, 1)
                link(nc.vector.scalar_tensor_tensor(tmp_f, bc_f, 0.0, tmp_f, ALU.min, ALU.subtract))

            def running_sums():
                nc.vector.tensor_tensor_scan(bc_f, reset_f, tmp_f, 0.0, ALU.mult, ALU.add).then_inc(bc_ready, 1)

            def sums_to_end():
                dve.wait_ge(bc_ready, 1)
                nc.vector.tensor_tensor(chunks(tmp_f), chunks(bc_f)[:, :, CHUNK - 1:CHUNK].to_broadcast([P, GJ * NCH, CHUNK]),
                                        chunks(bc_f), ALU.subtract).then_inc(bc_ready, 1)

            def gla_keys(i):
                def f():
                    dve.wait_ge(blocks_turned, S0["gk"] + i + 1)
                    dve.wait_ge(decay_ready, 4)
                    turned = ps[:, 6:8, :].rearrange("p a (b t) -> p (a b) t", b=2)
                    js = slice(4 * i, 4 * i + 4)
                    for n in range(NCH):
                        c = slice(n * CHUNK, (n + 1) * CHUNK)
                        ins = nc.vector.tensor_tensor(KK[n][:, js, c], turned[:, :, c], gEki[:, js, c], ALU.mult)
                        if n + 1 < NCH:
                            ins = nc.vector.tensor_tensor(KK[n + 1][:, js, c], turned[:, :, c], gEks[:, js, c], ALU.mult)
                    ins.then_inc(turned_dve, 1)
                return f

            def gla_decayed():
                dve.wait_ge(turned_dve, 2)
                for n in (2, 3):
                    w = CHUNK * (n - 1)
                    link(nc.vector.tensor_tensor(KK[n][:, :, 0:w], KK[n - 1][:, :, 0:w],
                                                 decay[:, :, n - 1:n].to_broadcast([P, GJ, w]), ALU.mult))

            def gla_queries(i):
                def f():
                    dve.wait_ge(blocks_turned, S0["gq"] + i + 1)
                    turned = ps[:, 6:8, :].rearrange("p a n -> p (a n)")
                    js = slice(4 * i, 4 * i + 4)
                    nc.vector.scalar_tensor_tensor(gqd[:, js, :].rearrange("p j t -> p (j t)"), turned, GLA_DK ** -0.5,
                                                   gEq[:, js, :].rearrange("p j t -> p (j t)"), ALU.mult, ALU.mult)\
                      .then_inc(turned_dve, 1)
                return f

            def scores_masked_out():
                dve.wait_ge(scores_copied, 1)
                for st in range(TOK):
                    lo = slice(st * SEQ + st * P, st * SEQ + st * P + CHUNK)
                    hi = slice(st * SEQ + st * P + CHUNK, st * SEQ + (st + 1) * P)
                    nc.vector.tensor_tensor(SC[0:CHUNK, :, st, st * P:st * P + CHUNK], ps[0:CHUNK, 4:8, lo],
                                            incl[0:CHUNK, 0:CHUNK].unsqueeze(1).to_broadcast([CHUNK, GLA_H, CHUNK]), ALU.mult)
                    ins = nc.vector.tensor_tensor(SC[:, :, st, st * P + CHUNK:(st + 1) * P], ps[:, 4:8, hi],
                                                  incl[:, CHUNK:P].unsqueeze(1).to_broadcast([P, GLA_H, CHUNK]), ALU.mult)
                ins.then_inc(scores_masked, 1)

            K, V, RR, O = T0["gk"], T0["gv"], T0["gr"], T0["go"]
            for at, f in ((3, gate_logits), (7, log_sigmoid), (8, running_sums), (10, sums_to_end), (15, gla_keys(0)),
                          (23, gla_keys(1)), (24, gla_decayed), (31, gla_queries(0)), (39, gla_queries(1)),
                          (47, scores_masked_out)):
                H[K + at].append(f)

            def o_square(h):
                def f():
                    dve.wait_ge(o_copied, h + 1)
                    if h:
                        dve.wait_ge(o_squares, h)
                    for tok in range(TOK):
                        o = gO[:, tok, h * GLA_DV:(h + 1) * GLA_DV]
                        ins = nc.vector.scalar_tensor_tensor(o_junk, o, 1.0, o, ALU.mult, ALU.mult,
                                                             accum_out=ssq[:, 2 * h + tok:2 * h + tok + 1])
                        if tok == 0:
                            link(ins)
                    ins.then_inc(o_squares, 1)
                return f

            def o_norm(h):
                def f():
                    dve.wait_ge(o_rstd, h + 1)
                    for tok in range(TOK):
                        o = gO[:, tok, h * GLA_DV:(h + 1) * GLA_DV]
                        ins = nc.vector.scalar_tensor_tensor(o, o, rstd[:, 2 * h + tok:2 * h + tok + 1], normg_sb, ALU.mult, ALU.mult)
                    link(ins)
                return f

            def r_logit(i):
                def f():
                    dve.wait_ge(r_ln, i + 1)
                    nc.vector.scalar_tensor_tensor(rows_buf.rearrange("p (a n) -> p a n", a=TOK), gR[:, :, i * SW:(i + 1) * SW], 0.0,
                                                   rows_buf.rearrange("p (a n) -> p a n", a=TOK), ALU.min, ALU.subtract).then_inc(r_log, 1)
                return f

            def o_gate(i):
                def f():
                    dve.wait_ge(r_sig, i + 1)
                    part, o = gR[:, :, i * SW:(i + 1) * SW], gO[:, :, i * SW:(i + 1) * SW]
                    link(nc.vector.tensor_tensor(part, part, rows_buf.rearrange("p (a n) -> p a n", a=TOK), ALU.mult))
                    nc.vector.tensor_tensor(o, o, part, ALU.mult).then_inc(o_ready, 1)
                return f

            for h in range(GLA_H):
                B = RR + 8 * h
                for at, f in ((7, o_square(h)), (9, o_norm(h)), (11, r_logit(h)), (13, o_gate(h))):
                    H[B + at].append(f)
            H[RR + 5].append(lambda: gate_diag(0, "g_a0"))
            for pr in range(PAIRS):
                H[GLAO_AT[pr] + 4].append(lambda pr=pr: h_pair(H_GLAO, pr))
            for j, f in half0(0, ALPHA).items():
                H[O + 16 + j] += f
            for i in range(8):
                run(K + BODY * i)
            make_coef(coef, "sc_m0", "sh_m0", 0)
            pre_split(T0["u0"])
            normalise(0, ALPHA)

            def mlp(layer):
                up, down, s, l = T0[f"u{layer}"], T0[f"d{layer}"], S0[f"u{layer}"], 2 * layer

                def square(i):
                    def f():
                        dve.wait_ge(turned_act, s - N_GLA_TURNED + i + 1)
                        nc.vector.tensor_tensor(R[:, bass.ds(i * TW, TW)], turned_buf, turned_buf, ALU.mult).then_inc(squared, 1)
                    return f

                def hooks(b):
                    return {15: [square(2 * b)], 7: [square(2 * b - 1)]}

                h_start(H_M0 if layer == 0 else H_M1, up)
                update_hooks(l, up + 7)
                H[up + 15].append(square(0))
                run(up, skip=PRE)
                if layer == 0:
                    loop(up + BODY, 7, lambda b: hooks(b + 1))
                else:
                    loop(up + BODY, 3, lambda b: hooks(b + 1))
                    loop(up + 4 * BODY, 4, lambda b: hooks(b + 4))

                def split_src(kt, slot, m):
                    def f():
                        dve.wait_ge(src_hi, m)
                        dve.wait_ge(squared, 16 * (layer + 1) if not isinstance(kt, int) else 16 * layer + 4)
                        nc.vector.tensor_tensor(h_lo[:, slot:slot + 2, :], R[:, bass.ds(kt * SEQ, 2 * SEQ)].rearrange("p (a t) -> p a t", a=2),
                                                h_hi[:, slot:slot + 2, :].bitcast(F32), ALU.subtract).then_inc(src_lo, 1)
                    return f

                def bias_rows():
                    dve.wait_ge(g_copied, 4 + 4 * layer)
                    dve.wait_ge(b2_loaded, 16 * (layer + 1))
                    dve.wait_ge(x_updated, l + 1)
                    link(nc.vector.tensor_tensor(S[:], S[:], G[:], ALU.mult))

                def add_bias(tok):
                    return lambda: link(nc.vector.scalar_tensor_tensor(X[:, tok, :], X[:, tok, :], ALPHA, S[:], ALU.mult, ALU.add))

                for half in range(2):
                    t = down + 64 * half
                    m = 64 * layer + 32 * half

                    def src_hooks(b, m=m):
                        return {j: [split_src(16 * b + j, j, m + 8 * b + j // 2 + 1)] for j in range(0, BODY, 2)}

                    if half == 0:
                        extra = {7: [square(15)], 8: [lambda: gate_diag(1 + 2 * layer, f"g_m{layer}")]}
                    else:
                        extra = merge({1: [bias_rows], 3: [add_bias(0)], 5: [add_bias(1)]}, half0(1 + 2 * layer, 1.0))
                    run(t, merge(src_hooks(0), extra))
                    loop(t + BODY, 3, lambda b: src_hooks(b + 1))

            mlp(0)
            make_coef(coef, "sc_k", "sh_k", 1)
            make_coef(coef2, "sc_a1", "sh_a1", 1)
            pre_split(T0["aq"])
            normalise(1, 1.0)
            Q, K, V, O = T0["aq"], T0["ak"], T0["av"], T0["ao"]
            h_start(H_Q, Q)
            H[Q + 17].append(lambda: gate_diag(2, "g_a1"))
            for pr in range(PAIRS):
                H[Q + 28 + pr].append(lambda pr=pr: h_pair(H_KV, pr))
            update_hooks(1, K + 5)

            def z_part(p):
                def f():
                    z, w1, w2 = ps[:, 4:6, 0:ZW], wk[p % 2][0], wk[p % 2][1]
                    dve.wait_ge(z_ln, p + 1)
                    if p >= 2:
                        dve.wait_ge(sp_ready, p)
                    nc.vector.scalar_tensor_tensor(w2, z, 0.0, w1, ALU.max, ALU.add)
                    nc.vector.scalar_tensor_tensor(w1, z, 0.0, w1, ALU.min, ALU.subtract).then_inc(sp_ready, 1)
                return f

            def a_part(p):
                def f():
                    w1 = wk[p % 2][0]
                    dve.wait_ge(sp_ready, p + 1)
                    dve.wait_ge(later_done, p + 1)
                    nc.vector.tensor_tensor(w1, w1, ps[:, 4:6, 0:ZW], ALU.add).then_inc(logit_ready, 1)
                return f

            def o_split(p):
                def f():
                    dve.wait_ge(head_hi, p + 1)
                    nc.vector.tensor_tensor(h_lo[:, 2 * p:2 * p + 2, :], qT[:, 2 * p:2 * p + 2, :],
                                            h_hi[:, 2 * p:2 * p + 2, :].bitcast(F32), ALU.subtract).then_inc(head_lo, 1)
                return f

            for p in range(SB_H // 2):
                H[Z_AT[p] + 4].append(z_part(p))
                H[Z_AT[p] + 6].append(a_part(p))
                H[HEAD_SPLIT_AT[p] + 1].append(o_split(p))
            for j, f in half0(2, ALPHA).items():
                H[O + 16 + j] += f
            run(Q, skip=PRE)
            for i in range(1, 8):
                run(Q + BODY * i)
            make_coef(coef, "sc_m1", "sh_m1", 2)
            pre_split(T0["u1"])
            normalise(2, ALPHA)
            mlp(1)
            normalise(3, 1.0)
            dve.wait_ge(ln_loaded, LN_LOADS[3])
            dve.wait_ge(xn_ready, 8)
            for tok in range(TOK):
                link(nc.vector.tensor_tensor(X[:, tok, :], X[:, tok, :], Bg[3], ALU.mult))
                nc.vector.tensor_tensor(X[:, tok, :], X[:, tok, :], Bb[3], ALU.add).then_inc(x_updated, 1)

        @block.tensor
        def _(pe):
            mm = nc.tensor.matmul

            def product(dst, hs, ws, start, stop, more=False):
                hh, hl = hs
                wh, wl = ws
                mm(dst, hh, wh, start=start, stop=False, skip_group_check=more)
                mm(dst, hh, wl, start=False, stop=False, skip_group_check=more)
                return mm(dst, hl, wh, start=False, stop=stop, skip_group_check=more)

            def h_part(kt, tok):
                c = slice(tok * P, (tok + 1) * P)
                return h_hi[:, kt, c], h_lo[:, kt, c]

            def w_part(slot, c):
                return w_hi[:, slot, c], w_lo[:, slot, c]

            def stripe_tile(t, j, par, inputs=None):
                pe.wait_ge(lo_ready, t + 1)
                if inputs is not None:
                    pe.wait_ge(h_lo_ready, inputs)
                slot = j % RING
                for i in range(2):
                    kt = 2 * (j % ST) + i
                    for tok in range(TOK):
                        last = product(ps[:, 2 * par + tok, :], h_part(kt, tok), w_part(slot, slice(i * SW, (i + 1) * SW)),
                                       kt == 0, kt == KT - 1)
                last.then_inc(tile_used, 1)

            H = defaultdict(list)

            def stripes(t, u, occ=None, hooks=None):
                for j in range(BODY):
                    if j % ST == 0 and not (isinstance(u, int) and u + j // ST < 2):
                        pe.wait_ge(rows_copied, u + j // ST - 1)
                    if isinstance(u, int) and u + j // ST == 1 and j % ST == 0:
                        pe.wait_ge(gl_copied, 1)
                    stripe_tile(t + j, j, j // ST, None if occ is None or j >= ST else PAIRS * occ + j + 1)
                    for f in (H.get(t + j, ()) if hooks is None else hooks.get(j, ())):
                        f()

            def turn(u, s, freed):
                def f():
                    pe.wait_ge(rows_copied, u + 1)
                    for sm, v in freed:
                        pe.wait_ge(sm, v)
                    for blk in range(4):
                        for tok in range(TOK):
                            o = (blk % 2) * SEQ + tok * P
                            last = nc.tensor.transpose(ps[:, 6 + blk // 2, o:o + P],
                                                       rows_buf[:, tok * SW + blk * P:tok * SW + (blk + 1) * P], ident[:])
                    last.then_inc(blocks_turned, 1)
                return f

            def turn_pair(occ, pr, src, bufs=4):
                if pr >= bufs:
                    pe.wait_ge(h_full, PAIRS * occ + pr - bufs + 1)
                for i in range(2):
                    kt = 2 * pr + i
                    for tok in range(TOK):
                        last = nc.tensor.transpose(ps[:, h_bank(occ, pr), i * SEQ + tok * P:i * SEQ + (tok + 1) * P],
                                                   src[:, tok, kt * P:(kt + 1) * P], ident[:])
                last.then_inc(h_turned, 1)

            def turn_all(occ, src):
                for pr in range(PAIRS):
                    turn_pair(occ, pr, src)

            def gate_sums(occ, r):
                def f():
                    pe.wait_ge(g_diag, occ + 1)
                    if r:
                        pe.wait_ge(g_copied, 2 * occ + 1)
                    for n in range(2):
                        last = mm(ps[:, GATE_BANK[occ] + n, :], ones[:], G[:, r * TW + n * 512:r * TW + (n + 1) * 512], start=True, stop=True)
                    last.then_inc(g_summed, 1)
                return f

            HALF_BANKS = {0: (0, 4), 1: (2, 6)}

            def wide(t, half, first, src, hooks=None, last=False):
                def tile(j, toks):
                    for tok in toks:
                        for n in range(2):
                            ins = product(ps[:, HALF_BANKS[half][tok] + n, :], h_part(j, tok), w_part(j % RING, slice(n * SW, (n + 1) * SW)),
                                          first and j == 0, first and j == BODY - 1, more=not first)
                    return ins

                for j in range(BODY - 2 if last else BODY):
                    pe.wait_ge(lo_ready, t + j + 1)
                    if src(j) is not None:
                        pe.wait_ge(*src(j))
                    tile(j, range(TOK)).then_inc(tile_used, 1)
                    for f in (H.get(t + j, ()) if hooks is None else hooks.get(j, ())):
                        f()
                if last:
                    pe.wait_ge(lo_ready, t + BODY)
                    for j in (BODY - 2, BODY - 1):
                        if src(j) is not None:
                            pe.wait_ge(*src(j))
                        ins = tile(j, [0])
                    ins.then_inc(tok0_done, 1)
                    for j in (BODY - 2, BODY - 1):
                        tile(j, [1]).then_inc(tile_used, 1)

            pe.wait_ge(x_loaded, 16)
            pe.wait_ge(consts_made, CONSTS)
            turn_all(H_GLA, X)
            pe.wait_ge(h_lo_ready, PAIRS)
            for j in range(4):
                pe.wait_ge(lo_ready, j + 1)
                for i in range(4):
                    kt = 4 * j + i
                    c = slice(i * SEQ, i * SEQ + P)
                    last = product(ps[:, 2, 0:SEQ], (w_hi[:, j, c], w_lo[:, j, c]), (h_hi[:, kt, :], h_lo[:, kt, :]), kt == 0, kt == KT - 1)
                last.then_inc(tile_used, 1)

            def gates():
                pe.wait_ge(gl_copied, 1)
                pe.wait_ge(setup_loaded, 96)
                pe.wait_ge(h_full, PAIRS)
                for j in range(GJ):
                    last = mm(ps[:, 4 + j // 2, (j % 2) * SEQ:(j % 2 + 1) * SEQ], wgu_f[:, j * P:(j + 1) * P], glT, start=True, stop=True)
                last.then_inc(gate_done, 1)

            def scores():
                pe.wait_ge(turned_dve, 4)
                for h in range(GLA_H):
                    for n in range(NCH):
                        for st in range(n // 2 + 1):
                            m = min(P, CHUNK * (n + 1) - st * P)
                            for j in (2 * h, 2 * h + 1):
                                last = mm(ps[0:m, 4 + h, st * SEQ + n * CHUNK:st * SEQ + (n + 1) * CHUNK],
                                          KK[n][:, j, st * P:st * P + m], gqd[:, j, n * CHUNK:(n + 1) * CHUNK],
                                          start=j % 2 == 0, stop=j % 2 == 1)
                last.then_inc(scores_done, 1)

            def o_head(h):
                def f():
                    if h == 0:
                        pe.wait_ge(scores_copied, 1)
                        pe.wait_ge(scores_masked, 1)
                        pe.wait_ge(rows_copied, U0["gv"] + 4)
                    else:
                        pe.wait_ge(o_copied, h)
                        pe.wait_ge(g_copied, min(h, 2))
                    for tok in range(TOK):
                        for st in range(tok + 1):
                            last = mm(ps[:, 4 + tok, :], SC[:, h, st, tok * P:(tok + 1) * P],
                                      gV[:, st, h * GLA_DV:(h + 1) * GLA_DV], start=st == 0, stop=st == tok)
                    last.then_inc(o_done, 1)
                return f

            def gate_sums_after(occ, r, sm, v):
                def f():
                    pe.wait_ge(sm, v)
                    gate_sums(occ, r)()
                return f

            def turn_o(pr):
                def f():
                    pe.wait_ge(o_ready, pr // 2 + 1)
                    turn_pair(H_GLAO, pr, gO, bufs=2)
                return f

            K, V, RR, O = T0["gk"], T0["gv"], T0["gr"], T0["go"]
            H[K + 0].append(gates)
            for i in range(4):
                H[K + 8 * i + 11].append(turn(i, i, [(gate_sum, 1)] if i == 0 else [(turned_dve, i)]))
            H[V + 11].append(scores)
            for h in range(GLA_H):
                H[RR + 8 * h + 3].append(o_head(h))
            H[RR + 7].append(gate_sums_after(0, 0, o_copied, 1))
            H[RR + 15].append(gate_sums_after(0, 1, o_copied, 2))
            for pr in range(PAIRS):
                H[GLAO_AT[pr]].append(turn_o(pr))
            for i in range(6):
                stripes(K + BODY * i, 2 * i, H_GLA if i == 0 else None)

            narrow = lambda j: (h_lo_ready, PAIRS * H_GLAO + j // 2 + 1)
            pe.wait_ge(rows_copied, U0["gr"] + 3)
            pe.wait_ge(o_copied, 4)
            wide(O, 0, True, narrow)
            pe.wait_ge(rows_copied, U0["gr"] + 4)
            wide(O + 16, 1, True, narrow, last=True)

            def mlp(layer):
                up, down, u, s = T0[f"u{layer}"], T0[f"d{layer}"], U0[f"u{layer}"], S0[f"u{layer}"]
                occ = H_M0 if layer == 0 else H_M1
                pe.wait_ge(xn_ready, 2 + 4 * layer)
                turn_all(occ, X)

                def freed(s):
                    return [] if isinstance(s, int) and s == N_GLA_TURNED else [(turned_act, s - N_GLA_TURNED)]

                def hooks(b, first=False):
                    i = 2 * b
                    late = {11: [turn(u + i, s + i, freed(s + i))]}
                    return late if first else {**late, 3: [turn(u + i - 1, s + i - 1, freed(s + i - 1))]}

                stripes(up, u, occ, hooks(0, first=True))
                with pe.Fori(1, 8) as b:
                    stripes(up + BODY * b, u + 2 * b, None, hooks(b))

                for half in range(2):
                    m = 64 * layer + 32 * half

                    def src(b, m=m):
                        return lambda j: (src_lo, m + 8 * b + j // 2 + 1)

                    pe.wait_ge(rows_copied, u + 15 + half)
                    if half == 1:
                        pe.wait_ge(turned_act, s - N_GLA_TURNED + 16)
                        pe.wait_ge(g_copied, 4 + 4 * layer)
                    t = down + 64 * half
                    hooks0 = {3: [turn(u + 15, s + 15, freed(s + 15))], 9: [gate_sums(1 + 2 * layer, 0)],
                              13: [gate_sums(1 + 2 * layer, 1)]} if half == 0 else {}
                    wide(t, half, True, src(0), hooks0)
                    with pe.Fori(1, 4 - half) as b:
                        wide(t + BODY * b, half, False, src(b), {})
                    if half == 1:
                        wide(t + 3 * BODY, half, False, src(3), {}, last=True)

            mlp(0)
            Q, K, V, O = T0["aq"], T0["ak"], T0["av"], T0["ao"]
            pe.wait_ge(xn_ready, 4)
            turn_all(H_Q, X)
            u, s = U0["aq"], S0["aq"]
            for i in range(8):
                H[Q + 8 * i + 11].append(turn(u + i, s + i, [(turned_act, s + i - N_GLA_TURNED)]))
            H[Q + 18].append(gate_sums(2, 0))
            H[Q + 23].append(gate_sums(2, 1))

            def turn_kv(pr):
                def f():
                    if pr == 0:
                        pe.wait_ge(g_copied, 6)
                    turn_pair(H_KV, pr, X, bufs=2)
                return f

            for pr in range(PAIRS):
                H[Q + 24 + pr].append(turn_kv(pr))

            def z_part(p):
                def f():
                    pe.wait_ge(turned_act, S0["ak"] + p // 2 + 1 - N_GLA_TURNED)
                    if p:
                        pe.wait_ge(logit_ready, p)
                    for i in range(2):
                        h, bank = 2 * p + i, ps[:, 4 + i, :]
                        mm(bank[:, 0:SEQ], kT[:, h, 0:P], qT[:, h, :], start=True, stop=False)
                        mm(bank[:, 0:P], ident_bf[:], mask_bf[:], start=False, stop=True)
                        mm(bank[:, SEQ:ZW], kT[:, h, P:SEQ], qT[:, h, P:SEQ], start=True, stop=False)
                        last = mm(bank[:, SEQ:ZW], ident_bf[:], mask_bf[:], start=False, stop=True)
                    last.then_inc(z_done, 1)
                return f

            def later_part(p):
                def f():
                    w2 = wk[p % 2][1]
                    pe.wait_ge(sp_ready, p + 1)
                    for i in range(2):
                        o = ps[:, 4 + i, :]
                        mm(o[:, 0:SEQ], neg_later[:], w2[:, i, 0:SEQ], start=True, stop=False)
                        mm(o[:, P:SEQ], neg_ones[:], w2[:, i, SEQ:ZW], start=False, stop=True)
                        last = mm(o[:, SEQ:ZW], neg_later[:], w2[:, i, SEQ:ZW], start=True, stop=True)
                    last.then_inc(later_done, 1)
                return f

            def head_part(p):
                def f():
                    pe.wait_ge(a_exp, p + 1)
                    pe.wait_ge(rows_copied, U0["av"] + p // 2 + 1)
                    pe.wait_ge(turned_act, S0["ak"] + 4 - N_GLA_TURNED)
                    if p >= 2:
                        pe.wait_ge(head_kept, p - 1)
                    for i in range(2):
                        h = 2 * p + i
                        c = slice(h * DH, (h + 1) * DH)
                        mm(ps[:, 6 + p % 2, i * SEQ:(i + 1) * SEQ], aV[:, 0, c], qT[:, h, :], start=True, stop=False)
                        last = mm(ps[:, 6 + p % 2, i * SEQ + P:(i + 1) * SEQ], aV[:, 1, c], kT[:, h, 0:P], start=False, stop=True)
                    last.then_inc(head_done, 1)
                return f

            for p in range(SB_H // 2):
                H[Z_AT[p]].append(z_part(p))
                H[Z_AT[p] + 3].append(later_part(p))
                H[HEAD_AT[p]].append(head_part(p))
            for i in range(6):
                stripes(Q + BODY * i, u + 2 * i, {0: H_Q, 2: H_KV}.get(i))
            heads = lambda j: (head_lo, j // 2 + 1)
            pe.wait_ge(rows_copied, U0["av"] + 3)
            pe.wait_ge(logit_ready, SB_H // 2)
            wide(O, 0, True, heads)
            pe.wait_ge(rows_copied, U0["av"] + 4)
            pe.wait_ge(head_kept, SB_H // 2)
            wide(O + 16, 1, True, heads, last=True)
            mlp(1)


def _stripes(w):
    n = w.shape[1] // SW
    return w.reshape(ST, 2, P, n, SW).transpose(3, 0, 2, 1, 4).reshape(n * ST, P, TW)


def _halves(w):
    k = w.shape[0] // P
    return w.reshape(k, P, 2, TW).transpose(2, 0, 1, 3).reshape(2 * k, P, TW)


def _cols(v):
    return v.reshape(-1, P).T


def _rows(v):
    return np.broadcast_to(v[None, :], (P, v.shape[0]))


def _layout(x, c, ada_w, ada_b, ln_g, ln_b, gla_w_in, gla_w_gate_up, gla_b_gate, gla_norm_g, gla_w_out, kv_ada_w,
            kv_ada_b, w_kv, sb_w_q, sb_w_out, mlp_w1, mlp_b1, mlp_w2, mlp_b2):
    qk = D // 2
    w_in = gla_w_in[0]
    gl = np.zeros((4, P, 4, SEQ), np.float32)
    gl[:, :, :, :RANK] = w_in[:, 2 * qk + 2 * D:].reshape(4, 4, P, RANK).transpose(0, 2, 1, 3)
    tiles = [gl.reshape(4, P, TW), _stripes(w_in[:, qk:2 * qk]), _stripes(w_in[:, :qk]),
             _stripes(w_in[:, 2 * qk:2 * qk + D]), _stripes(w_in[:, 2 * qk + D:2 * qk + 2 * D]), _halves(gla_w_out[0]),
             _stripes(mlp_w1[0]), _halves(mlp_w2[0]), _stripes(sb_w_q[0]), _stripes(w_kv[:, :D]),
             _stripes(w_kv[:, D:]), _halves(sb_w_out[0]), _stripes(mlp_w1[1]), _halves(mlp_w2[1])]
    at = {"sh_a": 0, "sc_a": 1, "g_a": 2, "sh_m": 3, "sc_m": 4, "g_m": 5}
    mods, mod_b = [], []
    for name in MODS:
        if name in ("sh_k", "sc_k"):
            w, b, i = kv_ada_w, kv_ada_b, int(name == "sc_k")
        else:
            w, b, i = ada_w[int(name[-1])], ada_b[int(name[-1])], at[name[:-1]]
        mods.append(w[:, i * D:(i + 1) * D].T.reshape(KT, P, D))
        mod_b.append(_cols(b[i * D:(i + 1) * D]))
    wgu = np.zeros((P, qk), np.float32)
    wgu[:RANK] = gla_w_gate_up[0]
    lns = [(l, i) for l in range(2) for i in range(2)]
    return {
        "tiles": np.concatenate(tiles), "mods": np.concatenate(mods), "c_rows": _rows(c[0]),
        "x_rows": x[0].reshape(TOK, P, D).transpose(1, 0, 2), "mod_b": np.concatenate(mod_b, axis=1),
        "ln_t": np.concatenate([_cols(v[l, i]) for l, i in lns for v in (ln_g, ln_b)], axis=1),
        "b1_t": np.concatenate([_cols(mlp_b1[l]) for l in range(2)], axis=1), "bg_t": _cols(gla_b_gate[0]),
        "wgu": wgu, "normg": _rows(gla_norm_g[0]),
        "ln_rows": np.stack([np.stack([_rows(v[l, i]) for v in (ln_g, ln_b)]) for l, i in lns]),
        "b2_rows": np.stack([_rows(mlp_b2[l]) for l in range(2)]),
    }


def kernel(**inputs):
    import concourse.bacc as _bacc
    from concourse.bass_utils import run_bass_kernel_spmd as _run

    nc = _bacc.Bacc("TRN2", target_bir_lowering=False, num_devices=1)
    arrays, args = {}, []
    for name, a in _layout(**{k: np.asarray(v) for k, v in inputs.items()}).items():
        a = np.ascontiguousarray(a)
        arrays[f"in_{name}"] = a
        args.append(nc.dram_tensor(f"in_{name}", a.shape, mybir.dt.from_np(a.dtype), kind="ExternalInput").ap())
    args.append(nc.dram_tensor("out", (SEQ, D), mybir.dt.float32, kind="ExternalOutput").ap())
    build_kernel(nc, *args)
    r = _run(nc, [arrays], core_ids=[0])
    return r.results[0]["out"].reshape(1, SEQ, D)
```

```python
import concourse.bass as bass
import numpy as np
from concourse import mybir
from collections import defaultdict
from contextlib import ExitStack

P = 128
D = 2048
SEQ = 256
TOK = SEQ // P
KT = D // P
FF = 4 * D
RANK = 16
TAU = 16.0
CHUNK = 64
NCH = SEQ // CHUNK
GLA_H = 4
GLA_DK = D // 2 // GLA_H
GLA_DV = D // GLA_H
GJ = D // 2 // P
SB_H = 16
DH = D // SB_H
ALPHA = 4.0 ** 0.25
EPS = 1e-5

TW = 1024
SW = 512
ST = 8
BODY = 16
RING = 4
_sizes = [("lead", 24), ("gq1", 8), ("gv", 32), ("gr", 32), ("go", 32),
          ("u0", 128), ("d0", 128), ("aq", 32), ("ak", 32), ("av", 32), ("ao", 32),
          ("u1", 128), ("d1", 128)]
T0 = {}
_at = 0
for _n, _s in _sizes:
    T0[_n] = _at
    _at += _s

MODS = ["lead", "lead", "g_a0", "sh_m0", "sc_m0", "g_m0", "sh_k", "sc_k", "sh_a1", "sc_a1",
        "g_a1", "sh_m1", "sc_m1", "g_m1"]
MOD = {n: KT * i for i, n in enumerate(MODS)}
N_MODT = KT * len(MODS)
LEAD, LEAD_BUFS = 2 * KT, 8
LEAD_MODS = 4
LEAD_TILES = 3
MOD_AT = {8: tuple(range(1, 16, 2)), 6: (1, 4, 6, 9, 12, 14), 4: (1, 5, 9, 13), 2: (6, 14), 0: ()}
SCHEDULE = [("gv", 0, 4, 8), ("go", 0, 2, 6), ("u0", 0, 8, 6), ("d0", 0, 4, 6), ("d0", 64, 1, 2), ("d0", 80, 3, 6),
            ("aq", 0, 4, 6), ("av", 0, 2, 2), ("ao", 0, 2, 4), ("u1", 0, 4, 4), ("u1", 64, 12, 0)]
HALF_BODY, HALF_BODY_MODS = 8, 4
PLAN = {T0["gq1"]: (LEAD, HALF_BODY_MODS)}
_a = LEAD + HALF_BODY_MODS
for _n, _off, _bodies, _per in SCHEDULE:
    for _b in range(_bodies):
        PLAN[T0[_n] + _off + BODY * _b] = (_a, _per)
        _a += _per
assert _a == N_MODT

STRIPE0 = {"gv": 4, "gr": 8, "u0": 12, "aq": 28, "ak": 32, "av": 36, "u1": 40}
TURNED0 = {"u0": 4, "aq": 20, "ak": 24, "u1": 28}
N_GLA_TURNED = 4
H_GLA, H_GLAO, H_M0, H_Q, H_KV, H_M1 = range(6)
PAIRS = KT // 2
Z_AT = [T0["ak"] + 15 + 6 * p for p in range(SB_H // 2)]
HEAD_AT = [T0["av"] + 8 * (p // 2) + 12 + p % 2 for p in range(SB_H // 2)]
HEAD_SPLIT_AT = [T0["av"] + 28 + p for p in range(4)] + [T0["ao"] + i for i in (1, 2, 9, 10)]
GLAO_AT = [T0["gr"] + i for i in (24, 25, 26, 27, 31)] + [T0["go"] + i for i in (0, 7, 8)]
LAST_PARTS = [(0, (0, 1)), (1, (0,)), (1, (1,))]
WARM = 20
PRE = 2


def build_kernel(nc, tiles, mods, c_t, x_rows, mod_b, ln_t, b1_t, bg_t, w_gl, wgu, normg, ln_rows, b2_rows, out):
    F32, F32R, BF16 = mybir.dt.float32, mybir.dt.float32r, mybir.dt.bfloat16
    ACT, ALU = mybir.ActivationFunctionType, mybir.AluOpType
    ctx = ExitStack()
    with ctx:
        def sb(name, shape, dt=F32):
            return ctx.enter_context(nc.sbuf_tensor(name, shape, dt))

        def sem(name):
            return ctx.enter_context(nc.semaphore(name))

        raw = sb("raw", [P, RING, TW])
        w_hi = sb("w_hi", [P, RING, TW], F32R)
        w_lo = sb("w_lo", [P, RING, TW], F32R)
        mod_w = sb("mod_w", [P, 2, D])
        cs = sb("cs", [P, D])
        X = sb("X", [P, TOK, D])
        h_hi = sb("h_hi", [P, KT, SEQ], F32R)
        h_lo = sb("h_lo", [P, KT, SEQ], F32R)
        R = sb("R", [P, 8 * D])
        G = sb("G", [P, D])
        S = sb("S", [P, D])
        ident = sb("ident", [P, P])
        ones = sb("ones", [P, P])
        neg_ones = sb("neg_ones", [P, P])
        neg_later = sb("neg_later", [P, P])
        incl = sb("incl", [P, P])
        mask_bf = sb("mask_bf", [P, P], BF16)
        ident_bf = sb("ident_bf", [P, P], BF16)
        mod_t = sb("mod_t", [P, N_MODT])
        mod_bt = sb("mod_bt", [P, N_MODT])
        lnt = sb("lnt", [P, 4 * 2 * KT])
        b1t = sb("b1t", [P, 2 * FF // P])
        bgt = sb("bgt", [P, GJ])
        coef = sb("coef", [P, 4, KT])
        coef2 = sb("coef2", [P, 4, KT])
        c_col = sb("c_col", [P, 2, KT])
        stats = sb("stats", [P, TOK, 4, 6])
        mv = sb("mv", [P, TOK, 2])
        rstd = sb("rstd", [P, 8])
        ssq = sb("ssq", [P, 8])
        eps = sb("eps", [P, 1])
        ps = ctx.enter_context(nc.psum_tensor("ps", [P, 8, 512], F32))
        rows_buf, turned_buf = S[:, 0:TW], S[:, TW:2 * TW]

        gEki, gEks, gEq, gqd = (R[:, i * D:(i + 1) * D].rearrange("p (j t) -> p j t", j=GJ) for i in range(4))
        kk_at = [4 * D + GJ * CHUNK * (n * (n + 1) // 2) for n in range(NCH + 1)]
        KK = [R[:, kk_at[n]:kk_at[n + 1]].rearrange("p (j t) -> p j t", j=GJ) for n in range(NCH)]
        bc_f, tmp_f = R[:, 4 * D:5 * D], R[:, 5 * D:6 * D]
        reset_f, wgu_f = R[:, 3 * D:4 * D], R[0:RANK, 2 * D:2 * D + D // 2]
        SC = R[:, kk_at[NCH]:kk_at[NCH] + D].rearrange("p (h s t) -> p h s t", h=GLA_H, s=TOK)
        o_junk = R[:, 8 * D - GLA_DV:8 * D]
        normg_sb = R[:, kk_at[NCH] + D:kk_at[NCH] + D + GLA_DV]
        gV = R[:, 0:2 * D].rearrange("p (a d) -> p a d", a=TOK)
        gR = R[:, 2 * D:4 * D].rearrange("p (a d) -> p a d", a=TOK)
        gO = R[:, 4 * D:6 * D].rearrange("p (a d) -> p a d", a=TOK)
        glT = S[0:RANK, TW:TW + SEQ]
        xT = R[:, 0:2 * D].rearrange("p (k t) -> p k t", k=KT)
        gl_w = R[:, 2 * D + D // 2:2 * D + D // 2 + KT * RANK]
        gla_rows = [rows_buf, G[:, 0:TW], G[:, TW:2 * TW], rows_buf]
        decay = sb("decay", [P, GJ, NCH])
        kT = R[:, 0:2 * D].rearrange("p (h t) -> p h t", h=SB_H)
        aV = R[:, 2 * D:4 * D].rearrange("p (a d) -> p a d", a=TOK)
        qT = R[:, 4 * D:6 * D].rearrange("p (h t) -> p h t", h=SB_H)
        ZW = SEQ + P
        wk = [[R[:, 6 * D + (2 * a + b) * 2 * ZW:6 * D + (2 * a + b + 1) * 2 * ZW].rearrange("p (h c) -> p h c", h=2)
               for b in range(2)] for a in range(2)]
        ln_at = [6 * D, 6 * D, 6 * D, 0]
        Bg = [R[:, a:a + D] for a in ln_at]
        Bb = [R[:, a + D:a + 2 * D] for a in ln_at]
        lead_bufs = [mod_w[:, 0, :], mod_w[:, 1, :], *(R[:, i * D:(i + 1) * D] for i in range(4, 8)), G[:], S[:]]

        raw_loaded = [sem(f"raw_loaded{i}") for i in range(RING)]
        mod_loaded = [sem(f"mod_loaded{i}") for i in range(2)]
        c_loaded, x_loaded, setup_loaded = sem("c_loaded"), sem("x_loaded"), sem("setup_loaded")
        ln_loaded, b2_loaded, out_stored = sem("ln_loaded"), sem("b2_loaded"), sem("out_stored")
        lead_loaded = [sem(f"lead_loaded{i}") for i in range(LEAD_BUFS)]
        consts_made, sc_cleared, normg_loaded = sem("consts_made"), sem("sc_cleared"), sem("normg_loaded")
        c_diag, c_spread, diag_made = sem("c_diag"), sem("c_spread"), sem("diag_made")
        o_normed, x_normed, x_scaled, tok0_final = sem("o_normed"), sem("x_normed"), sem("x_scaled"), sem("tok0_final")
        mod_b_loaded, gl_loaded = sem("mod_b_loaded"), sem("gl_loaded")
        xt_copied, lead_coef, gl_done = sem("xt_copied"), sem("lead_coef"), sem("gl_done")
        hi_ready, lo_ready, tile_used, mod_done = sem("hi_ready"), sem("lo_ready"), sem("tile_used"), sem("mod_done")
        c_ln, c_log, c_sig, cs_ready = sem("c_ln"), sem("c_log"), sem("c_sig"), sem("cs_ready")
        coef_ready, xn_ready, x_updated = sem("coef_ready"), sem("xn_ready"), sem("x_updated")
        h_turned, h_full, h_hi_ready, h_lo_ready = (sem(n) for n in ("h_turned", "h_full", "h_hi_ready", "h_lo_ready"))
        rows_copied, blocks_turned = sem("rows_copied"), sem("blocks_turned")
        turned_act, turned_dve, squared = sem("turned_act"), sem("turned_dve"), sem("squared")
        src_hi, src_lo = sem("src_hi"), sem("src_lo")
        g_diag, g_summed, g_copied = sem("g_diag"), sem("g_summed"), sem("g_copied")
        var_ready, rstd_ready = sem("var_ready"), sem("rstd_ready")
        act_step, dve_step = sem("act_step"), sem("dve_step")
        gl_copied, gate_done, gate_sum = sem("gl_copied"), sem("gate_done"), sem("gate_sum")
        gate_ln, bc_ready, decay_ready = sem("gate_ln"), sem("bc_ready"), sem("decay_ready")
        scores_done, scores_copied, scores_masked = sem("scores_done"), sem("scores_copied"), sem("scores_masked")
        r_ln, r_log, r_sig, part_done = sem("r_ln"), sem("r_log"), sem("r_sig"), sem("part_done")
        o_done, o_copied, r_gated, o_rstd, o_ready = (
            sem("o_done"), sem("o_copied"), sem("r_gated"), sem("o_rstd"), sem("o_ready"))
        z_done, z_ln, sp_ready, later_done, logit_ready, a_exp, head_done, head_kept, head_hi, head_lo = (
            sem(n) for n in ("z_done", "z_ln", "sp_ready", "later_done", "logit_ready", "a_exp",
                             "head_done", "head_kept", "head_hi", "head_lo"))

        block = ctx.enter_context(nc.Block())

        def h_bank(occ, pr):
            return {H_GLAO: 6 + pr % 2, H_KV: 4 + pr % 2}.get(occ, 4 + pr % 4)

        HALF_AT = {2 * i: i for i in range(HALF_BODY_MODS)}

        def mod_positions(per_body):
            return {j: i for i, j in enumerate(MOD_AT[per_body])}

        CONSTS, SETUP = 11, 64
        GATE_BANK = [4, 2, 4, 2]
        HALF_END = [[T0[n] + k * (h + 1) for h in range(2)] for n, k in (("go", 16), ("d0", 64), ("ao", 16), ("d1", 64))]
        LN_LOADS = [32, 64, 96, 128]

        @block.sync
        def _(sp):
            sp.dma_start(c_col[:, 0, :], c_t).then_inc(c_loaded, 16)
            sp.dma_start(mod_bt[:], mod_b).then_inc(mod_b_loaded, 16)

            def load_tile(t, slot, first=False):
                if not first:
                    sp.wait_ge(lo_ready, t - RING + 1)
                sp.dma_start(raw[:, slot, :], tiles[bass.ds(t, 1), :, :].rearrange("a p n -> p (a n)"))\
                  .then_inc(raw_loaded[slot], 16)

            def load_mod(a, slot, first=False):
                if not first:
                    sp.wait_ge(mod_done, a - 1)
                sp.dma_start(mod_w[:, slot, :], mods[bass.ds(a, 1), :, :].rearrange("a p n -> p (a n)"))\
                  .then_inc(mod_loaded[slot], 16)

            def body(t, a, per_body, at=None, n=BODY):
                at = at or mod_positions(per_body)
                for j in range(n):
                    load_tile(t + j, j % RING)
                    if j in at:
                        load_mod(a + at[j], at[j] % 2)

            def load_lead(a):
                buf = a % LEAD_BUFS
                if a >= LEAD_BUFS:
                    sp.wait_ge(mod_done, a - LEAD_BUFS + 1)
                elif buf == LEAD_BUFS - 1:
                    sp.wait_ge(cs_ready, 1)
                sp.dma_start(lead_bufs[buf], mods[a, :, :]).then_inc(lead_loaded[buf], 16)

            for pr in range(PAIRS):
                for i in range(LEAD_MODS):
                    load_lead(LEAD_MODS * pr + i)
                    if pr == 0 and i == 0:
                        sp.dma_start(X[:], x_rows).then_inc(x_loaded, 16)
                        sp.dma_start(gl_w, w_gl).then_inc(gl_loaded, 16)
                for i in range(LEAD_TILES):
                    t = LEAD_TILES * pr + i
                    load_tile(t, t % RING, first=t < RING)
            body(T0["gq1"], LEAD, None, HALF_AT, HALF_BODY)
            for name, off, bodies, per in SCHEDULE:
                t = T0[name] + off
                with sp.Fori(0, bodies) as b:
                    body(t + BODY * b, PLAN[t][0] + per * b, per)
            for half in range(2):
                for tok in range(TOK):
                    cols = slice(half * TW, (half + 1) * TW)
                    sp.wait_ge(*((tok0_final, half + 1), (x_updated, 3 + half + 1))[tok])
                    sp.dma_start(out[tok * P:(tok + 1) * P, cols], X[:, tok, cols]).then_inc(out_stored, 16)
            sp.wait_ge(out_stored, 16 * 2 * TOK)

        @block.gpsimd
        def _(pool):
            nc.gpsimd.memset(ident[:], 0.0).then_inc(diag_made, 1)
            nc.gpsimd.memset(ones[:], 1.0).then_inc(diag_made, 1)
            pool.wait_ge(diag_made, 2)
            nc.gpsimd.affine_select(out=ident[:], in_=ident[:], compare_op=ALU.not_equal, fill=1.0, base=0,
                                    pattern=[[-1, P]], channel_multiplier=1).then_inc(diag_made, 1)
            for dst, src in ((lnt, ln_t), (b1t, b1_t), (bgt, bg_t)):
                pool.dma_start(dst[:], src).then_inc(setup_loaded, 16)
            pool.dma_start(wgu_f, wgu).then_inc(setup_loaded, 16)
            nc.gpsimd.memset(neg_ones[:], -1.0).then_inc(consts_made, 1)
            nc.gpsimd.memset(neg_later[:], -1.0).then_inc(consts_made, 1)
            nc.gpsimd.memset(incl[:], 1.0).then_inc(consts_made, 1)
            nc.gpsimd.memset(mask_bf[:], -1e30).then_inc(consts_made, 1)
            nc.gpsimd.memset(eps[:], EPS).then_inc(consts_made, 1)
            nc.gpsimd.memset(reset_f, 1.0).then_inc(consts_made, 1)
            pool.wait_ge(consts_made, 6)
            nc.gpsimd.memset(reset_f.rearrange("p (c t) -> p c t", t=CHUNK)[:, :, 0:1], 0.0).then_inc(consts_made, 1)
            nc.gpsimd.affine_select(out=neg_later[:], in_=neg_later[:], compare_op=ALU.is_ge, fill=0.0, base=-1,
                                    pattern=[[-1, P]], channel_multiplier=1).then_inc(consts_made, 1)
            nc.gpsimd.affine_select(out=incl[:], in_=incl[:], compare_op=ALU.is_ge, fill=0.0, base=0,
                                    pattern=[[1, P]], channel_multiplier=-1).then_inc(consts_made, 1)
            nc.gpsimd.affine_select(out=mask_bf[:], in_=mask_bf[:], compare_op=ALU.is_ge, fill=0.0, base=0,
                                    pattern=[[-1, P]], channel_multiplier=1).then_inc(consts_made, 1)
            pool.wait_ge(consts_made, 10)
            nc.gpsimd.tensor_copy(ident_bf[:], ident[:]).then_inc(consts_made, 1)

            pool.wait_ge(mod_done, LEAD)
            nc.gpsimd.memset(SC, 0.0).then_inc(sc_cleared, 1)
            pool.dma_start(normg_sb, normg).then_inc(normg_loaded, 16)
            for i in range(4):
                part = gR[:, :, i * SW:(i + 1) * SW]
                pool.wait_ge(r_sig, i + 1)
                nc.gpsimd.tensor_tensor(part, part, rows_buf.rearrange("p (a n) -> p a n", a=TOK), ALU.mult).then_inc(r_gated, 1)
                pool.wait_ge(r_gated, i + 1)
                pool.wait_ge(o_normed, i + 1)
                o = gO[:, :, i * SW:(i + 1) * SW]
                nc.gpsimd.tensor_tensor(o, o, part, ALU.mult).then_inc(o_ready, 1)

            def load_rows(l):
                pool.dma_start(Bg[l], ln_rows[l, 0, :, :]).then_inc(ln_loaded, 16)
                pool.dma_start(Bb[l], ln_rows[l, 1, :, :]).then_inc(ln_loaded, 16)

            def load_b2(layer):
                pool.wait_ge(squared, 16 * (layer + 1))
                pool.dma_start(S[:], b2_rows[layer, :, :]).then_inc(b2_loaded, 16)

            pool.wait_ge(h_lo_ready, PAIRS * (H_GLAO + 1))
            load_rows(0)
            load_b2(0)
            pool.wait_ge(tile_used, T0["d0"] + 128)
            load_rows(1)
            pool.wait_ge(a_exp, SB_H // 2)
            load_rows(2)
            load_b2(1)
            pool.wait_ge(tile_used, T0["d1"] + 64 + 32)
            load_rows(3)
            pool.wait_ge(ln_loaded, LN_LOADS[3])
            for half in range(2):
                cols = slice(half * TW, (half + 1) * TW)
                x = X[:, 0, cols]
                pool.wait_ge(x_normed, half + 1)
                nc.gpsimd.tensor_tensor(x, x, Bg[3][:, cols], ALU.mult).then_inc(x_scaled, 1)
                pool.wait_ge(x_scaled, half + 1)
                nc.gpsimd.tensor_tensor(x, x, Bb[3][:, cols], ALU.add).then_inc(tok0_final, 1)

        @block.scalar
        def _(act):
            steps = [0]

            def link(ins):
                steps[0] += 1
                ins.then_inc(act_step, 1)
                act.wait_ge(act_step, steps[0])

            def split_tile(t, slot, lap, first=False):
                act.wait_ge(raw_loaded[slot], 16 * lap)
                if not first:
                    act.wait_ge(tile_used, t - RING + 1)
                nc.scalar.activation(w_hi[:, slot, :], raw[:, slot, :], ACT.Copy).then_inc(hi_ready, 1)

            H = defaultdict(list)

            def body(t, hooks=None, lap0=None, skip=0, n=BODY):
                for j in range(skip, n):
                    split_tile(t + j, j % RING, (t // RING if lap0 is None else lap0) + j // RING + 1)
                    for f in (H.get(t + j, ()) if hooks is None else hooks.get(j, ())):
                        f()

            def pre_split(t):
                for j in range(PRE):
                    split_tile(t + j, j % RING, t // RING + 1)

            def loop(t_first, n, make_hooks):
                with act.Fori(0, n) as b:
                    body(t_first + BODY * b, make_hooks(b), t_first // RING + (BODY // RING) * b)

            def rows_out(done, par, dst, s=None):
                def f():
                    act.wait_ge(tile_used, done)
                    if s is not None:
                        act.wait_ge(blocks_turned, s)
                    nc.scalar.activation(dst, ps[:, 2 * par:2 * par + 2, :], ACT.Copy).then_inc(rows_copied, 1)
                return f

            def staged():
                return rows_buf.rearrange("p (a n) -> p a n", a=TOK)

            def relu(s, i, layer, first=False):
                def f():
                    act.wait_ge(blocks_turned, s + 1)
                    if not (first and layer == 0):
                        act.wait_ge(squared, 16 * layer + i)
                    for blk in range(4):
                        col = 64 * layer + 4 * i + blk
                        ins = nc.scalar.activation(turned_buf[:, blk * SEQ:(blk + 1) * SEQ], ps[:, 6 + blk // 2, (blk % 2) * SEQ:(blk % 2 + 1) * SEQ],
                                                   ACT.Relu, bias=b1t[:, bass.ds(col, 1)])
                    ins.then_inc(turned_act, 1)
                return f

            def keep_turned(s, dst, scale=1.0):
                def f():
                    act.wait_ge(blocks_turned, s + 1)
                    nc.scalar.activation(dst, ps[:, 6:8, :].rearrange("p a n -> p (a n)"), ACT.Copy, scale=scale)\
                      .then_inc(turned_act, 1)
                return f

            def h_full_pair(occ, pr, plain=False, co=None):
                act.wait_ge(h_turned, PAIRS * occ + pr + 1)
                if pr >= 2:
                    act.wait_ge(h_lo_ready, PAIRS * occ + pr - 1)
                full = turned_buf[:, (pr % 2) * 512:(pr % 2 + 1) * 512]
                if plain:
                    ins = nc.scalar.activation(full, ps[:, h_bank(occ, pr), :], ACT.Copy)
                else:
                    for i in range(2):
                        kt = 2 * pr + i
                        ins = nc.scalar.activation(full[:, i * SEQ:(i + 1) * SEQ], ps[:, h_bank(occ, pr), i * SEQ:(i + 1) * SEQ],
                                                   ACT.Identity, scale=co[:, 0, kt:kt + 1], bias=co[:, 1, kt:kt + 1])
                ins.then_inc(h_full, 1)

            def h_split_pair(occ, pr, used=None):
                act.wait_ge(h_full, PAIRS * occ + pr + 1)
                if used is not None:
                    act.wait_ge(tile_used, used)
                full = turned_buf[:, (pr % 2) * 512:(pr % 2 + 1) * 512]
                nc.scalar.activation(h_hi[:, 2 * pr:2 * pr + 2, :], full.rearrange("p (a t) -> p a t", a=2), ACT.Copy)\
                  .then_inc(h_hi_ready, 1)

            def h_pair(occ, pr, plain=False, co=None, used=None):
                def f():
                    h_full_pair(occ, pr, plain, co)
                    h_split_pair(occ, pr, used)
                return f

            def h_start(occ, n_coef, t, co):
                act.wait_ge(coef_ready, n_coef)
                for pr in range(2):
                    h_full_pair(occ, pr, co=co)
                    h_split_pair(occ, pr)
                for pr in range(2, PAIRS):
                    H[t + pr].append(h_pair(occ, pr, co=co))

            def gate_rows(occ, r):
                def f():
                    bank = GATE_BANK[occ]
                    act.wait_ge(g_summed, 2 * occ + r + 1)
                    nc.scalar.activation(G[:, r * TW:(r + 1) * TW], ps[:, bank:bank + 2, :].rearrange("p a n -> p (a n)"), ACT.Copy)\
                      .then_inc(g_copied, 1)
                return f

            def norm_scale(occ, t=None, final=False):
                for tok in range(TOK):
                    if tok and t is not None:
                        pre_split(t)
                    act.wait_ge(var_ready, 2 * occ + tok + 1)
                    link(nc.scalar.activation(rstd[:, tok:tok + 1], mv[:, tok, 1:2], ACT.Ln, bias=eps[:]))
                    nc.scalar.activation(rstd[:, tok:tok + 1], rstd[:, tok:tok + 1], ACT.Exp, scale=-0.5).then_inc(rstd_ready, 1)
                    if final and tok == 0:
                        act.wait_ge(rstd_ready, 2 * occ + 1)
                        link(nc.scalar.activation(ssq[:, 0:1], rstd[:, 0:1], ACT.Copy, scale=-1.0))
                        link(nc.scalar.activation(ssq[:, 1:2], mv[:, 0, 0:1], ACT.Identity, scale=ssq[:, 0:1]))
                        for half in range(2):
                            x = X[:, 0, half * TW:(half + 1) * TW]
                            nc.scalar.activation(x, x, ACT.Identity, scale=rstd[:, 0:1], bias=ssq[:, 1:2]).then_inc(x_normed, 1)

            def ln_of_exp(dst, src, done):
                link(nc.scalar.activation(dst, src, ACT.Abs))
                link(nc.scalar.activation(dst, dst, ACT.Exp, scale=-1.0))
                nc.scalar.activation(dst, dst, ACT.Ln, bias=1.0).then_inc(done, 1)

            nc.scalar.preload_act_table_set("natural_log_exp_and_others")
            act.wait_ge(c_loaded, 16)
            ln_of_exp(c_col[:, 1, :], c_col[:, 0, :], c_ln)
            act.wait_ge(c_log, 1)
            nc.scalar.activation(c_col[:, 1, :], c_col[:, 1, :], ACT.Exp).then_inc(c_sig, 1)
            act.wait_ge(c_spread, 1)
            nc.scalar.activation(cs[:], ps[:, 0:4, :].rearrange("p a n -> p (a n)"), ACT.Copy).then_inc(cs_ready, 1)
            act.wait_ge(consts_made, CONSTS)
            for pr in range(PAIRS):
                act.wait_ge(h_turned, pr + 1)
                nc.scalar.activation(xT[:, 2 * pr:2 * pr + 2, :].rearrange("p a t -> p (a t)"), ps[:, h_bank(H_GLA, pr), :], ACT.Copy)\
                  .then_inc(xt_copied, 1)
            act.wait_ge(xt_copied, PAIRS)
            for pr in range(PAIRS):
                act.wait_ge(lead_coef, pr + 1)
                for kt in (2 * pr, 2 * pr + 1):
                    ins = nc.scalar.activation(xT[:, kt, :], xT[:, kt, :], ACT.Identity, scale=coef[:, 0, kt:kt + 1], bias=coef[:, 1, kt:kt + 1])
                ins.then_inc(h_full, 1)
                act.wait_ge(h_full, pr + 1)
                nc.scalar.activation(h_hi[:, 2 * pr:2 * pr + 2, :], xT[:, 2 * pr:2 * pr + 2, :], ACT.Copy).then_inc(h_hi_ready, 1)
                for i in range(LEAD_TILES):
                    t = LEAD_TILES * pr + i
                    split_tile(t, t % RING, t // RING + 1, first=t < RING)

            def gl_out():
                act.wait_ge(gl_done, 1)
                nc.scalar.activation(glT, ps[0:RANK, 6, 0:SEQ], ACT.Copy).then_inc(gl_copied, 1)

            gl_out()
            act.wait_ge(setup_loaded, SETUP)

            flat = lambda v: v.rearrange("p j t -> p (j t)")

            def gate_log():
                act.wait_ge(gate_sum, 1)
                link(nc.scalar.activation(tmp_f, bc_f, ACT.Abs))

            def gate_log2():
                link(nc.scalar.activation(tmp_f, tmp_f, ACT.Exp, scale=-1.0))

            def gate_log3():
                nc.scalar.activation(tmp_f, tmp_f, ACT.Ln, bias=1.0).then_inc(gate_ln, 1)

            def decays1():
                act.wait_ge(bc_ready, 1)
                nc.scalar.activation(flat(gEq), bc_f, ACT.Exp, scale=1.0 / TAU).then_inc(decay_ready, 1)
                nc.scalar.activation(decay[:], bc_f.rearrange("p (j n t) -> p j n t", j=GJ, t=CHUNK)[:, :, :, CHUNK - 1],
                                     ACT.Exp, scale=1.0 / TAU).then_inc(decay_ready, 1)

            def decays2():
                nc.scalar.activation(flat(gEki), bc_f, ACT.Exp, scale=-1.0 / TAU).then_inc(decay_ready, 1)

            def decays3():
                act.wait_ge(bc_ready, 2)
                nc.scalar.activation(flat(gEks), tmp_f, ACT.Exp, scale=1.0 / TAU).then_inc(decay_ready, 1)

            def v_out(i, dst, t):
                return rows_out(t + ST * (i + 1), i % 2, dst[:, :, i * SW:(i + 1) * SW])

            def scores_out():
                act.wait_ge(scores_done, 1)
                act.wait_ge(sc_cleared, 1)
                nc.scalar.activation(SC[:, :, 0, P:SEQ], ps[:, 4:8, P:SEQ], ACT.Copy).then_inc(scores_copied, 1)

            K, V, RR, O = T0["gq1"], T0["gv"], T0["gr"], T0["go"]
            rows3 = lambda v: v.rearrange("p (a n) -> p a n", a=TOK)
            for j, (bank, dst) in enumerate(((2, gla_rows[1]), (0, gla_rows[0]), (4, gla_rows[2]))):
                def f(j=j, bank=bank, dst=dst):
                    act.wait_ge(tile_used, K - LEAD_TILES + j + 1)
                    nc.scalar.activation(rows3(dst), ps[:, bank:bank + 2, :], ACT.Copy).then_inc(rows_copied, 1)
                H[K + j].append(f)
            for at, f in ((4, gate_log), (5, gate_log2), (6, gate_log3), (9, decays1), (10, decays2), (12, decays3)):
                H[K + at].append(f)
            H[K + 14].append(rows_out(K + 8, 1, rows3(gla_rows[3]), 1))
            H[V + 23].append(scores_out)

            def v_first():
                act.wait_ge(turned_dve, 2)
                v_out(0, gV, V)()

            H[V + 14].append(v_first)
            for i in range(1, 4):
                H[V + 8 * i + 10].append(v_out(i, gV, V))

            def o_out(h):
                def f():
                    act.wait_ge(o_done, h + 1)
                    nc.scalar.activation(gO[:, :, h * GLA_DV:(h + 1) * GLA_DV], ps[:, 4:6, :], ACT.Copy).then_inc(o_copied, 1)
                return f

            def o_scale(h):
                def f():
                    act.wait_ge(o_copied, h + 1)
                    for tok in range(TOK):
                        link(nc.scalar.activation(o_junk, gO[:, tok, h * GLA_DV:(h + 1) * GLA_DV], ACT.Square,
                                                  accum_out=ssq[:, 2 * h + tok:2 * h + tok + 1]))
                    two = slice(2 * h, 2 * h + 2)
                    link(nc.scalar.activation(rstd[:, two], ssq[:, two], ACT.Ln, scale=1.0 / GLA_DV, bias=eps[:]))
                    nc.scalar.activation(rstd[:, two], rstd[:, two], ACT.Exp, scale=-0.5).then_inc(o_rstd, 1)
                return f

            def r_out(i):
                def f():
                    v_out(i, gR, RR)()
                    if i:
                        act.wait_ge(r_sig, i)
                        act.wait_ge(o_ready, i)
                    else:
                        act.wait_ge(blocks_turned, N_GLA_TURNED)
                    act.wait_ge(rows_copied, STRIPE0["gr"] + i + 1)
                    ln_of_exp(staged(), gR[:, :, i * SW:(i + 1) * SW], r_ln)
                return f

            def r_gate(i):
                def f():
                    act.wait_ge(r_log, i + 1)
                    nc.scalar.activation(rows_buf, rows_buf, ACT.Exp).then_inc(r_sig, 1)
                return f

            for h in range(GLA_H):
                B = RR + 8 * h
                H[B + 6].append(o_out(h))
                H[B + 8].append(o_scale(h))
                H[B + 10].append(r_out(h))
                H[B + 12].append(r_gate(h))
            H[RR + 9].append(gate_rows(0, 0))
            H[RR + 17].append(gate_rows(0, 1))
            for pr in range(PAIRS):
                H[GLAO_AT[pr] + 3].append(h_pair(H_GLAO, pr, plain=True, used=RR + 24 + pr + 1))
            body(K, n=HALF_BODY)
            for i in range(6):
                body(V + BODY * i)
            norm_scale(0, T0["u0"])

            def mlp(layer):
                up, down, s = T0[f"u{layer}"], T0[f"d{layer}"], TURNED0[f"u{layer}"]

                def hooks(b, first=False):
                    i, t = 2 * b, up + BODY * b
                    late = {10: [rows_out(t + 8, 0, staged(), s + i)], 14: [relu(s + i, i, layer, first)]}
                    early = {2: [rows_out(t, 1, staged(), s + i - 1)], 6: [relu(s + i - 1, i - 1, layer)]}
                    return late if first else {**late, **early}

                h_start(H_M0 if layer == 0 else H_M1, 1 if layer == 0 else 4, up, coef)
                for j, f in hooks(0, first=True).items():
                    H[up + j] += f
                body(up, skip=PRE)
                loop(up + BODY, 7, lambda b: hooks(b + 1))

                def split_src(kt, slot, m, made):
                    def f():
                        act.wait_ge(tile_used, m)
                        act.wait_ge(squared, 16 * layer + made)
                        nc.scalar.activation(h_hi[:, slot:slot + 2, :], R[:, bass.ds(kt * SEQ, 2 * SEQ)].rearrange("p (a t) -> p a t", a=2),
                                             ACT.Copy).then_inc(src_hi, 1)
                    return f

                def src_hooks(t, b, extra={}, made=16):
                    hooks = {j: [split_src(16 * b + j, j, t + j - 14, made)] for j in range(0, BODY, 2)}
                    for j, f in extra.items():
                        hooks[j] = f + hooks.get(j, [])
                    return hooks

                for half in range(2):
                    t = down + 64 * half
                    extra = {2: [rows_out(down, 1, staged(), s + 15)], 6: [relu(s + 15, 15, layer)],
                             12: [gate_rows(1 + 2 * layer, 0)], 15: [gate_rows(1 + 2 * layer, 1)]} if half == 0 else {}
                    body(t, src_hooks(t, 0, extra, made=4))
                    loop(t + BODY, 3, lambda b: src_hooks(t + BODY + BODY * b, b + 1))
                norm_scale(1 + 2 * layer, T0["aq"] if layer == 0 else None, final=layer == 1)

            mlp(0)
            Q, K, V, O = T0["aq"], T0["ak"], T0["av"], T0["ao"]
            h_start(H_Q, 3, Q, coef2)
            for i in range(8):
                t = Q + 8 * i
                dst, scale = (qT, DH ** -0.5) if i < 4 else (kT, 1.0)
                H[t + 10].append(rows_out(t + 8, i % 2, staged(), TURNED0["aq"] + i))
                H[t + 14].append(keep_turned(TURNED0["aq"] + i, dst[:, 4 * (i % 4):4 * (i % 4) + 4, :].rearrange("p h t -> p (h t)"), scale))
            H[Q + 21].append(gate_rows(2, 0))
            H[Q + 26].append(gate_rows(2, 1))
            for pr in range(PAIRS):
                H[Q + 27 + pr].append(h_pair(H_KV, pr, co=coef, used=Q + 24 + pr + 1))
            for i in range(4):
                H[V + 8 * i + 10].append(v_out(i, aV, V))

            def z_part(p):
                def f():
                    if p < 2:
                        act.wait_ge(x_updated, 2)
                    act.wait_ge(z_done, p + 1)
                    if p >= 2:
                        act.wait_ge(a_exp, p - 1)
                    ln_of_exp(wk[p % 2][0], ps[:, 4:6, 0:ZW], z_ln)
                return f

            def a_part(p):
                def f():
                    act.wait_ge(logit_ready, p + 1)
                    w1 = wk[p % 2][0]
                    nc.scalar.activation(qT[:, 2 * p:2 * p + 2, :], w1[:, :, 0:SEQ], ACT.Exp)
                    nc.scalar.activation(kT[:, 2 * p:2 * p + 2, 0:P], w1[:, :, SEQ:ZW], ACT.Exp).then_inc(a_exp, 1)
                return f

            def o_part(p):
                def f():
                    act.wait_ge(head_done, p + 1)
                    nc.scalar.activation(qT[:, 2 * p:2 * p + 2, :], ps[:, 6 + p % 2, :].rearrange("p (a t) -> p a t", a=2), ACT.Copy)\
                      .then_inc(head_kept, 1)
                return f

            def o_split(p):
                def f():
                    act.wait_ge(head_kept, p + 1)
                    act.wait_ge(tile_used, V + 24 + p + 1)
                    nc.scalar.activation(h_hi[:, 2 * p:2 * p + 2, :], qT[:, 2 * p:2 * p + 2, :], ACT.Copy).then_inc(head_hi, 1)
                return f

            for p in range(SB_H // 2):
                H[Z_AT[p] + 3].append(z_part(p))
                H[Z_AT[p] + 7].append(a_part(p))
                H[HEAD_AT[p] + 3].append(o_part(p))
                H[HEAD_SPLIT_AT[p]].append(o_split(p))
            body(Q, skip=PRE)
            for i in range(1, 8):
                body(Q + BODY * i)
            norm_scale(2, T0["u1"])
            mlp(1)

        @block.vector
        def _(dve):
            steps = [0]

            def link(ins):
                steps[0] += 1
                ins.then_inc(dve_step, 1)
                dve.wait_ge(dve_step, steps[0])

            def split_tile(t, slot, first=False):
                dve.wait_ge(hi_ready, t + 1)
                if not first:
                    dve.wait_ge(tile_used, t - RING + 1)
                nc.vector.tensor_tensor(w_lo[:, slot, :], raw[:, slot, :], w_hi[:, slot, :].bitcast(F32), ALU.subtract)\
                  .then_inc(lo_ready, 1)

            def mod_tile(a, buf, loaded, lap):
                dve.wait_ge(loaded, 16 * lap)
                nc.vector.scalar_tensor_tensor(buf, buf, 1.0, cs[:], ALU.mult, ALU.mult,
                                               accum_out=mod_t[:, bass.ds(a, 1)]).then_inc(mod_done, 1)

            H = defaultdict(list)

            def body(t, a, lap, per, hooks, skip=0, at=None, n=BODY):
                at = at or mod_positions(per)
                for j in range(n):
                    if j >= skip:
                        split_tile(t + j, j % RING)
                    if j in at:
                        mod_tile(a + at[j], mod_w[:, at[j] % 2, :], mod_loaded[at[j] % 2], lap + at[j] // 2 + 1)
                    for f in hooks.get(j, ()):
                        f()

            def run(t, hooks=None, skip=0):
                a, per = PLAN[t]
                body(t, a, (a - LEAD) // 2, per, {j: H.get(t + j, []) for j in range(BODY)} if hooks is None else hooks, skip)

            def loop(t_first, n, make_hooks):
                a, per = PLAN[t_first]
                with dve.Fori(0, n) as b:
                    body(t_first + BODY * b, a + per * b, (a - LEAD) // 2 + (per // 2) * b, per, make_hooks(b))

            def make_coef(co, scale, shift, ln):
                sc, sh = MOD[scale], MOD[shift]
                dve.wait_ge(mod_done, max(sc, sh) + KT)
                link(nc.vector.tensor_tensor(co[:, 2, :], mod_t[:, sc:sc + KT], mod_bt[:, sc:sc + KT], ALU.add))
                link(nc.vector.tensor_tensor(co[:, 1, :], mod_t[:, sh:sh + KT], mod_bt[:, sh:sh + KT], ALU.add))
                g, b = lnt[:, 2 * ln * KT:(2 * ln + 1) * KT], lnt[:, (2 * ln + 1) * KT:(2 * ln + 2) * KT]
                link(nc.vector.scalar_tensor_tensor(co[:, 3, :], co[:, 2, :], 1.0, b, ALU.add, ALU.mult))
                link(nc.vector.tensor_tensor(co[:, 1, :], co[:, 1, :], co[:, 3, :], ALU.add))
                nc.vector.scalar_tensor_tensor(co[:, 0, :], co[:, 2, :], 1.0, g, ALU.add, ALU.mult).then_inc(coef_ready, 1)

            def h_pair(occ, pr):
                dve.wait_ge(h_hi_ready, PAIRS * occ + pr + 1)
                full = turned_buf[:, (pr % 2) * 512:(pr % 2 + 1) * 512]
                nc.vector.tensor_tensor(h_lo[:, 2 * pr:2 * pr + 2, :], full.rearrange("p (a t) -> p a t", a=2),
                                        h_hi[:, 2 * pr:2 * pr + 2, :].bitcast(F32), ALU.subtract).then_inc(h_lo_ready, 1)

            def h_start(occ, t):
                for pr in range(2, PAIRS):
                    H[t + pr].append(lambda pr=pr: h_pair(occ, pr))

            def gate_diag(occ, name):
                g = MOD[name]
                dve.wait_ge(mod_done, g + KT)
                link(nc.vector.scalar_tensor_tensor(coef[:, 2, :], mod_t[:, g:g + KT], 1.0, mod_bt[:, g:g + KT], ALU.add, ALU.add))
                nc.vector.tensor_tensor(G[:].rearrange("p (j n) -> p j n", n=P), ident[:].unsqueeze(1).to_broadcast([P, KT, P]),
                                        coef[:, 2, :].unsqueeze(2).to_broadcast([P, KT, P]), ALU.mult).then_inc(g_diag, 1)

            def residual(occ, half, tok, alpha, ns=(0, 1)):
                bank = {(0, 0): 0, (0, 1): 4, (1, 0): 2, (1, 1): 6}[half, tok] + ns[0]
                at, width = half * TW + ns[0] * SW, len(ns) * SW
                cols = slice(at, at + width)
                stage = S[:, tok * TW + ns[0] * SW:tok * TW + ns[0] * SW + width]
                if half == 1 and (tok, ns) != LAST_PARTS[-1]:
                    dve.wait_ge(part_done, 2 * occ + LAST_PARTS.index((tok, ns)) + 1)
                else:
                    dve.wait_ge(tile_used, HALF_END[occ][half])
                dve.wait_ge(g_copied, 2 * occ + 2)
                link(nc.vector.tensor_tensor(stage, ps[:, bank:bank + len(ns), :].rearrange("p a n -> p (a n)"), G[:, cols], ALU.mult))
                link(nc.vector.scalar_tensor_tensor(X[:, tok, cols], X[:, tok, cols], alpha, stage, ALU.mult, ALU.add))
                for i in ns:
                    ins = nc.vector.bn_stats(stats[:, tok, 2 * half + i, :], X[:, tok, half * TW + i * SW:half * TW + (i + 1) * SW])
                return ins

            def variance(tok):
                nc.vector.bn_aggr(mv[:, tok, :], stats[:, tok, :, :].rearrange("p a b -> p (a b)")).then_inc(var_ready, 1)

            def norm_columns(occ, q):
                for tok in range(TOK):
                    dve.wait_ge(var_ready, 2 * occ + tok + 1)
                    dve.wait_ge(rstd_ready, 2 * occ + tok + 1)
                    x = X[:, tok, q * SW:(q + 1) * SW]
                    ins = nc.vector.tensor_scalar(x, x, mv[:, tok, 0:1], rstd[:, tok:tok + 1], ALU.subtract, ALU.mult)
                ins.then_inc(xn_ready, 1)

            def last_parts(occ, alpha):
                for tok, ns in LAST_PARTS:
                    link(residual(occ, 1, tok, alpha, ns))
                    if ns[-1] == 1:
                        variance(tok)

            def normalise(occ, alpha, t, h):
                last_parts(occ, alpha)
                norm_columns(occ, 0)
                split_tile(t, 0)
                split_tile(t + 1, 1)
                norm_columns(occ, 1)
                h_pair(h, 0)
                h_pair(h, 1)
                norm_columns(occ, 2)
                norm_columns(occ, 3)

            def half0(occ, alpha):
                return {8: [lambda: link(residual(occ, 0, 0, alpha))], 12: [lambda: link(residual(occ, 0, 1, alpha))]}

            def update_piece(l, q, mult):
                tok, cols = q // 2, slice((q % 2) * TW, (q % 2 + 1) * TW)

                def f():
                    if q == 0 and mult:
                        dve.wait_ge(ln_loaded, LN_LOADS[l])
                        dve.wait_ge(h_turned, PAIRS * {0: H_M0, 1: H_KV, 2: H_M1}[l] + PAIRS)
                        dve.wait_ge(xn_ready, 4 * (l + 1))
                    row = (Bg if mult else Bb)[l][:, cols]
                    ins = nc.vector.tensor_tensor(X[:, tok, cols], X[:, tok, cols], row, ALU.mult if mult else ALU.add)
                    if q == 3 and not mult:
                        ins.then_inc(x_updated, 1)
                    else:
                        link(ins)
                return f

            def update_hooks(l, t):
                pieces = [update_piece(l, q, m) for q in range(4) for m in (True, False)]
                for j, f in enumerate(pieces):
                    H[t + j].append(f)

            def merge(a, b):
                return {j: a.get(j, []) + b.get(j, []) for j in {*a, *b}}

            dve.wait_ge(c_ln, 1)
            nc.vector.scalar_tensor_tensor(c_col[:, 1, :], c_col[:, 0, :], 0.0, c_col[:, 1, :], ALU.min, ALU.subtract).then_inc(c_log, 1)
            dve.wait_ge(c_sig, 1)
            link(nc.vector.tensor_tensor(c_col[:, 0, :], c_col[:, 0, :], c_col[:, 1, :], ALU.mult))
            dve.wait_ge(diag_made, 3)
            nc.vector.tensor_tensor(S[:].rearrange("p (j n) -> p j n", n=P), ident[:].unsqueeze(1).to_broadcast([P, KT, P]),
                                    c_col[:, 0, :].unsqueeze(2).to_broadcast([P, KT, P]), ALU.mult).then_inc(c_diag, 1)
            dve.wait_ge(cs_ready, 1)
            dve.wait_ge(mod_b_loaded, 16)

            def lead_mod(a):
                mod_tile(a, lead_bufs[a % LEAD_BUFS], lead_loaded[a % LEAD_BUFS], a // LEAD_BUFS + 1)

            def lead_h(pr):
                dve.wait_ge(h_hi_ready, pr + 1)
                nc.vector.tensor_tensor(h_lo[:, 2 * pr:2 * pr + 2, :], xT[:, 2 * pr:2 * pr + 2, :],
                                        h_hi[:, 2 * pr:2 * pr + 2, :].bitcast(F32), ALU.subtract).then_inc(h_lo_ready, 1)

            def lead_tile(t):
                split_tile(t, t % RING, first=t < RING)

            for pr in range(PAIRS + 1):
                for i in range(LEAD_MODS):
                    if pr < PAIRS:
                        lead_mod(LEAD_MODS * pr + i)
                    if pr and i == 0:
                        lead_h(pr - 1)
                    if pr and i < LEAD_TILES:
                        lead_tile(LEAD_TILES * (pr - 1) + i)
                if pr < PAIRS:
                    a, kts = LEAD_MODS * pr, slice(2 * pr, 2 * pr + 2)
                    dve.wait_ge(mod_done, LEAD_MODS * (pr + 1))
                    nc.vector.scalar_tensor_tensor(coef[:, 0, kts], mod_t[:, a:a + 2], 1.0, mod_bt[:, a:a + 2], ALU.add, ALU.add)
                    nc.vector.tensor_tensor(coef[:, 1, kts], mod_t[:, a + 2:a + 4], mod_bt[:, a + 2:a + 4], ALU.add).then_inc(lead_coef, 1)
            g3 = lambda v: v.rearrange("p (j t) -> p j t", j=GJ)
            chunks = lambda v: v.rearrange("p (c t) -> p c t", t=CHUNK)

            def gate_logits():
                dve.wait_ge(gate_done, 1)
                dve.wait_ge(setup_loaded, SETUP)
                nc.vector.tensor_tensor(g3(bc_f), ps[:, 4:8, :].rearrange("p a (b t) -> p (a b) t", b=2),
                                        bgt[:].unsqueeze(2).to_broadcast([P, GJ, SEQ]), ALU.add).then_inc(gate_sum, 1)

            def log_sigmoid():
                dve.wait_ge(gate_sum, 1)
                dve.wait_ge(gate_ln, 1)
                link(nc.vector.scalar_tensor_tensor(tmp_f, bc_f, 0.0, tmp_f, ALU.min, ALU.subtract))

            def running_sums():
                nc.vector.tensor_tensor_scan(bc_f, reset_f, tmp_f, 0.0, ALU.mult, ALU.add).then_inc(bc_ready, 1)

            def sums_to_end():
                dve.wait_ge(bc_ready, 1)
                nc.vector.tensor_tensor(chunks(tmp_f), chunks(bc_f)[:, :, CHUNK - 1:CHUNK].to_broadcast([P, GJ * NCH, CHUNK]),
                                        chunks(bc_f), ALU.subtract).then_inc(bc_ready, 1)

            def gla_keys(i):
                def f():
                    dve.wait_ge(blocks_turned, i + 1)
                    dve.wait_ge(decay_ready, 4)
                    turned = ps[:, 6:8, :].rearrange("p a (b t) -> p (a b) t", b=2)
                    js = slice(4 * i, 4 * i + 4)
                    for n in range(NCH):
                        c = slice(n * CHUNK, (n + 1) * CHUNK)
                        ins = nc.vector.tensor_tensor(KK[n][:, js, c], turned[:, :, c], gEki[:, js, c], ALU.mult)
                        if n + 1 < NCH:
                            ins = nc.vector.tensor_tensor(KK[n + 1][:, js, c], turned[:, :, c], gEks[:, js, c], ALU.mult)
                    ins.then_inc(turned_dve, 1)
                return f

            def gla_decayed():
                dve.wait_ge(turned_dve, 2)
                for n in (2, 3):
                    w = CHUNK * (n - 1)
                    link(nc.vector.tensor_tensor(KK[n][:, :, 0:w], KK[n - 1][:, :, 0:w],
                                                 decay[:, :, n - 1:n].to_broadcast([P, GJ, w]), ALU.mult))

            def gla_queries(i):
                def f():
                    dve.wait_ge(blocks_turned, 2 + i + 1)
                    turned = ps[:, 6:8, :].rearrange("p a n -> p (a n)")
                    js = slice(4 * i, 4 * i + 4)
                    nc.vector.scalar_tensor_tensor(gqd[:, js, :].rearrange("p j t -> p (j t)"), turned, GLA_DK ** -0.5,
                                                   gEq[:, js, :].rearrange("p j t -> p (j t)"), ALU.mult, ALU.mult)\
                      .then_inc(turned_dve, 1)
                return f

            def scores_masked_out():
                dve.wait_ge(scores_copied, 1)
                for st in range(TOK):
                    lo = slice(st * SEQ + st * P, st * SEQ + st * P + CHUNK)
                    hi = slice(st * SEQ + st * P + CHUNK, st * SEQ + (st + 1) * P)
                    nc.vector.tensor_tensor(SC[0:CHUNK, :, st, st * P:st * P + CHUNK], ps[0:CHUNK, 4:8, lo],
                                            incl[0:CHUNK, 0:CHUNK].unsqueeze(1).to_broadcast([CHUNK, GLA_H, CHUNK]), ALU.mult)
                    ins = nc.vector.tensor_tensor(SC[:, :, st, st * P + CHUNK:(st + 1) * P], ps[:, 4:8, hi],
                                                  incl[:, CHUNK:P].unsqueeze(1).to_broadcast([P, GLA_H, CHUNK]), ALU.mult)
                ins.then_inc(scores_masked, 1)

            K, V, RR, O = T0["gq1"], T0["gv"], T0["gr"], T0["go"]
            for at, f in ((3, gate_logits), (7, log_sigmoid), (8, running_sums), (10, sums_to_end), (15, gla_keys(0)),
                          (19, gla_keys(1)), (20, gla_decayed), (23, gla_queries(0)), (27, gla_queries(1)),
                          (32, scores_masked_out)):
                H[K + at].append(f)

            def o_norm(h):
                def f():
                    dve.wait_ge(o_rstd, h + 1)
                    if h == 0:
                        dve.wait_ge(normg_loaded, 16)
                    for tok in range(TOK):
                        o = gO[:, tok, h * GLA_DV:(h + 1) * GLA_DV]
                        ins = nc.vector.scalar_tensor_tensor(o, o, rstd[:, 2 * h + tok:2 * h + tok + 1], normg_sb, ALU.mult, ALU.mult)
                    ins.then_inc(o_normed, 1)
                return f

            def r_logit(i):
                def f():
                    dve.wait_ge(r_ln, i + 1)
                    nc.vector.scalar_tensor_tensor(rows_buf.rearrange("p (a n) -> p a n", a=TOK), gR[:, :, i * SW:(i + 1) * SW], 0.0,
                                                   rows_buf.rearrange("p (a n) -> p a n", a=TOK), ALU.min, ALU.subtract).then_inc(r_log, 1)
                return f

            for h in range(GLA_H):
                B = RR + 8 * h
                for at, f in ((9, o_norm(h)), (11, r_logit(h))):
                    H[B + at].append(f)
            H[RR + 5].append(lambda: gate_diag(0, "g_a0"))
            for pr in range(PAIRS):
                H[GLAO_AT[pr] + 4].append(lambda pr=pr: h_pair(H_GLAO, pr))
            for j, f in half0(0, ALPHA).items():
                H[O + 16 + j] += f
            body(K, LEAD, 0, None, {j: H.get(K + j, []) for j in range(HALF_BODY)}, at=HALF_AT, n=HALF_BODY)
            for i in range(6):
                run(V + BODY * i)
            make_coef(coef, "sc_m0", "sh_m0", 0)
            normalise(0, ALPHA, T0["u0"], H_M0)

            def mlp(layer):
                up, down, s, l = T0[f"u{layer}"], T0[f"d{layer}"], TURNED0[f"u{layer}"], 2 * layer

                def square(i):
                    def f():
                        dve.wait_ge(turned_act, s - N_GLA_TURNED + i + 1)
                        nc.vector.tensor_tensor(R[:, bass.ds(i * TW, TW)], turned_buf, turned_buf, ALU.mult).then_inc(squared, 1)
                    return f

                def hooks(b):
                    return {15: [square(2 * b)], 7: [square(2 * b - 1)]}

                h_start(H_M0 if layer == 0 else H_M1, up)
                update_hooks(l, up + 7)
                H[up + 15].append(square(0))
                run(up, skip=PRE)
                if layer == 0:
                    loop(up + BODY, 7, lambda b: hooks(b + 1))
                else:
                    loop(up + BODY, 3, lambda b: hooks(b + 1))
                    loop(up + 4 * BODY, 4, lambda b: hooks(b + 4))

                def split_src(kt, slot, m, made):
                    def f():
                        dve.wait_ge(src_hi, m)
                        dve.wait_ge(squared, 16 * layer + made)
                        nc.vector.tensor_tensor(h_lo[:, slot:slot + 2, :], R[:, bass.ds(kt * SEQ, 2 * SEQ)].rearrange("p (a t) -> p a t", a=2),
                                                h_hi[:, slot:slot + 2, :].bitcast(F32), ALU.subtract).then_inc(src_lo, 1)
                    return f

                def bias_rows():
                    dve.wait_ge(g_copied, 4 + 4 * layer)
                    dve.wait_ge(b2_loaded, 16 * (layer + 1))
                    dve.wait_ge(x_updated, l + 1)
                    link(nc.vector.tensor_tensor(S[:], S[:], G[:], ALU.mult))

                def add_bias(tok):
                    return lambda: link(nc.vector.scalar_tensor_tensor(X[:, tok, :], X[:, tok, :], ALPHA, S[:], ALU.mult, ALU.add))

                for half in range(2):
                    t = down + 64 * half
                    m = 64 * layer + 32 * half

                    def src_hooks(b, m=m, made=16):
                        return {j: [split_src(16 * b + j, j, m + 8 * b + j // 2 + 1, made)] for j in range(0, BODY, 2)}

                    if half == 0:
                        extra = {7: [square(15)], 8: [lambda: gate_diag(1 + 2 * layer, f"g_m{layer}")]}
                    else:
                        extra = merge({1: [bias_rows], 3: [add_bias(0)], 5: [add_bias(1)]}, half0(1 + 2 * layer, 1.0))
                    run(t, merge(src_hooks(0, made=4), extra))
                    loop(t + BODY, 3, lambda b: src_hooks(b + 1))

            mlp(0)
            make_coef(coef, "sc_k", "sh_k", 1)
            make_coef(coef2, "sc_a1", "sh_a1", 1)
            normalise(1, 1.0, T0["aq"], H_Q)
            Q, K, V, O = T0["aq"], T0["ak"], T0["av"], T0["ao"]
            h_start(H_Q, Q)
            H[Q + 17].append(lambda: gate_diag(2, "g_a1"))
            for pr in range(PAIRS):
                H[Q + 28 + pr].append(lambda pr=pr: h_pair(H_KV, pr))
            update_hooks(1, K + 5)

            def z_part(p):
                def f():
                    z, w1, w2 = ps[:, 4:6, 0:ZW], wk[p % 2][0], wk[p % 2][1]
                    dve.wait_ge(z_ln, p + 1)
                    if p >= 2:
                        dve.wait_ge(sp_ready, p)
                    nc.vector.scalar_tensor_tensor(w2, z, 0.0, w1, ALU.max, ALU.add)
                    nc.vector.scalar_tensor_tensor(w1, z, 0.0, w1, ALU.min, ALU.subtract).then_inc(sp_ready, 1)
                return f

            def a_part(p):
                def f():
                    w1 = wk[p % 2][0]
                    dve.wait_ge(sp_ready, p + 1)
                    dve.wait_ge(later_done, p + 1)
                    nc.vector.tensor_tensor(w1, w1, ps[:, 4:6, 0:ZW], ALU.add).then_inc(logit_ready, 1)
                return f

            def o_split(p):
                def f():
                    dve.wait_ge(head_hi, p + 1)
                    nc.vector.tensor_tensor(h_lo[:, 2 * p:2 * p + 2, :], qT[:, 2 * p:2 * p + 2, :],
                                            h_hi[:, 2 * p:2 * p + 2, :].bitcast(F32), ALU.subtract).then_inc(head_lo, 1)
                return f

            for p in range(SB_H // 2):
                H[Z_AT[p] + 4].append(z_part(p))
                H[Z_AT[p] + 6].append(a_part(p))
                H[HEAD_SPLIT_AT[p] + 1].append(o_split(p))
            for j, f in half0(2, ALPHA).items():
                H[O + 16 + j] += f
            run(Q, skip=PRE)
            for i in range(1, 8):
                run(Q + BODY * i)
            make_coef(coef, "sc_m1", "sh_m1", 2)
            normalise(2, ALPHA, T0["u1"], H_M1)
            mlp(1)
            last_parts(3, 1.0)
            dve.wait_ge(ln_loaded, LN_LOADS[3])
            dve.wait_ge(var_ready, 8)
            for half in range(2):
                cols = slice(half * TW, (half + 1) * TW)
                x = X[:, 1, cols]
                link(nc.vector.scalar_tensor_tensor(x, x, mv[:, 1, 0:1], Bg[3][:, cols], ALU.subtract, ALU.mult))
                dve.wait_ge(rstd_ready, 8)
                nc.vector.scalar_tensor_tensor(x, x, rstd[:, 1:2], Bb[3][:, cols], ALU.mult, ALU.add).then_inc(x_updated, 1)

        @block.tensor
        def _(pe):
            mm = nc.tensor.matmul

            def product(dst, hs, ws, start, stop, more=False):
                hh, hl = hs
                wh, wl = ws
                mm(dst, hh, wh, start=start, stop=False, skip_group_check=more)
                mm(dst, hh, wl, start=False, stop=False, skip_group_check=more)
                return mm(dst, hl, wh, start=False, stop=stop, skip_group_check=more)

            def h_part(kt, tok):
                c = slice(tok * P, (tok + 1) * P)
                return h_hi[:, kt, c], h_lo[:, kt, c]

            def w_part(slot, c):
                return w_hi[:, slot, c], w_lo[:, slot, c]

            def stripe_tile(t, j, par, inputs=None, slot=None, bank=None):
                pe.wait_ge(lo_ready, t + 1)
                if inputs is not None:
                    pe.wait_ge(h_lo_ready, inputs)
                slot = j % RING if slot is None else slot
                bank = 2 * par if bank is None else bank
                for i in range(2):
                    kt = 2 * (j % ST) + i
                    for tok in range(TOK):
                        last = product(ps[:, bank + tok, :], h_part(kt, tok), w_part(slot, slice(i * SW, (i + 1) * SW)),
                                       kt == 0, kt == KT - 1)
                last.then_inc(tile_used, 1)

            H = defaultdict(list)

            def stripes(t, u, occ=None, hooks=None):
                for j in range(BODY):
                    if j % ST == 0:
                        pe.wait_ge(rows_copied, u + j // ST - 1)
                    stripe_tile(t + j, j, j // ST, None if occ is None or j >= ST else PAIRS * occ + j + 1)
                    for f in (H.get(t + j, ()) if hooks is None else hooks.get(j, ())):
                        f()

            def turn(u, s, freed, rows=rows_buf):
                def f():
                    pe.wait_ge(rows_copied, u + 1)
                    for sm, v in freed:
                        pe.wait_ge(sm, v)
                    for blk in range(4):
                        for tok in range(TOK):
                            o = (blk % 2) * SEQ + tok * P
                            last = nc.tensor.transpose(ps[:, 6 + blk // 2, o:o + P],
                                                       rows[:, tok * SW + blk * P:tok * SW + (blk + 1) * P], ident[:])
                    last.then_inc(blocks_turned, 1)
                return f

            def turn_pair(occ, pr, src, bufs=4):
                if occ == H_GLA and pr >= bufs:
                    pe.wait_ge(xt_copied, pr - bufs + 1)
                elif pr >= bufs:
                    pe.wait_ge(h_full, PAIRS * occ + pr - bufs + 1)
                for i in range(2):
                    kt = 2 * pr + i
                    for tok in range(TOK):
                        last = nc.tensor.transpose(ps[:, h_bank(occ, pr), i * SEQ + tok * P:i * SEQ + (tok + 1) * P],
                                                   src[:, tok, kt * P:(kt + 1) * P], ident[:])
                last.then_inc(h_turned, 1)

            def turn_normed(occ, pr, l):
                def f():
                    pe.wait_ge(xn_ready, 4 * l + pr // 2 + 1)
                    turn_pair(occ, pr, X)
                return f

            def turn_first(occ, l):
                for pr in range(PAIRS // 2):
                    turn_normed(occ, pr, l)()
                return [turn_normed(occ, PAIRS // 2 + j, l) for j in range(PAIRS // 2)]

            def gate_sums(occ, r):
                def f():
                    pe.wait_ge(g_diag, occ + 1)
                    if r:
                        pe.wait_ge(g_copied, 2 * occ + 1)
                    for n in range(2):
                        last = mm(ps[:, GATE_BANK[occ] + n, :], ones[:], G[:, r * TW + n * 512:r * TW + (n + 1) * 512], start=True, stop=True)
                    last.then_inc(g_summed, 1)
                return f

            HALF_BANKS = {0: (0, 4), 1: (2, 6)}

            def wide(t, half, first, src, hooks=None, last=False):
                def ready(j):
                    pe.wait_ge(lo_ready, t + j + 1)
                    if src(j) is not None:
                        pe.wait_ge(*src(j))

                def tile(j, toks, ns=(0, 1)):
                    for tok in toks:
                        for n in ns:
                            ins = product(ps[:, HALF_BANKS[half][tok] + n, :], h_part(j, tok), w_part(j % RING, slice(n * SW, (n + 1) * SW)),
                                          first and j == 0, first and j == BODY - 1, more=not first)
                    return ins

                for j in range(BODY - RING if last else BODY):
                    ready(j)
                    tile(j, range(TOK)).then_inc(tile_used, 1)
                    for f in (H.get(t + j, ()) if hooks is None else hooks.get(j, ())):
                        f()
                if last:
                    for part, (tok, ns) in enumerate(LAST_PARTS):
                        for j in range(BODY - RING, BODY):
                            if part == 0:
                                ready(j)
                            ins = tile(j, [tok], ns)
                            if part == len(LAST_PARTS) - 1:
                                ins.then_inc(tile_used, 1)
                        if part < len(LAST_PARTS) - 1:
                            ins.then_inc(part_done, 1)
                    for i in range(WARM):
                        nc.tensor.transpose(ps[:, 5, (i % 4) * P:(i % 4 + 1) * P], ident[:], ident[:])

            pe.wait_ge(c_diag, 1)
            for n in range(4):
                last = mm(ps[:, n, :], ones[:], S[:, n * SW:(n + 1) * SW], start=True, stop=True)
            last.then_inc(c_spread, 1)
            pe.wait_ge(x_loaded, 16)
            pe.wait_ge(consts_made, CONSTS)
            for pr in range(PAIRS):
                turn_pair(H_GLA, pr, X)
            pe.wait_ge(xt_copied, PAIRS)
            pe.wait_ge(gl_loaded, 16)
            for pr in range(PAIRS):
                pe.wait_ge(h_lo_ready, pr + 1)
                for kt in (2 * pr, 2 * pr + 1):
                    c = slice(kt * RANK, (kt + 1) * RANK)
                    last = mm(ps[0:RANK, 6, 0:SEQ], gl_w[:, c], xT[:, kt, :], start=kt == 0, stop=kt == KT - 1)
                if pr == PAIRS - 1:
                    last.then_inc(gl_done, 1)
                for i, bank in enumerate((2, 0, 4)):
                    t = LEAD_TILES * pr + i
                    stripe_tile(t, pr, None, slot=t % RING, bank=bank)

            def gates():
                pe.wait_ge(gl_copied, 1)
                pe.wait_ge(setup_loaded, SETUP)
                pe.wait_ge(rows_copied, 3)
                for j in range(GJ):
                    last = mm(ps[:, 4 + j // 2, (j % 2) * SEQ:(j % 2 + 1) * SEQ], wgu_f[:, j * P:(j + 1) * P], glT, start=True, stop=True)
                last.then_inc(gate_done, 1)

            def scores():
                pe.wait_ge(turned_dve, 4)
                for h in range(GLA_H):
                    for n in range(NCH):
                        for st in range(n // 2 + 1):
                            m = min(P, CHUNK * (n + 1) - st * P)
                            for j in (2 * h, 2 * h + 1):
                                last = mm(ps[0:m, 4 + h, st * SEQ + n * CHUNK:st * SEQ + (n + 1) * CHUNK],
                                          KK[n][:, j, st * P:st * P + m], gqd[:, j, n * CHUNK:(n + 1) * CHUNK],
                                          start=j % 2 == 0, stop=j % 2 == 1)
                last.then_inc(scores_done, 1)

            def o_head(h):
                def f():
                    if h == 0:
                        pe.wait_ge(scores_copied, 1)
                        pe.wait_ge(scores_masked, 1)
                        pe.wait_ge(rows_copied, STRIPE0["gv"] + 4)
                    else:
                        pe.wait_ge(o_copied, h)
                        pe.wait_ge(g_copied, min(h, 2))
                    for tok in range(TOK):
                        for st in range(tok + 1):
                            last = mm(ps[:, 4 + tok, :], SC[:, h, st, tok * P:(tok + 1) * P],
                                      gV[:, st, h * GLA_DV:(h + 1) * GLA_DV], start=st == 0, stop=st == tok)
                    last.then_inc(o_done, 1)
                return f

            def gate_sums_after(occ, r, sm, v):
                def f():
                    pe.wait_ge(sm, v)
                    gate_sums(occ, r)()
                return f

            def turn_o(pr):
                def f():
                    pe.wait_ge(o_ready, pr // 2 + 1)
                    turn_pair(H_GLAO, pr, gO, bufs=2)
                return f

            K, V, RR, O = T0["gq1"], T0["gv"], T0["gr"], T0["go"]
            H[K + 0].append(gates)
            for i, copied in enumerate((1, 0, 2, 3)):
                H[K + 4 * i + 11].append(turn(copied, i, [(gate_sum, 1)] if i == 0 else [(turned_dve, i)], gla_rows[i]))
            H[V + 20].append(scores)
            for h in range(GLA_H):
                H[RR + 8 * h + 3].append(o_head(h))
            H[RR + 7].append(gate_sums_after(0, 0, o_copied, 1))
            H[RR + 15].append(gate_sums_after(0, 1, o_copied, 2))
            for pr in range(PAIRS):
                H[GLAO_AT[pr]].append(turn_o(pr))
            pe.wait_ge(rows_copied, 1)
            for j in range(ST):
                stripe_tile(K + j, j, 1)
                for f in H.get(K + j, ()):
                    f()
            for i in range(4):
                stripes(V + BODY * i, STRIPE0["gv"] + 2 * i)

            narrow = lambda j: (h_lo_ready, PAIRS * H_GLAO + j // 2 + 1)
            pe.wait_ge(rows_copied, STRIPE0["gr"] + 3)
            pe.wait_ge(o_copied, 4)
            wide(O, 0, True, narrow)
            pe.wait_ge(rows_copied, STRIPE0["gr"] + 4)
            wide(O + 16, 1, True, narrow, last=True)

            def mlp(layer):
                up, down, u, s = T0[f"u{layer}"], T0[f"d{layer}"], STRIPE0[f"u{layer}"], TURNED0[f"u{layer}"]
                occ = H_M0 if layer == 0 else H_M1
                rest = turn_first(occ, 2 * layer)

                def freed(s, first=False):
                    return [] if first and layer == 0 else [(turned_act, s - N_GLA_TURNED)]

                def hooks(b, first=False):
                    i = 2 * b
                    late = {11: [turn(u + i, s + i, freed(s + i, first))]}
                    return {**late, **{j: [f] for j, f in enumerate(rest)}} if first else {**late, 3: [turn(u + i - 1, s + i - 1, freed(s + i - 1))]}

                stripes(up, u, occ, hooks(0, first=True))
                with pe.Fori(1, 8) as b:
                    stripes(up + BODY * b, u + 2 * b, None, hooks(b))

                for half in range(2):
                    m = 64 * layer + 32 * half

                    def src(b, m=m):
                        return lambda j: (src_lo, m + 8 * b + j // 2 + 1)

                    pe.wait_ge(rows_copied, u + 15 + half)
                    if half == 1:
                        pe.wait_ge(turned_act, s - N_GLA_TURNED + 16)
                        pe.wait_ge(g_copied, 4 + 4 * layer)
                    t = down + 64 * half
                    hooks0 = {3: [turn(u + 15, s + 15, freed(s + 15))], 9: [gate_sums(1 + 2 * layer, 0)],
                              13: [gate_sums(1 + 2 * layer, 1)]} if half == 0 else {}
                    wide(t, half, True, src(0), hooks0)
                    with pe.Fori(1, 4 - half) as b:
                        wide(t + BODY * b, half, False, src(b), {})
                    if half == 1:
                        wide(t + 3 * BODY, half, False, src(3), {}, last=True)

            mlp(0)
            Q, K, V, O = T0["aq"], T0["ak"], T0["av"], T0["ao"]
            for j, f in enumerate(turn_first(H_Q, 1)):
                H[Q + j].append(f)
            u, s = STRIPE0["aq"], TURNED0["aq"]
            for i in range(8):
                H[Q + 8 * i + 11].append(turn(u + i, s + i, [(turned_act, s + i - N_GLA_TURNED)]))
            H[Q + 18].append(gate_sums(2, 0))
            H[Q + 23].append(gate_sums(2, 1))

            def turn_kv(pr):
                def f():
                    if pr == 0:
                        pe.wait_ge(g_copied, 6)
                    turn_pair(H_KV, pr, X, bufs=2)
                return f

            for pr in range(PAIRS):
                H[Q + 24 + pr].append(turn_kv(pr))

            def z_part(p):
                def f():
                    pe.wait_ge(turned_act, TURNED0["ak"] + p // 2 + 1 - N_GLA_TURNED)
                    if p:
                        pe.wait_ge(logit_ready, p)
                    for i in range(2):
                        h, bank = 2 * p + i, ps[:, 4 + i, :]
                        mm(bank[:, 0:SEQ], kT[:, h, 0:P], qT[:, h, :], start=True, stop=False)
                        mm(bank[:, 0:P], ident_bf[:], mask_bf[:], start=False, stop=True)
                        mm(bank[:, SEQ:ZW], kT[:, h, P:SEQ], qT[:, h, P:SEQ], start=True, stop=False)
                        last = mm(bank[:, SEQ:ZW], ident_bf[:], mask_bf[:], start=False, stop=True)
                    last.then_inc(z_done, 1)
                return f

            def later_part(p):
                def f():
                    w2 = wk[p % 2][1]
                    pe.wait_ge(sp_ready, p + 1)
                    for i in range(2):
                        o = ps[:, 4 + i, :]
                        mm(o[:, 0:SEQ], neg_later[:], w2[:, i, 0:SEQ], start=True, stop=False)
                        mm(o[:, P:SEQ], neg_ones[:], w2[:, i, SEQ:ZW], start=False, stop=True)
                        last = mm(o[:, SEQ:ZW], neg_later[:], w2[:, i, SEQ:ZW], start=True, stop=True)
                    last.then_inc(later_done, 1)
                return f

            def head_part(p):
                def f():
                    pe.wait_ge(a_exp, p + 1)
                    pe.wait_ge(rows_copied, STRIPE0["av"] + p // 2 + 1)
                    pe.wait_ge(turned_act, TURNED0["ak"] + 4 - N_GLA_TURNED)
                    if p >= 2:
                        pe.wait_ge(head_kept, p - 1)
                    for i in range(2):
                        h = 2 * p + i
                        c = slice(h * DH, (h + 1) * DH)
                        mm(ps[:, 6 + p % 2, i * SEQ:(i + 1) * SEQ], aV[:, 0, c], qT[:, h, :], start=True, stop=False)
                        last = mm(ps[:, 6 + p % 2, i * SEQ + P:(i + 1) * SEQ], aV[:, 1, c], kT[:, h, 0:P], start=False, stop=True)
                    last.then_inc(head_done, 1)
                return f

            for p in range(SB_H // 2):
                H[Z_AT[p]].append(z_part(p))
                H[Z_AT[p] + 3].append(later_part(p))
                H[HEAD_AT[p]].append(head_part(p))
            for i in range(6):
                stripes(Q + BODY * i, u + 2 * i, {0: H_Q, 2: H_KV}.get(i))
            heads = lambda j: (head_lo, j // 2 + 1)
            pe.wait_ge(rows_copied, STRIPE0["av"] + 3)
            pe.wait_ge(logit_ready, SB_H // 2)
            wide(O, 0, True, heads)
            pe.wait_ge(rows_copied, STRIPE0["av"] + 4)
            pe.wait_ge(head_kept, SB_H // 2)
            wide(O + 16, 1, True, heads, last=True)
            mlp(1)


def _stripes(w):
    n = w.shape[1] // SW
    return w.reshape(ST, 2, P, n, SW).transpose(3, 0, 2, 1, 4).reshape(n * ST, P, TW)


def _halves(w):
    k = w.shape[0] // P
    return w.reshape(k, P, 2, TW).transpose(2, 0, 1, 3).reshape(2 * k, P, TW)


def _cols(v):
    return v.reshape(-1, P).T


def _rows(v):
    return np.broadcast_to(v[None, :], (P, v.shape[0]))


def _layout(x, c, ada_w, ada_b, ln_g, ln_b, gla_w_in, gla_w_gate_up, gla_b_gate, gla_norm_g, gla_w_out, kv_ada_w,
            kv_ada_b, w_kv, sb_w_q, sb_w_out, mlp_w1, mlp_b1, mlp_w2, mlp_b2):
    qk = D // 2
    w_in = gla_w_in[0]
    keys, queries = _stripes(w_in[:, qk:2 * qk]), _stripes(w_in[:, :qk])
    lead = np.stack([keys[ST:], keys[:ST], queries[:ST]], axis=1)
    tiles = [lead.reshape(-1, P, TW), queries[ST:],
             _stripes(w_in[:, 2 * qk:2 * qk + D]), _stripes(w_in[:, 2 * qk + D:2 * qk + 2 * D]), _halves(gla_w_out[0]),
             _stripes(mlp_w1[0]), _halves(mlp_w2[0]), _stripes(sb_w_q[0]), _stripes(w_kv[:, :D]),
             _stripes(w_kv[:, D:]), _halves(sb_w_out[0]), _stripes(mlp_w1[1]), _halves(mlp_w2[1])]
    at = {"sh_a": 0, "sc_a": 1, "g_a": 2, "sh_m": 3, "sc_m": 4, "g_m": 5}
    wa, ba = ada_w[0][:, :2 * D].T.reshape(2, PAIRS, 2, P, D)[::-1], ada_b[0][:2 * D].reshape(2, PAIRS, 2, P)[::-1]
    mods, mod_b = [wa.transpose(1, 0, 2, 3, 4).reshape(LEAD, P, D)], [_cols(ba.transpose(1, 0, 2, 3).reshape(-1))]
    for name in MODS[2:]:
        if name in ("sh_k", "sc_k"):
            w, b, i = kv_ada_w, kv_ada_b, int(name == "sc_k")
        else:
            w, b, i = ada_w[int(name[-1])], ada_b[int(name[-1])], at[name[:-1]]
        mods.append(w[:, i * D:(i + 1) * D].T.reshape(KT, P, D))
        mod_b.append(_cols(b[i * D:(i + 1) * D]))
    lns = [(l, i) for l in range(2) for i in range(2)]
    return {
        "tiles": np.concatenate(tiles), "mods": np.concatenate(mods), "c_t": _cols(c[0]),
        "x_rows": x[0].reshape(TOK, P, D).transpose(1, 0, 2), "mod_b": np.concatenate(mod_b, axis=1),
        "ln_t": np.concatenate([_cols(v[l, i]) for l, i in lns for v in (ln_g, ln_b)], axis=1),
        "b1_t": np.concatenate([_cols(mlp_b1[l]) for l in range(2)], axis=1), "bg_t": _cols(gla_b_gate[0]),
        "w_gl": w_in[:, 2 * qk + 2 * D:].reshape(KT, P, RANK).transpose(1, 0, 2).reshape(P, KT * RANK),
        "wgu": gla_w_gate_up[0], "normg": _rows(gla_norm_g[0]),
        "ln_rows": np.stack([np.stack([_rows(v[l, i]) for v in (ln_g, ln_b)]) for l, i in lns]),
        "b2_rows": np.stack([_rows(mlp_b2[l]) for l in range(2)]),
    }


def kernel(**inputs):
    import concourse.bacc as _bacc
    from concourse.bass_utils import run_bass_kernel_spmd as _run

    nc = _bacc.Bacc("TRN2", target_bir_lowering=False, num_devices=1)
    arrays, args = {}, []
    for name, a in _layout(**{k: np.asarray(v) for k, v in inputs.items()}).items():
        a = np.ascontiguousarray(a)
        arrays[f"in_{name}"] = a
        args.append(nc.dram_tensor(f"in_{name}", a.shape, mybir.dt.from_np(a.dtype), kind="ExternalInput").ap())
    args.append(nc.dram_tensor("out", (SEQ, D), mybir.dt.float32, kind="ExternalOutput").ap())
    build_kernel(nc, *args)
    r = _run(nc, [arrays], core_ids=[0])
    return r.results[0]["out"].reshape(1, SEQ, D)
```
